# Optimizing a Trainium2 kernel written in Bass

```python
import math
import jax, jax.numpy as jnp
from jax import lax
import numpy as np
import jax
import jax.numpy as jnp

D_MODEL = 1024
BATCH = 1
SEQ = 512
DEPTH = 1

D_MIX = D_MODEL
SB_HEADS = 8
SB_HEAD_DIM = 64
SB_WIDTH = SB_HEADS * SB_HEAD_DIM
RW_HEADS = 8
RW_HEAD_DIM = 64
RW_WIDTH = RW_HEADS * RW_HEAD_DIM
LORA_W = 64
LORA_A = 64
LORA_G = 128
RW_IN = 3 * RW_WIDTH + LORA_W + LORA_A + LORA_G
SB_IN = 3 * SB_WIDTH
N_IN = SB_IN + RW_IN
Q_BLOCK = 128
N_GROUPS = 4
EXPERTS_PER_GROUP = 8
N_EXPERTS = N_GROUPS * EXPERTS_PER_GROUP
TOP_K_IN_GROUP = 2
D_EXPERT = 256
RMS_EPS = 1e-6
GN_EPS = 64e-5


def rmsnorm(x, g):
    xf = x.astype(jnp.float32)
    y = xf * lax.rsqrt(jnp.mean(xf * xf, axis=-1, keepdims=True) + RMS_EPS)
    return (y * g.astype(jnp.float32)).astype(x.dtype)

def token_shift(u):
    return jnp.pad(u, ((0, 0), (1, 0), (0, 0)))[:, :-1]

def stick_breaking_attention(q, k, v):
    B, H, S, dh = q.shape
    scale = 1.0 / math.sqrt(dh)
    outs = []
    for blk in range(S // Q_BLOCK):
        t0 = blk * Q_BLOCK
        kv_len = t0 + Q_BLOCK
        qb = q[:, :, t0:kv_len].astype(jnp.float32)
        kb = k[:, :, :kv_len].astype(jnp.float32)
        vb = v[:, :, :kv_len].astype(jnp.float32)
        z = jnp.einsum('bhqd,bhkd->bhqk', qb, kb) * scale
        t_pos = t0 + jnp.arange(Q_BLOCK)[:, None]
        s_pos = jnp.arange(kv_len)[None, :]
        strict = s_pos < t_pos
        log_rest = jnp.where(strict, jax.nn.log_sigmoid(-z), 0.0)
        suffix = lax.cumsum(log_rest, axis=3, reverse=True) - log_rest
        weights = jnp.where(strict, jnp.exp(jax.nn.log_sigmoid(z) + suffix), 0.0)
        outs.append(jnp.einsum('bhqk,bhkd->bhqd', weights, vb))
    return jnp.concatenate(outs, axis=2)

def rwkv7_scan(r, w, k, v, kk, a):
    B, S, H, N = r.shape
    xs = tuple(jnp.moveaxis(t, 1, 0) for t in (r, w, k, v, kk, a))

    def step(state, inp):
        r_t, w_t, k_t, v_t, kk_t, a_t = inp
        sa = jnp.einsum('bhij,bhj->bhi', state, -kk_t)
        state = (state * w_t[:, :, None, :]
                 + sa[..., None] * (kk_t * a_t)[:, :, None, :]
                 + v_t[..., None] * k_t[:, :, None, :])
        out = jnp.einsum('bhij,bhj->bhi', state, r_t)
        return state, out

    state0 = jnp.zeros((B, H, N, N), jnp.float32)
    _, outs = lax.scan(step, state0, xs)
    return jnp.moveaxis(outs, 0, 1)

def rwkv7_group(u_rw, shift_mu, w0, w2, a0, a2, g2, k_k, k_a, r_k, ln_w, ln_b):
    B, S, _ = u_rw.shape
    uf = u_rw.astype(jnp.float32)
    um = uf + (token_shift(uf) - uf) * shift_mu.astype(jnp.float32)
    o = 0
    r = um[..., o:o + RW_WIDTH]; o += RW_WIDTH
    k = um[..., o:o + RW_WIDTH]; o += RW_WIDTH
    v = um[..., o:o + RW_WIDTH]; o += RW_WIDTH
    xw = um[..., o:o + LORA_W]; o += LORA_W
    xa = um[..., o:o + LORA_A]; o += LORA_A
    xg = um[..., o:o + LORA_G]
    w_log = -jax.nn.softplus(-(w0 + jnp.tanh(xw) @ w2)) - 0.5
    decay = jnp.exp(-jnp.exp(w_log))
    a = jax.nn.sigmoid(a0 + xa @ a2)
    g = jax.nn.sigmoid(xg) @ g2
    hs = lambda t: t.reshape(B, S, RW_HEADS, RW_HEAD_DIM)
    kk = hs(k * k_k)
    kk = kk * lax.rsqrt(jnp.maximum(jnp.sum(kk * kk, axis=-1, keepdims=True), 1e-24))
    k = k * (1.0 + (a - 1.0) * k_a)
    r_h, k_h, v_h, w_h, a_h = hs(r), hs(k), hs(v), hs(decay), hs(a)
    out = rwkv7_scan(r_h, w_h, k_h, v_h, kk, a_h)
    mean = jnp.mean(out, axis=-1, keepdims=True)
    var = jnp.mean(jnp.square(out - mean), axis=-1, keepdims=True)
    out = ((out - mean) * lax.rsqrt(var + GN_EPS)).reshape(B, S, RW_WIDTH) * ln_w + ln_b
    bonus = jnp.sum(r_h * k_h * r_k, axis=-1, keepdims=True) * v_h
    out = (out + bonus.reshape(B, S, RW_WIDTH)) * g
    return out.astype(u_rw.dtype)

def sb_group(u_sb, sb_out_g):
    B, S, _ = u_sb.shape
    heads = lambda t: t.reshape(B, S, SB_HEADS, SB_HEAD_DIM).transpose(0, 2, 1, 3)
    q = heads(u_sb[..., :SB_WIDTH])
    k = heads(u_sb[..., SB_WIDTH:2 * SB_WIDTH])
    v = heads(u_sb[..., 2 * SB_WIDTH:])
    o = stick_breaking_attention(q, k, v).transpose(0, 2, 1, 3)
    o = o * lax.rsqrt(jnp.mean(o * o, axis=-1, keepdims=True) + RMS_EPS)
    return (o.reshape(B, S, SB_WIDTH) * sb_out_g).astype(u_sb.dtype)

def hier_moe(x2d, w_grp, b_grp, w_exp, b_exp, w_gate, w_up, w_down):
    T = x2d.shape[0]
    xf = x2d.astype(jnp.float32)
    grp_prob = jax.nn.softmax(xf @ w_grp.astype(jnp.float32) + b_grp.astype(jnp.float32), axis=-1)
    g_val, g_idx = lax.top_k(grp_prob, 1)
    exp_logits = (xf @ w_exp.astype(jnp.float32) + b_exp.astype(jnp.float32)).reshape(T, N_GROUPS, EXPERTS_PER_GROUP)
    sel = jnp.take_along_axis(exp_logits, g_idx[:, :, None], axis=1)[:, 0]
    e_val, e_idx = lax.top_k(jax.nn.softmax(sel, axis=-1), TOP_K_IN_GROUP)
    weights = g_val * e_val / jnp.sum(e_val, axis=-1, keepdims=True)
    global_idx = g_idx * EXPERTS_PER_GROUP + e_idx
    combine = jnp.sum(jax.nn.one_hot(global_idx, N_EXPERTS, dtype=jnp.float32) * weights[..., None], axis=1)
    combine = combine.astype(x2d.dtype)
    y = jnp.zeros_like(x2d)
    for e in range(N_EXPERTS):
        h = jax.nn.silu(x2d @ w_gate[e]) * (x2d @ w_up[e])
        y = y + combine[:, e:e + 1] * (h @ w_down[e])
    return y

def first_inputs(seed: int = 0) -> dict:
    key = jax.random.key(seed)
    ks = jax.random.split(key, 28)
    f32 = jnp.float32
    nrm = lambda k, shape, s: jax.random.normal(k, shape, f32) * s
    L = DEPTH
    return {
        "x": jax.random.normal(ks[0], (BATCH, SEQ, D_MODEL), f32),
        "norm_mix_g": 1.0 + nrm(ks[1], (L, D_MODEL), 0.02),
        "w_in": nrm(ks[2], (L, D_MODEL, N_IN), D_MODEL ** -0.5),
        "shift_mu": jax.random.uniform(ks[3], (L, RW_IN), f32, 0.1, 0.9),
        "sb_out_g": 1.0 + nrm(ks[4], (L, SB_WIDTH), 0.02),
        "rw_w0": jax.random.uniform(ks[5], (L, RW_WIDTH), f32, -6.5, -1.5),
        "rw_w2": nrm(ks[6], (L, LORA_W, RW_WIDTH), 0.5 * LORA_W ** -0.5),
        "rw_a0": nrm(ks[7], (L, RW_WIDTH), 0.1),
        "rw_a2": nrm(ks[8], (L, LORA_A, RW_WIDTH), LORA_A ** -0.5),
        "rw_g2": nrm(ks[9], (L, LORA_G, RW_WIDTH), LORA_G ** -0.5),
        "rw_k_k": 0.85 + nrm(ks[10], (L, RW_WIDTH), 0.02),
        "rw_k_a": 1.0 + nrm(ks[11], (L, RW_WIDTH), 0.02),
        "rw_r_k": nrm(ks[12], (L, RW_HEADS, RW_HEAD_DIM), 0.1),
        "rw_ln_w": 1.0 + nrm(ks[13], (L, RW_WIDTH), 0.02),
        "rw_ln_b": nrm(ks[14], (L, RW_WIDTH), 0.02),
        "w_out": nrm(ks[15], (L, D_MIX, D_MODEL), D_MIX ** -0.5),
        "norm_ffn_g": 1.0 + nrm(ks[16], (L, D_MODEL), 0.02),
        "router_grp_w": nrm(ks[17], (L, D_MODEL, N_GROUPS), D_MODEL ** -0.5),
        "router_grp_b": nrm(ks[18], (L, N_GROUPS), 0.01),
        "router_exp_w": nrm(ks[19], (L, D_MODEL, N_EXPERTS), D_MODEL ** -0.5),
        "router_exp_b": nrm(ks[20], (L, N_EXPERTS), 0.01),
        "exp_w_gate": nrm(ks[21], (L, N_EXPERTS, D_MODEL, D_EXPERT), D_MODEL ** -0.5),
        "exp_w_up": nrm(ks[22], (L, N_EXPERTS, D_MODEL, D_EXPERT), D_MODEL ** -0.5),
        "exp_w_down": nrm(ks[23], (L, N_EXPERTS, D_EXPERT, D_MODEL), D_EXPERT ** -0.5),
        "final_norm_g": 1.0 + nrm(ks[24], (D_MODEL,), 0.02),
    }

def first_block(x, norm_mix_g, w_in, shift_mu, sb_out_g, rw_w0, rw_w2, rw_a0, rw_a2, rw_g2,
              rw_k_k, rw_k_a, rw_r_k, rw_ln_w, rw_ln_b, w_out, norm_ffn_g,
              router_grp_w, router_grp_b, router_exp_w, router_exp_b,
              exp_w_gate, exp_w_up, exp_w_down, final_norm_g):
    B, S, D = x.shape
    h = x
    for l in range(DEPTH):
        u = rmsnorm(h, norm_mix_g[l]) @ w_in[l]
        o_sb = sb_group(u[..., :SB_IN], sb_out_g[l])
        o_rw = rwkv7_group(u[..., SB_IN:], shift_mu[l], rw_w0[l], rw_w2[l], rw_a0[l], rw_a2[l],
                           rw_g2[l], rw_k_k[l], rw_k_a[l], rw_r_k[l], rw_ln_w[l], rw_ln_b[l])
        h = h + jnp.concatenate([o_sb, o_rw], axis=-1) @ w_out[l]
        xn = rmsnorm(h, norm_ffn_g[l]).reshape(B * S, D)
        y = hier_moe(xn, router_grp_w[l], router_grp_b[l], router_exp_w[l], router_exp_b[l],
                     exp_w_gate[l], exp_w_up[l], exp_w_down[l])
        h = h + y.reshape(B, S, D)
    return rmsnorm(h, final_norm_g)


HEAD_DIM = 64
A_Q_HEADS = 8
A_KV_HEADS = 2
A_WINDOW = 128
B_GROUPS = ((128, 1), (512, 4), (2048, 16))
B_HEADS_PER_GROUP = 8
A_WIDTH = A_Q_HEADS * HEAD_DIM
B_WIDTH = B_HEADS_PER_GROUP * HEAD_DIM
N_BRANCHES = 2
N_BUCKETS = 32
MAX_DISTANCE = 1024
REL_HEADS = A_Q_HEADS + len(B_GROUPS) * B_HEADS_PER_GROUP
PROJ_SIZES = (A_WIDTH, A_KV_HEADS * HEAD_DIM, A_KV_HEADS * HEAD_DIM,
              len(B_GROUPS) * B_WIDTH, len(B_GROUPS) * B_WIDTH, len(B_GROUPS) * B_WIDTH,
              A_WIDTH, B_WIDTH, N_BRANCHES * D_MODEL)
IN_WIDTH = sum(PROJ_SIZES)
EPS = 1e-6
NEG_INF = -1e30


def rms_norm(x, gain):
    xf = x.astype(jnp.float32)
    y = xf * lax.rsqrt(jnp.mean(xf * xf, axis=-1, keepdims=True) + EPS)
    return (y * gain.astype(jnp.float32)).astype(x.dtype)

def t5_bucket(rel):
    half = N_BUCKETS // 2
    max_exact = half // 2
    ret = (rel > 0).astype(jnp.int32) * half
    n = jnp.abs(rel)
    nf = jnp.maximum(n, max_exact).astype(jnp.float32)
    large = max_exact + (jnp.log(nf / max_exact) / math.log(MAX_DISTANCE / max_exact)
                         * (half - max_exact)).astype(jnp.int32)
    large = jnp.minimum(large, half - 1)
    return ret + jnp.where(n < max_exact, n, large)

def banded_attention(q, k, v, half_window, stride, bias_table, sink):
    bsz, L, H, dh = q.shape
    KV = k.shape[2]
    G = H // KV
    blk = half_window
    nb = -(-L // blk)
    Lp = nb * blk
    pad = Lp - L
    qb = jnp.pad(q, ((0, 0), (0, pad), (0, 0), (0, 0))).reshape(bsz, nb, blk, KV, G, dh)

    def windows(t):
        tp = jnp.pad(t, ((0, 0), (blk, blk + pad), (0, 0), (0, 0))).reshape(bsz, nb + 2, blk, KV, dh)
        return jnp.concatenate([tp[:, :-2], tp[:, 1:-1], tp[:, 2:]], axis=2)

    kw = windows(k)
    vw = windows(v)
    scores = jnp.einsum('bnqkgd,bnmkd->bkgnqm', qb, kw).astype(jnp.float32)

    qi = jnp.arange(blk)
    mi = jnp.arange(3 * blk)
    rel = mi[None, :] - blk - qi[:, None]
    bias = bias_table[t5_bucket(rel * stride)]
    bias = bias.transpose(2, 0, 1).reshape(KV, G, 1, blk, 3 * blk).astype(jnp.float32)
    blocks = jnp.arange(nb)[:, None, None] * blk
    qpos = blocks + qi[None, :, None]
    kpos = blocks - blk + mi[None, None, :]
    valid = (kpos >= 0) & (kpos < L) & (jnp.abs(kpos - qpos) <= half_window)

    logits = jnp.where(valid, scores + bias, NEG_INF)
    lse = jax.nn.logsumexp(logits, axis=-1)
    if sink is not None:
        lse = jnp.logaddexp(lse, sink.astype(jnp.float32).reshape(KV, G, 1, 1))
    probs = jnp.exp(logits - lse[..., None])
    out = jnp.einsum('bkgnqm,bnmkd->bnqkgd', probs.astype(v.dtype), vw)
    out = out.reshape(bsz, Lp, H, dh)[:, :L]
    lse = lse.transpose(0, 3, 4, 1, 2).reshape(bsz, Lp, H)[:, :L]
    return out, lse

def dilated_group(q, k, v, window, dilation, bias_table):
    bsz, S, H, dh = q.shape
    L = S // dilation

    def to_sub(t):
        return t.reshape(bsz, L, dilation, H, dh).transpose(0, 2, 1, 3, 4).reshape(bsz * dilation, L, H, dh)

    out, lse = banded_attention(to_sub(q), to_sub(k), to_sub(v), window // (2 * dilation),
                                dilation, bias_table, None)
    out = out.reshape(bsz, dilation, L, H, dh).transpose(0, 2, 1, 3, 4).reshape(bsz, S, H, dh)
    lse = lse.reshape(bsz, dilation, L, H).transpose(0, 2, 1, 3).reshape(bsz, S, H)
    return out, lse

def head_rms_norm(t, gain):
    return rms_norm(t, gain)

def second_inputs(seed: int = 0) -> dict:
    key = jax.random.key(seed)
    ks = jax.random.split(key, 16)
    f32 = jnp.float32
    x = jax.random.normal(ks[0], (BATCH, SEQ, D_MODEL), f32)
    norm_gain = 1.0 + 0.02 * jax.random.normal(ks[1], (DEPTH, D_MODEL), f32)
    w_in = jax.random.normal(ks[2], (DEPTH, D_MODEL, IN_WIDTH), f32) * D_MODEL ** -0.5
    q_norm_a = 1.0 + 0.02 * jax.random.normal(ks[3], (DEPTH, HEAD_DIM), f32)
    k_norm_a = 1.0 + 0.02 * jax.random.normal(ks[4], (DEPTH, HEAD_DIM), f32)
    q_norm_b = 1.0 + 0.02 * jax.random.normal(ks[5], (DEPTH, HEAD_DIM), f32)
    k_norm_b = 1.0 + 0.02 * jax.random.normal(ks[6], (DEPTH, HEAD_DIM), f32)
    sink_a = 0.5 * jax.random.normal(ks[7], (DEPTH, A_Q_HEADS), f32)
    rel_bias = 0.5 * jax.random.normal(ks[8], (N_BUCKETS, REL_HEADS), f32)
    w_branch_a = jax.random.normal(ks[9], (DEPTH, A_WIDTH, D_MODEL), f32) * A_WIDTH ** -0.5
    w_branch_b = jax.random.normal(ks[10], (DEPTH, B_WIDTH, D_MODEL), f32) * B_WIDTH ** -0.5
    b_merge = 0.1 * jax.random.normal(ks[11], (DEPTH, N_BRANCHES, D_MODEL), f32)
    w_out = jax.random.normal(ks[12], (DEPTH, D_MODEL, D_MODEL), f32) * D_MODEL ** -0.5
    return {"x": x, "norm_gain": norm_gain, "w_in": w_in, "q_norm_a": q_norm_a,
            "k_norm_a": k_norm_a, "q_norm_b": q_norm_b, "k_norm_b": k_norm_b,
            "sink_a": sink_a, "rel_bias": rel_bias, "w_branch_a": w_branch_a,
            "w_branch_b": w_branch_b, "b_merge": b_merge, "w_out": w_out}

def second_block(x, norm_gain, w_in, q_norm_a, k_norm_a, q_norm_b, k_norm_b, sink_a,
              rel_bias, w_branch_a, w_branch_b, b_merge, w_out):
    bsz, S, D = x.shape
    n_groups = len(B_GROUPS)
    scale = HEAD_DIM ** -0.5
    split_idx = [int(i) for i in np.cumsum(PROJ_SIZES)[:-1]]
    for layer in range(DEPTH):
        h = rms_norm(x, norm_gain[layer])
        proj = h @ w_in[layer]
        qa, ka, va, qb, kb, vb, ga, gb, mg = jnp.split(proj, split_idx, axis=-1)

        qa = head_rms_norm(qa.reshape(bsz, S, A_Q_HEADS, HEAD_DIM), q_norm_a[layer]) * scale
        ka = head_rms_norm(ka.reshape(bsz, S, A_KV_HEADS, HEAD_DIM), k_norm_a[layer])
        va = va.reshape(bsz, S, A_KV_HEADS, HEAD_DIM)
        ya, _ = banded_attention(qa, ka, va, A_WINDOW, 1, rel_bias[:, :A_Q_HEADS], sink_a[layer])
        ya = ya.reshape(bsz, S, A_WIDTH) * jax.nn.silu(ga)

        qb = head_rms_norm(qb.reshape(bsz, S, n_groups, B_HEADS_PER_GROUP, HEAD_DIM), q_norm_b[layer]) * scale
        kb = head_rms_norm(kb.reshape(bsz, S, n_groups, B_HEADS_PER_GROUP, HEAD_DIM), k_norm_b[layer])
        vb = vb.reshape(bsz, S, n_groups, B_HEADS_PER_GROUP, HEAD_DIM)
        outs = []
        lses = []
        for g, (window, dilation) in enumerate(B_GROUPS):
            c0 = A_Q_HEADS + g * B_HEADS_PER_GROUP
            o, l = dilated_group(qb[:, :, g], kb[:, :, g], vb[:, :, g], window, dilation,
                                 rel_bias[:, c0:c0 + B_HEADS_PER_GROUP])
            outs.append(o)
            lses.append(l)
        alpha = jax.nn.softmax(jnp.stack(lses, axis=0), axis=0)
        yb = jnp.sum(alpha[..., None].astype(x.dtype) * jnp.stack(outs, axis=0), axis=0)
        yb = yb.reshape(bsz, S, B_WIDTH) * jax.nn.silu(gb)

        br_a = ya @ w_branch_a[layer]
        br_b = yb @ w_branch_b[layer]
        gates = jax.nn.sigmoid(mg.reshape(bsz, S, N_BRANCHES, D).astype(jnp.float32)
                               + b_merge[layer].astype(jnp.float32)).astype(x.dtype)
        merged = gates[:, :, 0] * br_a + gates[:, :, 1] * br_b
        x = x + merged @ w_out[layer]
    return x


def setup_inputs(seed=0):
    out = dict(first_inputs(seed))
    for name, value in second_inputs(seed + 1).items():
        if name != "x":
            out[name + "_2"] = value
    return out


def reference(
    x, norm_mix_g, w_in, shift_mu, sb_out_g, rw_w0, rw_w2, rw_a0, rw_a2, rw_g2, rw_k_k, rw_k_a,
    rw_r_k, rw_ln_w, rw_ln_b, w_out, norm_ffn_g, router_grp_w, router_grp_b, router_exp_w,
    router_exp_b, exp_w_gate, exp_w_up, exp_w_down, final_norm_g, norm_gain_2, w_in_2,
    q_norm_a_2, k_norm_a_2, q_norm_b_2, k_norm_b_2, sink_a_2, rel_bias_2, w_branch_a_2,
    w_branch_b_2, b_merge_2, w_out_2,
):
    x = first_block(
        x, norm_mix_g, w_in, shift_mu, sb_out_g, rw_w0, rw_w2, rw_a0, rw_a2, rw_g2, rw_k_k,
        rw_k_a, rw_r_k, rw_ln_w, rw_ln_b, w_out, norm_ffn_g, router_grp_w, router_grp_b,
        router_exp_w, router_exp_b, exp_w_gate, exp_w_up, exp_w_down, final_norm_g,
    )
    return second_block(
        x, norm_gain_2, w_in_2, q_norm_a_2, k_norm_a_2, q_norm_b_2, k_norm_b_2, sink_a_2,
        rel_bias_2, w_branch_a_2, w_branch_b_2, b_merge_2, w_out_2,
    )


_drawn_inputs = setup_inputs


def setup_inputs(seed=0):
    import zlib

    import numpy as np

    out = dict(_drawn_inputs(seed))
    spreads = {}
    factors = {'sb_out_g': 3.172,
     'rw_w2': 4.104,
     'rw_a0': 3.041,
     'rw_k_k': 3.72,
     'rw_k_a': 4.116,
     'rw_ln_w': 3.579,
     'rw_ln_b': 4.055,
     'router_grp_b': 6.473,
     'router_exp_b': 5.078,
     'final_norm_g': 2.838,
     'norm_gain_2': 8.0,
     'q_norm_a_2': 8.0,
     'k_norm_a_2': 8.0,
     'q_norm_b_2': 8.0,
     'k_norm_b_2': 8.0,
     'sink_a_2': 8.0,
     'b_merge_2': 8.0}
    for name, (base, spread) in spreads.items():
        noise = np.random.default_rng([zlib.crc32(name.encode()), seed]).standard_normal(out[name].shape)
        drawn = base * np.exp(spread * noise) if base else spread * noise
        out[name] = jnp.asarray(drawn.astype(out[name].dtype))
    for name, factor in factors.items():
        out[name] = (out[name] * factor).astype(out[name].dtype)
    return out
```

```python
from contextlib import ExitStack

import numpy as np

import concourse.bass as bass
from concourse import mybir

F32 = mybir.dt.float32
I32 = mybir.dt.int32
U32 = mybir.dt.uint32
ALU = mybir.AluOpType
ACT = mybir.ActivationFunctionType
AX_X = mybir.AxisListType.X

P = 128
S = 512
TT = S // P
D = 1024
KC = D // P
NH = 8
HD = 64
HW = NH * HD
FT = HW // P
SB_IN = 3 * HW
RW_IN = 3 * HW + 64 + 64 + 128
RT = RW_IN // P
EPS = 1e-6
GN_EPS = 64e-5
DECAY = float(np.exp(-0.5))
NEG = -1e30
LOG_BITS = 30
CH = P
NC = S // CH

NG, EPG = 4, 8
NE = NG * EPG
DE = 256
CAP = 64

PARAM_ROWS = [("norm_mix_g", 8), ("shift_mu", RT), ("sb_out_g", 4), ("rw_w0", 4), ("rw_a0", 4), ("rw_k_k", 4),
              ("rw_k_a", 4), ("rw_r_k", 4), ("rw_ln_w", 4), ("rw_ln_b", 4), ("norm_gain_2", 8), ("b_merge_2", 16),
              ("q_norm_a_2", 1), ("k_norm_a_2", 1), ("q_norm_b_2", 1), ("k_norm_b_2", 1)]
PARAM_AT = {}
_row = 0
for _name, _n in PARAM_ROWS:
    PARAM_AT[_name] = _row
    _row += _n
N_PARAMS = _row


class Scope:

    ended = []

    def __init__(self, nc):
        self.nc = nc
        self.stack = ExitStack()
        self.own = []

    def __enter__(self):
        return self

    def __exit__(self, *e):
        Scope.ended += self.own
        self.own = []
        return self.stack.__exit__(*e)

    def sb(self, name, shape, dt=F32):
        return self.stack.enter_context(self.nc.sbuf_tensor(name, shape, dt))

    def ps(self, name, n=512):
        return self.stack.enter_context(self.nc.psum_tensor(name, [P, n], F32))

    def sem(self, name):
        self.own.append(self.nc.alloc_semaphore(name))
        return self.own[-1]

    def sems(self, name, n):
        return [self.sem(f"{name}{i}") for i in range(n)]


def recycle(nc):
    nc.clear_and_free_semaphores(Scope.ended)
    Scope.ended = []
    nc.all_engine_barrier()


def setup_constants(nc, A, const):
    with Scope(nc) as s:
        rows = s.sb("param_rows", [P, P])
        pst = s.ps("param_ps")
        loaded = s.sem("params_loaded")
        padded = s.sem("param_rows_padded")
        turned = s.sem("params_turned")
        copied = s.sem("params_copied")
        made = s.sem("masks_made")
        ident, par = const["ident"], const["par"]
        n_loads = 0
        for name, n in PARAM_ROWS:
            n_loads += 2 if "_norm_" in name else 1
        with nc.Block() as block:

            @block.sync
            def _(sp):
                sp.dma_start(const["h"][:, :, :], A["x"].rearrange("b (c p) d -> p (b c) d", p=P)).then_inc(const["x_loaded"], 16)
                sp.wait_ge(padded, 1)
                for name, n in PARAM_ROWS:
                    r = PARAM_AT[name]
                    if "_norm_" in name:
                        for half in range(2):
                            sp.dma_start(rows[r:r + 1, half * HD:(half + 1) * HD], A[name]).then_inc(loaded, 16)
                    else:
                        src = A[name]
                        if len(src.shape) == 3:
                            src = src.rearrange("l a b -> l (a b)")
                        sp.dma_start(rows[r:r + n, :], src.rearrange("l (n p) -> (l n) p", p=P)).then_inc(loaded, 16)
                sp.dma_start(const["ffn_g"][:, :], A["norm_ffn_g"][0:1, :].broadcast_to([P, D])).then_inc(const["row_params"], 16)
                sp.dma_start(const["fin_g"][:, :], A["final_norm_g"].rearrange("(a d) -> a d", a=1).broadcast_to([P, D])).then_inc(const["row_params"], 16)

            @block.gpsimd
            def _(pool):
                n = [0]

                def step(ins):
                    n[0] += 1
                    ins.then_inc(made, 1)
                    pool.wait_ge(made, n[0])

                step(pool.memset(const["eps"][:, :], EPS))
                step(pool.memset(const["gn_eps"][:, :], GN_EPS))
                step(pool.memset(const["log_shift"][:, :], float(0.5 * LOG_BITS * np.log(2.0))))
                step(pool.memset(ident[:, :], 0.0))
                step(pool.affine_select(out=ident[:, :], in_=ident[:, :], compare_op=ALU.not_equal, fill=1.0, base=0,
                                        pattern=[[-1, P]], channel_multiplier=1))
                cm = const["causal"]
                step(pool.memset(cm[:, :, :], 1.0))
                for k in range(4):
                    step(pool.affine_select(out=cm[:, k, :], in_=cm[:, k, :], fill=0.0, base=0, pattern=[[1, P]],
                                            compare_op=(ALU.is_gt, ALU.is_ge)[k % 2], channel_multiplier=-1))
                step(pool.memset(const["neg_causal"][:, :], 0.0))
                step(pool.affine_select(out=const["neg_causal"][:, :], in_=const["neg_causal"][:, :], fill=NEG, base=0,
                                        pattern=[[1, P]], compare_op=ALU.is_gt, channel_multiplier=-1))
                step(pool.memset(const["minus_ones"][:, :], -1.0))
                step(pool.memset(const["suffix"][:, :], -1.0))
                step(pool.affine_select(out=const["suffix"][:, :], in_=const["suffix"][:, :], fill=0.0, base=0,
                                        pattern=[[-1, P]], compare_op=ALU.is_ge, channel_multiplier=1))
                step(pool.memset(const["heads"][:, :], 0.0))
                step(pool.memset(const["heads"][0:HD, 0:HD], 1.0))
                step(pool.memset(const["heads"][HD:P, HD:P], 1.0))
                for l in range(7):
                    m = 1 << l
                    lv = const["level"][:, l, :]
                    step(pool.memset(lv, 0.0))
                    v = lv.rearrange("p (b h x) -> p b h x", h=2, x=m)[:, :, 0, :]
                    step(pool.memset(v, 1.0))
                    nb = P // (2 * m)
                    step(pool.affine_select(out=v, in_=v, fill=0.0, base=-m, pattern=[[-2 * m, nb], [0, m]],
                                            compare_op=ALU.is_ge, channel_multiplier=1))
                    step(pool.affine_select(out=v, in_=v, fill=0.0, base=2 * m, pattern=[[2 * m, nb], [0, m]],
                                            compare_op=ALU.is_gt, channel_multiplier=-1))
                const["n_masks"] = n[0]

            @block.tensor
            def _(pe):
                pe.wait_ge(made, 5)
                pe.wait_ge(loaded, 16 * n_loads)
                pe.transpose(pst[:, 0:P], rows[:, :], ident[:, :]).then_inc(turned, 1)

            @block.vector
            def _(dve):
                dve.memset(rows[:, :], 0.0).then_inc(padded, 1)
                dve.wait_ge(turned, 1)
                dve.tensor_copy(par[:, :], pst[:, 0:P]).then_inc(copied, 1)
                mu = PARAM_AT["shift_mu"]
                dve.wait_ge(copied, 1)
                dve.tensor_scalar(const["one_minus_mu"][:, :], par[:, mu:mu + RT], -1.0, 1.0, ALU.mult, ALU.add).then_inc(copied, 1)
                ka = PARAM_AT["rw_k_a"]
                dve.tensor_scalar(const["one_minus_ka"][:, :], par[:, ka:ka + FT], -1.0, 1.0, ALU.mult, ALU.add).then_inc(copied, 1)
                dve.wait_ge(copied, 3)


def norm_to_features(nc, src, gain, dst, const, tag, x_loaded=None):
    with Scope(nc) as s:
        sq = s.sb(tag + "_sq", [P, D])
        xs = s.sb(tag + "_scaled", [P, TT, D])
        ss = s.sb(tag + "_ss", [P, TT])
        rs = s.sb(tag + "_rstd", [P, TT])
        banks = [s.ps(f"{tag}_ps{i}") for i in range(4)]
        squared = s.sem(tag + "_squares_summed")
        rstd = s.sem(tag + "_rstd_ready")
        scaled = s.sem(tag + "_tokens_scaled")
        turned = s.sem(tag + "_chunk_turned")
        even_st = s.sem(tag + "_even_chunk_stored")
        odd_st = s.sem(tag + "_odd_chunk_stored")
        ident, par = const["ident"], const["par"]
        with nc.Block() as block:

            @block.scalar
            def _(act):
                if x_loaded is not None:
                    act.wait_ge(x_loaded, 16)
                for c in range(TT):
                    if c:
                        act.wait_ge(squared, c)
                    act.activation(sq[:, :], src[:, c, :], ACT.Square, accum_out=ss[:, c:c + 1]).then_inc(squared, 1)
                act.wait_ge(rstd, 1)
                act.activation(ss[:, :], ss[:, :], ACT.Sqrt).then_inc(rstd, 1)
                for k in range(0, KC, 2):
                    act.wait_ge(turned, k + 1)
                    act.activation(dst[:, k, :], banks[k % 4][:, :], ACT.Copy,
                                   scale=par[:, gain + k:gain + k + 1]).then_inc(even_st, 1)

            @block.vector
            def _(dve):
                dve.wait_ge(squared, TT)
                dve.tensor_scalar(ss[:, :], ss[:, :], 1.0 / D, EPS, ALU.mult, ALU.add).then_inc(rstd, 1)
                dve.wait_ge(rstd, 2)
                dve.reciprocal(rs[:, :], ss[:, :]).then_inc(rstd, 1)
                dve.wait_ge(rstd, 3)
                for c in range(TT):
                    dve.tensor_scalar(xs[:, c, :], src[:, c, :], rs[:, c:c + 1], None, ALU.mult).then_inc(scaled, 1)
                for k in range(1, KC, 2):
                    dve.wait_ge(turned, k + 1)
                    dve.tensor_scalar(dst[:, k, :], banks[k % 4][:, :], par[:, gain + k:gain + k + 1], None,
                                      ALU.mult).then_inc(odd_st, 1)

            @block.tensor
            def _(pe):
                for k in range(KC):
                    if k >= 4:
                        pe.wait_ge((even_st, odd_st)[k % 2], (k - 4) // 2 + 1)
                    for c in range(TT):
                        pe.wait_ge(scaled, c + 1)
                        t = pe.transpose(banks[k % 4][:, c * P:(c + 1) * P], xs[:, c, k * P:(k + 1) * P], ident[:, :])
                    t.then_inc(turned, 1)


def project_first(nc, A, xnT, um, qk, v, const):
    UNIT = 256
    NSLOT = 4
    NBANK = 6
    w = A["w_in"].rearrange("l (k p) n -> p (l k) n", p=P)
    units = [SB_IN + UNIT * i for i in range(RW_IN // UNIT)] + [UNIT * i for i in range(SB_IN // UNIT)]
    tiles = [(SB_IN + P * i) for i in range(RT)] + [P * i for i in range(2 * FT)]
    with Scope(nc) as s:
        ring = s.sb("w_in_ring", [P, NSLOT, KC, UNIT])
        shifted = s.sb("shifted", [P, 2, S])
        banks = [s.ps(f"u_ps{i}") for i in range(NBANK)]
        vbank = banks[0:4]
        loaded = s.sems("w_in_loaded", NSLOT)
        ready = s.sem("u_tile_ready")
        sh_zero = s.sem("shift_zeroed")
        sh = s.sem("u_shifted")
        mixed = s.sem("u_mixed")
        qk_st = s.sem("qk_stored")
        v_ready = s.sem("v_ready")
        v_st = s.sem("v_stored")
        with nc.Block() as block:

            @block.sync
            def _(sp):
                for i, col in enumerate(units):
                    if i >= NSLOT:
                        sp.wait_ge(ready, 2 * (i - NSLOT + 1))
                    sp.dma_start(ring[:, i % NSLOT, :, :], w[:, :, col:col + UNIT]).then_inc(loaded[i % NSLOT], 16)

            @block.tensor
            def _(pe):
                n = 0
                for i, col in enumerate(units):
                    pe.wait_ge(loaded[i % NSLOT], 16 * (i // NSLOT + 1))
                    if i < len(tiles) * P // UNIT:
                        for half in range(2):
                            if n >= NBANK:
                                done = n - NBANK + 1
                                pe.wait_ge(mixed, min(done, RT))
                                if done > RT:
                                    pe.wait_ge(qk_st, done - RT)
                            for k in range(KC):
                                m = pe.matmul(banks[n % NBANK][:, :], ring[:, i % NSLOT, k, half * P:(half + 1) * P],
                                              xnT[:, k, :], start=(k == 0), stop=(k == KC - 1))
                            m.then_inc(ready, 1)
                            n += 1
                    else:
                        part = i - len(tiles) * P // UNIT
                        if part == 0:
                            pe.wait_ge(qk_st, 2 * FT)
                        for c in range(TT):
                            for k in range(KC):
                                m = pe.matmul(vbank[c][:, part * UNIT:(part + 1) * UNIT], xnT[:, k, c * P:(c + 1) * P],
                                              ring[:, i % NSLOT, k, :], start=(k == 0), stop=(k == KC - 1))
                            if c == TT - 1 and part == 1:
                                m.then_inc(v_ready, 1)

            @block.scalar
            def _(act):
                mu = PARAM_AT["shift_mu"]
                act.wait_ge(sh_zero, 1)
                for j in range(RT):
                    act.wait_ge(ready, j + 1)
                    if j >= 2:
                        act.wait_ge(mixed, j - 1)
                    act.activation(shifted[:, j % 2, 1:S], banks[j % NBANK][:, 0:S - 1], ACT.Copy,
                                   scale=par_col(const, mu + j)).then_inc(sh, 1)
                for j in range(2 * FT):
                    n = RT + j
                    act.wait_ge(ready, n + 1)
                    act.activation(qk[:, j, :], banks[n % NBANK][:, :], ACT.Copy,
                                   scale=HD ** -0.5 if j < FT else 1.0).then_inc(qk_st, 1)

            @block.vector
            def _(dve):
                dve.memset(shifted[:, :, 0:1], 0.0).then_inc(sh_zero, 1)
                for j in range(RT):
                    dve.wait_ge(sh, j + 1)
                    dve.scalar_tensor_tensor(out=um[:, j, :], in0=banks[j % NBANK][:, :],
                                             scalar=const["one_minus_mu"][:, j:j + 1], in1=shifted[:, j % 2, :],
                                             op0=ALU.mult, op1=ALU.add).then_inc(mixed, 1)
                dve.wait_ge(v_ready, 1)
                for c in range(TT):
                    dve.tensor_copy(v[:, c, :], vbank[c][:, :]).then_inc(v_st, 1)


def par_col(const, i):
    return const["par"][:, i:i + 1]


def normalize_heads(nc, const, tiles, tag):
    with Scope(nc) as s:
        sq = s.sb(tag + "_sq", [P, 2, S])
        rs = s.sb(tag + "_rstd", [P, 2, S])
        banks = [s.ps(f"{tag}_ps{i}") for i in range(2)]
        squared = s.sem("head_squares")
        summed = s.sem("head_sums")
        logged = s.sem("head_logs")
        rstd = s.sem("head_rstd")
        scaled = s.sem("head_scaled")
        n = len(tiles)
        with nc.Block() as block:

            @block.scalar
            def _(act):
                act.preload_act_table_set("natural_log_exp_and_others")
                for j in range(n + 1):
                    if j < n:
                        if j >= 2:
                            act.wait_ge(summed, j - 1)
                        act.activation(sq[:, j % 2, :], tiles[j][0], ACT.Square).then_inc(squared, 1)
                    if j >= 1:
                        i = j - 1
                        act.wait_ge(summed, i + 1)
                        if i >= 2:
                            act.wait_ge(scaled, i - 1)
                        act.activation(rs[:, i % 2, :], banks[i % 2][:, :], ACT.Ln, scale=1.0 / HD,
                                       bias=const["eps"][:, :]).then_inc(logged, 1)
                        act.wait_ge(logged, i + 1)
                        act.activation(rs[:, i % 2, :], rs[:, i % 2, :], ACT.Exp, scale=-0.5).then_inc(rstd, 1)

            @block.tensor
            def _(pe):
                for j in range(n):
                    pe.wait_ge(squared, j + 1)
                    if j >= 2:
                        pe.wait_ge(logged, j - 1)
                    pe.matmul(banks[j % 2][:, :], const["heads"][:, :], sq[:, j % 2, :], start=True, stop=True).then_inc(summed, 1)

            @block.vector
            def _(dve):
                for j in range(n):
                    src, gain, dst = tiles[j]
                    dve.wait_ge(rstd, j + 1)
                    dve.scalar_tensor_tensor(out=dst, in0=src, scalar=gain, in1=rs[:, j % 2, :],
                                             op0=ALU.mult, op1=ALU.mult).then_inc(scaled, 1)


def stick_breaking(nc, const, qk, v, mixT):
    OFF = [0, 512, 1024, 896]
    N = 1280
    with Scope(nc) as outer, Scope(nc) as s:
        raw = outer.sb("stick_out", [P, FT, S])
        zt = [s.stack.enter_context(nc.psum_tensor(f"z_ps{i}", [P, 3 * 512], F32)) for i in range(2)]
        avt = [s.ps(f"av_ps{i}") for i in range(2)]
        ln = s.sb("ln_rest", [P, 2, N])
        spl = s.sb("softplus", [P, 2, N])
        wt = s.sb("stick_weights", [P, 2, N])
        z_ready = s.sem("z_ready")
        abs_ready = s.sem("abs_ready")
        e_ready = s.sem("exp_ready")
        l_ready = s.sem("log_ready")
        sp_ready = s.sem("softplus_ready")
        masked = s.sem("softplus_masked")
        suf_ready = s.sem("suffix_ready")
        neg_ready = s.sem("diagonal_masked")
        w_ready = s.sem("stick_weights_ready")
        av_ready = s.sem("stick_av_ready")
        raw_ready = s.sem("stick_out_ready")

        def blk(t, i, t0=None):
            t0 = i if t0 is None else t0
            return t[:, OFF[i] + (t0 - i) * P:OFF[i] + (TT - i) * P]

        with nc.Block() as block:

            @block.tensor
            def _(pe):
                def scores(h):
                    f, b = h // 2, HD * (h % 2)
                    if h >= 2:
                        pe.wait_ge(w_ready, h - 1)
                    for i in (0, 1, 3, 2):
                        m = pe.matmul(blk(zt[h % 2], i), qk[b:b + HD, FT + f, i * P:(i + 1) * P], qk[b:b + HD, f, i * P:S],
                                      start=(i != 3), stop=True, skip_group_check=True)
                    m.then_inc(z_ready, 1)

                def suffix(h):
                    pe.wait_ge(masked, 4 * (h + 1))
                    for i in range(TT):
                        for j in range(i, TT):
                            m = pe.matmul(blk(zt[h % 2], i, j), const["suffix" if j == i else "minus_ones"][:, :],
                                          blk(spl[:, h % 2, :], j), start=False, stop=True, skip_group_check=True)
                    m.then_inc(suf_ready, 1)

                def values(h):
                    b = HD * (h % 2)
                    pe.wait_ge(w_ready, h + 1)
                    if h >= 4:
                        pe.wait_ge(raw_ready, h // 2 - 1)
                    for i in range(TT):
                        m = pe.matmul(avt[h // 2 % 2][b:b + HD, i * P:S], v[:, i, h * HD:(h + 1) * HD],
                                      blk(wt[:, h % 2, :], i), start=(i == 0), stop=(i == TT - 1))
                    m.then_inc(av_ready, 1)

                scores(0)
                scores(1)
                for h in range(NH):
                    suffix(h)
                    if h >= 1:
                        values(h - 1)
                    if h + 2 < NH:
                        scores(h + 2)
                values(NH - 1)

            @block.vector
            def _(dve):
                def softplus(h):
                    dve.wait_ge(l_ready, h + 1)
                    if h >= 2:
                        dve.wait_ge(suf_ready, h - 1)
                    dve.scalar_tensor_tensor(out=spl[:, h % 2, :], in0=zt[h % 2][:, 0:N], scalar=0.0, in1=ln[:, h % 2, :],
                                             op0=ALU.max, op1=ALU.add).then_inc(sp_ready, 1)

                def mask(h):
                    dve.wait_ge(suf_ready, h + 1)
                    for i in range(TT):
                        d = zt[h % 2][:, OFF[i]:OFF[i] + P]
                        dve.tensor_tensor(d, d, const["neg_causal"][:, :], ALU.add).then_inc(neg_ready, 1)

                softplus(0)
                for h in range(NH):
                    if h + 1 < NH:
                        softplus(h + 1)
                    mask(h)

            @block.gpsimd
            def _(pool):
                for h in range(NH):
                    pool.wait_ge(sp_ready, h + 1)
                    for i in range(TT):
                        d = spl[:, h % 2, OFF[i]:OFF[i] + P]
                        pool.tensor_tensor(d, d, const["causal"][:, 0, :], ALU.mult).then_inc(masked, 1)

            @block.scalar
            def _(act):
                def log_rest(h):
                    x = ln[:, h % 2, :]
                    act.wait_ge(z_ready, h + 1)
                    if h >= 2:
                        act.wait_ge(sp_ready, h - 1)
                    act.activation(x, zt[h % 2][:, 0:N], ACT.Abs).then_inc(abs_ready, 1)
                    act.wait_ge(abs_ready, h + 1)
                    act.activation(x, x, ACT.Exp, scale=-1.0).then_inc(e_ready, 1)
                    act.wait_ge(e_ready, h + 1)
                    act.activation(x, x, ACT.Ln, bias=1.0).then_inc(l_ready, 1)

                def weights(h):
                    act.wait_ge(neg_ready, 4 * (h + 1))
                    if h >= 2:
                        act.wait_ge(av_ready, h - 1)
                    act.activation(wt[:, h % 2, :], zt[h % 2][:, 0:N], ACT.Exp).then_inc(w_ready, 1)

                act.preload_act_table_set("natural_log_exp_and_others")
                log_rest(0)
                for h in range(NH):
                    if h + 1 < NH:
                        log_rest(h + 1)
                    weights(h)
                    if h % 2 == 0 and h >= 2:
                        f = h // 2 - 1
                        act.wait_ge(av_ready, h)
                        act.activation(raw[:, f, :], avt[f % 2][:, :], ACT.Copy).then_inc(raw_ready, 1)
                act.wait_ge(av_ready, NH)
                act.activation(raw[:, FT - 1, :], avt[(FT - 1) % 2][:, :], ACT.Copy).then_inc(raw_ready, 1)

        s.stack.close()
        g = PARAM_AT["sb_out_g"]
        normalize_heads(nc, const, [(raw[:, f, :], par_col(const, g + f), mixT[:, f, :]) for f in range(FT)],
                        "sbn")


def rwkv_features(nc, A, const, um, R):
    r, k, vv = um[:, 0:FT, :], um[:, FT:2 * FT, :], um[:, 2 * FT:3 * FT, :]
    with Scope(nc) as s:
        wa2 = s.sb("lora_w2_a2", [P, HW])
        g2 = s.sb("lora_g2", [P, HW])
        lora = s.sb("lora_in", [P, 2, S])
        sig = s.sb("decay_sigmoid", [P, FT, S])
        rate = s.sb("rate", [P, FT, S])
        kkn = s.sb("kkn", [P, FT, S])
        cum = s.sb("decay_sums", [P, FT, S])
        e1 = s.sb("e1", [P, FT, S])
        e2 = s.sb("e2", [P, FT, S])
        ones0 = s.sb("chunk_starts", [P, S])
        banks = [s.ps(f"lora_ps{i}") for i in range(8)]
        loaded = s.sem("lora_loaded")
        lora_in = s.sem("lora_in_ready")
        prod = s.sem("lora_product")
        act_st = s.sem("lora_act_stored")
        gate_st = s.sem("gate_stored")
        sq_r = s.sem("kk_squared")
        ss_r = s.sem("kk_summed")
        mx = s.sem("kk_sum_bounded")
        rs_l = s.sem("kk_log")
        rs_r = s.sem("kk_rstd")
        dv = s.sem("rwkv_vector_step")
        ex = s.sem("decay_exp_ready")
        bz = s.sem("bonus_summed")
        start = s.sem("chunk_starts_ready")
        names = {}
        kk_col = PARAM_AT["rw_k_k"]
        with nc.Block() as block:

            @block.sync
            def _(sp):
                sp.dma_start(wa2[0:64, :], A["rw_w2"][0]).then_inc(loaded, 16)
                sp.dma_start(wa2[64:128, :], A["rw_a2"][0]).then_inc(loaded, 16)
                sp.dma_start(g2[:, :], A["rw_g2"][0]).then_inc(loaded, 16)

            @block.gpsimd
            def _(pool):
                pool.memset(ones0[:, :], 1.0).then_inc(start, 1)
                pool.wait_ge(start, 1)
                pool.memset(ones0[:, 0:S:CH], 0.0).then_inc(start, 1)

            @block.vector
            def _(dve):
                n = [0]

                def step(name, ins):
                    n[0] += 1
                    names[name] = n[0]
                    ins.then_inc(dv, 1)
                    return n[0]

                for f in range(FT):
                    dve.wait_ge(ss_r, f + 1)
                    dve.tensor_scalar(e2[:, f, :], banks[f][:, :], 1e-24, None, ALU.max).then_inc(mx, 1)
                dve.wait_ge(start, 2)
                for f in range(FT):
                    dve.wait_ge(act_st, f + 1)
                    a = step("cum", dve.tensor_tensor_scan(cum[:, f, :], ones0[:, :], sig[:, f, :], 0.0, ALU.mult, ALU.add))
                dve.wait_ge(dv, a)
                cum3 = cum[:, :, :].rearrange("p f (c t) -> p (f c) t", t=CH)
                sig3 = sig[:, :, :].rearrange("p f (c t) -> p (f c) t", t=CH)
                a = step("ends", dve.tensor_copy(R["ends"][:, :], cum3[:, :, CH - 1]))
                dve.wait_ge(dv, a)
                ends = R["ends"][:, :].unsqueeze(2).to_broadcast([P, FT * NC, CH])
                a = step("csc", dve.scalar_tensor_tensor(out=cum3, in0=ends, scalar=-0.5, in1=cum3, op0=ALU.mult, op1=ALU.add))
                dve.wait_ge(dv, a)
                step("csx", dve.tensor_tensor(sig3, cum3, sig3, ALU.subtract))
                dve.wait_ge(rs_r, 1)
                for f in range(FT):
                    a = step("kkn", dve.scalar_tensor_tensor(out=kkn[:, f, :], in0=k[:, f, :], scalar=par_col(const, kk_col + f),
                                                             in1=e2[:, f, :], op0=ALU.mult, op1=ALU.mult))
                dve.wait_ge(act_st, 2 * FT)
                for f in range(FT):
                    b = step("fac", dve.tensor_scalar(e1[:, f, :], rate[:, f, :], par_col(const, PARAM_AT["rw_k_a"] + f),
                                                      const["one_minus_ka"][:, f:f + 1], ALU.mult, ALU.add))
                dve.wait_ge(dv, b)
                a = step("k2", dve.tensor_tensor(k, k, e1[:, :, :], ALU.mult))
                a = step("b", dve.tensor_tensor(rate[:, :, :], kkn[:, :, :], rate[:, :, :], ALU.mult))
                dve.wait_ge(dv, a)
                names["kkn"] = a
                c4 = lambda x: x.rearrange("p f (c t) -> p (f c) t", t=CH)
                KR = R["kr"]
                dve.wait_ge(ex, 1)
                step("krk", dve.tensor_tensor(KR[:, :, 0, :], c4(kkn[:, :, :]), sig3, ALU.mult))
                dve.wait_ge(ex, 3)
                step("krr", dve.tensor_tensor(KR[:, :, 1, :], c4(r), c4(e1[:, :, :]), ALU.mult))
                step("bh", dve.tensor_tensor(R["bh"][:, :, :], rate[:, :, :], e2[:, :, :], ALU.mult))
                a = step("kh", dve.tensor_tensor(R["kh"][:, :, :], k, e2[:, :, :], ALU.mult))
                dve.wait_ge(dv, a)
                for f in range(FT):
                    step("rk", dve.scalar_tensor_tensor(out=rate[:, f, :], in0=r[:, f, :], scalar=par_col(const, PARAM_AT["rw_r_k"] + f),
                                                        in1=k[:, f, :], op0=ALU.mult, op1=ALU.mult))
                for f in range(FT):
                    dve.wait_ge(bz, f + 1)
                    step("bonus", dve.tensor_tensor(R["bonus"][:, f, :], banks[f][:, :], vv[:, f, :], ALU.mult))

            @block.tensor
            def _(pe):
                pe.wait_ge(sq_r, FT)
                for f in range(FT):
                    pe.matmul(banks[f][:, :], const["heads"][:, :], e1[:, f, :], start=True, stop=True).then_inc(ss_r, 1)
                pe.wait_ge(loaded, 48)
                pe.wait_ge(lora_in, 3)
                for f in range(FT):
                    cols = slice(f * P, (f + 1) * P)
                    pe.matmul(banks[4 + f][:, :], wa2[0:64, cols], lora[0:64, 0, :], start=True, stop=True).then_inc(prod, 1)
                for f in range(FT):
                    cols = slice(f * P, (f + 1) * P)
                    pe.wait_ge(mx, f + 1)
                    pe.matmul(banks[f][:, :], wa2[64:128, cols], lora[64:128, 0, :], start=True, stop=True).then_inc(prod, 1)
                for f in range(FT):
                    cols = slice(f * P, (f + 1) * P)
                    pe.wait_ge(act_st, f + 1)
                    pe.matmul(banks[4 + f][:, :], g2[:, cols], lora[:, 1, :], start=True, stop=True).then_inc(prod, 1)
                pe.wait_ge(dv, names["rk"])
                for f in range(FT):
                    pe.wait_ge(act_st, 4 + f + 1)
                    pe.matmul(banks[f][:, :], const["heads"][:, :], rate[:, f, :], start=True, stop=True).then_inc(bz, 1)

            @block.scalar
            def _(act):
                for f in range(FT):
                    act.activation(e1[:, f, :], k[:, f, :], ACT.Square, scale=par_col(const, kk_col + f)).then_inc(sq_r, 1)
                act.activation(lora[0:64, 0, :], um[0:64, 3 * FT, :], ACT.Tanh).then_inc(lora_in, 1)
                act.activation(lora[64:128, 0, :], um[64:128, 3 * FT, :], ACT.Copy).then_inc(lora_in, 1)
                act.activation(lora[:, 1, :], um[:, 3 * FT + 1, :], ACT.Sigmoid).then_inc(lora_in, 1)
                for f in range(FT):
                    act.wait_ge(prod, f + 1)
                    act.activation(sig[:, f, :], banks[4 + f][:, :], ACT.Sigmoid,
                                   bias=par_col(const, PARAM_AT["rw_w0"] + f)).then_inc(act_st, 1)
                for f in range(FT):
                    act.wait_ge(prod, 4 + f + 1)
                    act.activation(rate[:, f, :], banks[f][:, :], ACT.Sigmoid,
                                   bias=par_col(const, PARAM_AT["rw_a0"] + f)).then_inc(act_st, 1)
                act.preload_act_table_set("natural_log_exp_and_others")
                act.wait_ge(mx, FT)
                act.activation(e2[:, :, :], e2[:, :, :], ACT.Ln, scale=float(2.0 ** LOG_BITS)).then_inc(rs_l, 1)
                act.wait_ge(rs_l, 1)
                act.activation(e2[:, :, :], e2[:, :, :], ACT.Exp, scale=-0.5, bias=const["log_shift"][:, :]).then_inc(rs_r, 1)
                for f in range(FT):
                    act.wait_ge(prod, 8 + f + 1)
                    act.activation(R["gate"][:, f, :], banks[4 + f][:, :], ACT.Copy).then_inc(gate_st, 1)
                act.wait_ge(dv, names["csx"])
                act.activation(sig[:, :, :], sig[:, :, :], ACT.Exp, scale=-DECAY).then_inc(ex, 1)
                act.wait_ge(dv, names["kkn"])
                act.activation(e1[:, :, :], cum[:, :, :], ACT.Exp, scale=-DECAY).then_inc(ex, 1)
                act.activation(e2[:, :, :], cum[:, :, :], ACT.Exp, scale=DECAY).then_inc(ex, 1)
                act.activation(R["mid"][:, :], R["ends"][:, :], ACT.Exp, scale=-0.5 * DECAY).then_inc(ex, 1)


def rwkv_chunks(nc, const, um, R):
    LEVELS = 7
    G = 2 * NC
    vT = um[:, 2 * FT:3 * FT, :]
    with Scope(nc) as s:
        tok = s.sb("token_side", [P, 2, NC, 5, P])
        KK, BV, V, B, K = range(5)
        sc = s.sb("chunk_scores", [P, G, 4, CH])
        x = s.sb("inverse", [P, G, CH])
        xt = s.sb("inverse_t", [P, G, CH])
        u = s.sb("level_product", [P, G, CH])
        gh = s.sb("g_h", [P, G, 2, HD])
        s_bank = [s.ps(f"score_ps{i}") for i in range(2)]
        l_bank = [[s.ps(f"level_ps{q}{i}") for i in range(2)] for q in range(2)]
        f_bank = [s.ps(f"final_ps{i}") for i in range(2)]
        kk_st = s.sem("kk_tokens_stored")
        tok_ready, tok_st = s.sem("tokens_turned"), s.sem("tokens_stored")
        sc_ready, sc_st = s.sem("scores_ready"), s.sem("scores_stored")
        bv_ready, bv_st = s.sem("bv_ready"), s.sem("bv_stored")
        u_ready, u_st = s.sems("u_ready", 2), s.sems("u_stored", 2)
        xu_ready, ux_ready = s.sems("xu_ready", 2), s.sems("ux_ready", 2)
        x_st, xt_st = s.sems("x_stored", 2), s.sems("xt_stored", 2)
        gh_ready, gh_st = s.sem("gh_ready"), s.sem("gh_stored")
        qo_ready, mn_ready = s.sem("q_o_ready"), s.sem("m_n_ready")
        q_st, o_st, mn_st = s.sem("q_stored"), s.sem("o_stored"), s.sem("m_n_stored")
        ident = const["ident"][:, :]
        with nc.Block() as block:

            @block.tensor
            def _(pe):
                for f in range(FT):
                    t = tok[:, f % 2]
                    for c in range(NC):
                        i = NC * f + c
                        bank = f_bank[c % 2]
                        if c >= 2:
                            pe.wait_ge(tok_st, i - 1)
                        elif f:
                            pe.wait_ge(gh_st, 2 * f)
                            pe.wait_ge(q_st, 2 * f)
                            pe.wait_ge(o_st, 2 * f)
                        cs = slice(c * CH, (c + 1) * CH)
                        for j, src in enumerate((R["kr"][:, i, 0, :], vT[:, f, cs], R["bh"][:, f, cs], R["kh"][:, f, cs])):
                            m = pe.transpose(bank[:, j * P:(j + 1) * P], src, ident)
                        m.then_inc(tok_ready, 1)
                    if f:
                        pe.wait_ge(bv_st, f)
                        pe.wait_ge(mn_st, 2 * f)
                    for g in range(G):
                        c, b = g // 2, HD * (g % 2)
                        i = G * f + g
                        if g >= 2:
                            pe.wait_ge(sc_st, i - 1)
                        cs = slice(c * CH, (c + 1) * CH)
                        kr = R["kr"][b:b + HD, NC * f + c, :, :]
                        pe.matmul(s_bank[g % 2][:, 0:2 * CH], R["bh"][b:b + HD, f, cs], kr, start=True, stop=True)
                        pe.matmul(s_bank[g % 2][:, 2 * CH:4 * CH], R["kh"][b:b + HD, f, cs], kr, start=True, stop=True).then_inc(sc_ready, 1)
                    pe.wait_ge(sc_st, G * (f + 1))
                    pe.wait_ge(kk_st, NC * (f + 1))
                    pe.wait_ge(tok_st, NC * (f + 1))
                    for g in range(G):
                        m = pe.matmul(s_bank[0][:, g * HD:(g + 1) * HD], sc[:, g, 2, :], t[:, g // 2, V, (g % 2) * HD:(g % 2 + 1) * HD],
                                      start=True, stop=True)
                    m.then_inc(bv_ready, 1)
                    for l in range(LEVELS):
                        for q in range(2):
                            if l:
                                pe.wait_ge(x_st[q], 6 * f + l)
                            for g in range(4 * q, 4 * q + 4):
                                cols = slice((g % 4) * CH, (g % 4 + 1) * CH)
                                m = pe.matmul(l_bank[q][0][:, cols], sc[:, g, 0, :], x[:, g, :] if l else ident, start=True, stop=True)
                            m.then_inc(u_ready[q], 1)
                        for q in range(2):
                            pe.wait_ge(u_st[q], LEVELS * f + l + 1)
                            if l:
                                pe.wait_ge(xt_st[q], LEVELS * f + l)
                            if 0 < l < LEVELS - 1:
                                for g in range(4 * q, 4 * q + 4):
                                    cols = slice((g % 4) * CH, (g % 4 + 1) * CH)
                                    m = pe.matmul(l_bank[q][0][:, cols], xt[:, g, :], u[:, g, :], start=True, stop=True)
                                m.then_inc(xu_ready[q], 1)
                            for g in range(4 * q, 4 * q + 4):
                                cols = slice((g % 4) * CH, (g % 4 + 1) * CH)
                                m = pe.matmul(l_bank[q][1][:, cols], u[:, g, :], xt[:, g, :] if l else ident, start=True, stop=True)
                            m.then_inc(ux_ready[q], 1)
                    for q in range(2):
                        pe.wait_ge(xt_st[q], LEVELS * (f + 1))
                        pe.wait_ge(bv_st, f + 1)
                        if q:
                            pe.wait_ge(gh_st, 2 * f + q)
                        for g in range(4 * q, 4 * q + 4):
                            b = HD * (g % 2)
                            m = pe.matmul(f_bank[0][:, (g % 4) * P:(g % 4 + 1) * P], xt[:, g, :], t[:, g // 2, KK:BV + 1, b:b + HD],
                                          start=True, stop=True)
                        m.then_inc(gh_ready, 1)
                        pe.wait_ge(gh_st, 2 * f + q + 1)
                        if q:
                            pe.wait_ge(q_st, 2 * f + q)
                            pe.wait_ge(o_st, 2 * f + q)
                            pe.wait_ge(mn_st, 2 * f + q)
                        for g in range(4 * q, 4 * q + 4):
                            c, b = g // 2, HD * (g % 2)
                            qo = f_bank[1][b:b + HD, (c % 2) * 2 * CH:(c % 2 + 1) * 2 * CH]
                            pe.matmul(qo[:, 0:CH], gh[:, g, 0, :], sc[:, g, 1, :], start=True, stop=True)
                            pe.matmul(qo[:, CH:2 * CH], gh[:, g, 1, :], sc[:, g, 1, :], start=True, stop=False)
                            m = pe.matmul(qo[:, CH:2 * CH], t[:, c, V, b:b + HD], sc[:, g, 3, :], start=False, stop=True)
                        m.then_inc(qo_ready, 1)
                        for g in range(4 * q, 4 * q + 4):
                            c, b = g // 2, HD * (g % 2)
                            mn = s_bank[1][b:b + HD, (c % 2) * 2 * HD:(c % 2 + 1) * 2 * HD]
                            pe.matmul(mn[:, 0:HD], gh[:, g, 0, :], t[:, c, B, b:b + HD], start=True, stop=True)
                            pe.matmul(mn[:, HD:2 * HD], t[:, c, B, b:b + HD], gh[:, g, 1, :], start=True, stop=False)
                            m = pe.matmul(mn[:, HD:2 * HD], t[:, c, K, b:b + HD], t[:, c, V, b:b + HD], start=False, stop=True)
                        m.then_inc(mn_ready, 1)

            @block.scalar
            def _(act):
                for f in range(FT):
                    for c in range(NC):
                        i = NC * f + c
                        act.wait_ge(tok_ready, i + 1)
                        bank = f_bank[c % 2][:, :].rearrange("p (j n) -> p j n", j=4)
                        act.activation(tok[:, f % 2, c, KK, :], bank[:, 0, :], ACT.Copy).then_inc(kk_st, 1)
                        act.activation(tok[:, f % 2, c, V:K + 1, :], bank[:, 1:4, :], ACT.Copy).then_inc(tok_st, 1)
                    act.wait_ge(bv_ready, f + 1)
                    act.activation(tok[:, f % 2, :, BV, :], s_bank[0][:, :].rearrange("p (c n) -> p c n", c=NC), ACT.Copy).then_inc(bv_st, 1)
                    for q in range(2):
                        act.wait_ge(gh_ready, 2 * f + q + 1)
                        act.activation(gh[:, 4 * q:4 * q + 4, :, :].rearrange("p g k n -> p (g k n)"), f_bank[0][:, :], ACT.Copy,
                                       scale=-1.0).then_inc(gh_st, 1)
                        act.wait_ge(q_st, 2 * f + q + 1)
                        qo = f_bank[1][:, :].rearrange("p (c k t) -> p c k t", c=2, k=2)
                        act.activation(R["o"][:, f, 2 * q * CH:2 * (q + 1) * CH].rearrange("p (c t) -> p c t", c=2), qo[:, :, 1, :],
                                       ACT.Copy).then_inc(o_st, 1)
                        act.wait_ge(mn_ready, 2 * f + q + 1)
                        i = NC * f + 2 * q
                        act.activation(R["mn"][:, i:i + 2, :, :].rearrange("p c k n -> p (c k n)"), s_bank[1][:, 0:4 * HD], ACT.Copy).then_inc(mn_st, 1)

            @block.vector
            def _(dve):
                for f in range(FT):
                    if f:
                        dve.wait_ge(mn_ready, 2 * f)
                        dve.wait_ge(qo_ready, 2 * f)
                    for g in range(G):
                        dve.wait_ge(sc_ready, G * f + g + 1)
                        dve.tensor_tensor(sc[:, g, :, :].rearrange("p k t -> p (k t)"), s_bank[g % 2][:, :],
                                          const["causal"][:, :, :].rearrange("p k t -> p (k t)"), ALU.mult).then_inc(sc_st, 1)
                    ids = const["ident"][:, :].unsqueeze(1).to_broadcast([P, 4, CH])
                    for l in range(LEVELS):
                        lv = const["level"][:, l, :].unsqueeze(1).to_broadcast([P, 4, CH])
                        for q in range(2):
                            gs = slice(4 * q, 4 * q + 4)
                            bank = [l_bank[q][j][:, :].rearrange("p (g t) -> p g t", g=4) for j in range(2)]
                            dve.wait_ge(u_ready[q], LEVELS * f + l + 1)
                            if l:
                                dve.wait_ge(ux_ready[q], LEVELS * f + l)
                            dve.tensor_tensor(u[:, gs, :], bank[0], lv, ALU.mult).then_inc(u_st[q], 1)
                        for q in range(2):
                            gs = slice(4 * q, 4 * q + 4)
                            bank = [l_bank[q][j][:, :].rearrange("p (g t) -> p g t", g=4) for j in range(2)]
                            if l == 0:
                                dve.wait_ge(u_st[q], LEVELS * f + 1)
                                dve.tensor_tensor(x[:, gs, :], ids, u[:, gs, :], ALU.subtract).then_inc(x_st[q], 1)
                            elif l < LEVELS - 1:
                                dve.wait_ge(xu_ready[q], 5 * f + l)
                                dve.tensor_tensor(x[:, gs, :], x[:, gs, :], bank[0], ALU.subtract).then_inc(x_st[q], 1)
                            dve.wait_ge(ux_ready[q], LEVELS * f + l + 1)
                            dve.tensor_tensor(xt[:, gs, :], xt[:, gs, :] if l else ids, bank[1], ALU.subtract).then_inc(xt_st[q], 1)
                    for q in range(2):
                        dve.wait_ge(qo_ready, 2 * f + q + 1)
                        qo = f_bank[1][:, :].rearrange("p (c k t) -> p c k t", c=2, k=2)
                        i = NC * f + 2 * q
                        dve.tensor_tensor(R["q"][:, f, 2 * q * CH:2 * (q + 1) * CH].rearrange("p (c t) -> p c t", c=2), qo[:, :, 0, :],
                                          R["kr"][:, i:i + 2, 1, :], ALU.add).then_inc(q_st, 1)


def rwkv_output(nc, const, R, mixT):
    with Scope(nc) as s:
        st = s.sb("chunk_state", [P, NC, FT, HD])
        z = s.sb("state_sum", [P, FT, HD])
        mm = s.sb("mid_products", [P, FT, NC])
        xc = s.sb("centred", [P, 2, S])
        sq = s.sb("centred_sq", [P, 2, S])
        rs = s.sb("group_rstd", [P, 2, S])
        z_bank = s.ps("state_ps")
        o_bank = [s.ps(f"out_ps{i}") for i in range(2)]
        m_bank = [s.ps(f"mean_ps{i}") for i in range(2)]
        v_bank = [s.ps(f"var_ps{i}") for i in range(2)]
        step_ready = s.sem("state_product_ready")
        zs = s.sem("state_step")
        o_ready, o_st = s.sem("out_ready"), s.sem("out_stored")
        mean, cent, sqd, var, lg, rstd, fin = (s.sem("group_" + n) for n in ("mean", "centred", "squared", "var", "log", "rstd", "done"))
        mid = R["mid"][:, :].rearrange("p (f c) -> p f c", c=NC)
        mn = R["mn"][:, :, :, :].rearrange("p (f c) k n -> p f c k n", c=NC)
        with nc.Block() as block:

            @block.tensor
            def _(pe):
                for c in range(1, NC - 1):
                    pe.wait_ge(zs, 1 + 3 * (c - 1) + 1)
                    for f in range(FT):
                        for b in (0, HD):
                            m = pe.matmul(z_bank[b:b + HD, f * HD:(f + 1) * HD], R["mn"][b:b + HD, f * NC + c, 0, :],
                                          st[b:b + HD, c, f, :], start=True, stop=True)
                    m.then_inc(step_ready, 1)
                pe.wait_ge(zs, 1 + 3 * (NC - 2) + 1)
                for j in range(FT + 2):
                    if j < FT:
                        if j >= 2:
                            pe.wait_ge(o_st, j - 1)
                        for c in range(1, NC):
                            for b in (0, HD):
                                m = pe.matmul(o_bank[j % 2][b:b + HD, c * CH:(c + 1) * CH], st[b:b + HD, c, j, :],
                                              R["q"][b:b + HD, j, c * CH:(c + 1) * CH], start=True, stop=True)
                        m.then_inc(o_ready, 1)
                    if 0 <= j - 1 < FT:
                        i = j - 1
                        pe.wait_ge(o_st, i + 1)
                        if i >= 2:
                            pe.wait_ge(cent, i - 1)
                        pe.matmul(m_bank[i % 2][:, :], const["heads"][:, :], R["o"][:, i, :], start=True, stop=True).then_inc(mean, 1)
                    if 0 <= j - 2 < FT:
                        i = j - 2
                        pe.wait_ge(sqd, i + 1)
                        if i >= 2:
                            pe.wait_ge(lg, i - 1)
                        pe.matmul(v_bank[i % 2][:, :], const["heads"][:, :], sq[:, i % 2, :], start=True, stop=True).then_inc(var, 1)

            @block.vector
            def _(dve):
                def bc(f3):
                    return f3.unsqueeze(2).to_broadcast([P, FT, HD])

                dve.tensor_tensor(mm[:, :, 0:NC - 1], mid[:, :, 0:NC - 1], mid[:, :, 1:NC], ALU.mult).then_inc(zs, 1)
                dve.wait_ge(zs, 1)
                dve.tensor_tensor(st[:, 1, :, :], mn[:, :, 0, 1, :], bc(mm[:, :, 0]), ALU.mult).then_inc(zs, 1)
                n = 2
                for c in range(1, NC - 1):
                    dve.wait_ge(zs, n)
                    dve.wait_ge(step_ready, c)
                    dve.tensor_tensor(z[:, :, :], z_bank[:, 0:FT * HD].rearrange("p (f n) -> p f n", f=FT), st[:, c, :, :], ALU.add).then_inc(zs, 1)
                    dve.wait_ge(zs, n + 1)
                    dve.tensor_tensor(z[:, :, :], z[:, :, :], mn[:, :, c, 1, :], ALU.add).then_inc(zs, 1)
                    dve.wait_ge(zs, n + 2)
                    dve.tensor_tensor(st[:, c + 1, :, :], z[:, :, :], bc(mm[:, :, c]), ALU.mult).then_inc(zs, 1)
                    n += 3
                w, bcol = PARAM_AT["rw_ln_w"], PARAM_AT["rw_ln_b"]
                for j in range(FT + 2):
                    if j < FT:
                        dve.wait_ge(o_ready, j + 1)
                        o = R["o"][:, j, CH:S]
                        dve.tensor_tensor(o, o_bank[j % 2][:, CH:S], o, ALU.add).then_inc(o_st, 1)
                    if 0 <= j - 1 < FT:
                        i = j - 1
                        dve.wait_ge(mean, i + 1)
                        if i >= 2:
                            dve.wait_ge(fin, 3 * (i - 1))
                            dve.wait_ge(sqd, i - 1)
                        dve.scalar_tensor_tensor(out=xc[:, i % 2, :], in0=m_bank[i % 2][:, :], scalar=-1.0 / HD,
                                                 in1=R["o"][:, i, :], op0=ALU.mult, op1=ALU.add).then_inc(cent, 1)
                    if 0 <= j - 2 < FT:
                        i = j - 2
                        dve.wait_ge(rstd, i + 1)
                        dve.wait_ge(cent, i + 1)
                        y = xc[:, i % 2, :]
                        dve.scalar_tensor_tensor(out=y, in0=y, scalar=par_col(const, w + i), in1=rs[:, i % 2, :],
                                                 op0=ALU.mult, op1=ALU.mult).then_inc(fin, 1)
                        dve.wait_ge(fin, 3 * i + 1)
                        dve.scalar_tensor_tensor(out=y, in0=y, scalar=par_col(const, bcol + i), in1=R["bonus"][:, i, :],
                                                 op0=ALU.add, op1=ALU.add).then_inc(fin, 1)
                        dve.wait_ge(fin, 3 * i + 2)
                        dve.tensor_tensor(mixT[:, FT + i, :], y, R["gate"][:, i, :], ALU.mult).then_inc(fin, 1)

            @block.scalar
            def _(act):
                act.preload_act_table_set("natural_log_exp_and_others")
                for i in range(FT):
                    act.wait_ge(cent, i + 1)
                    if i >= 2:
                        act.wait_ge(var, i - 1)
                    act.activation(sq[:, i % 2, :], xc[:, i % 2, :], ACT.Square).then_inc(sqd, 1)
                    act.wait_ge(var, i + 1)
                    if i >= 2:
                        act.wait_ge(fin, 3 * (i - 2) + 1)
                    act.activation(rs[:, i % 2, :], v_bank[i % 2][:, :], ACT.Ln, scale=1.0 / HD, bias=const["gn_eps"][:, :]).then_inc(lg, 1)
                    act.wait_ge(lg, i + 1)
                    act.activation(rs[:, i % 2, :], rs[:, i % 2, :], ACT.Exp, scale=-0.5).then_inc(rstd, 1)


def out_projection(nc, const, w, xT, n_in, h, tag, out=None):
    HALF = D // 2
    with Scope(nc) as s:
        wt = s.sb(tag + "_w", [P, 2, n_in, HALF])
        banks = [s.ps(f"{tag}_ps{i}") for i in range(4)]
        loaded = s.sems(tag + "_loaded", 2)
        ready = s.sem(tag + "_ready")
        added = s.sem(tag + "_added")
        stored = s.sem(tag + "_stored")
        wv = w.rearrange("l (k p) n -> p (l k) n", p=P)
        with nc.Block() as block:

            @block.sync
            def _(sp):
                for half in range(2):
                    sp.dma_start(wt[:, half, :, :], wv[:, :, half * HALF:(half + 1) * HALF]).then_inc(loaded[half], 16)
                if out is not None:
                    for half in range(2):
                        for c in range(TT):
                            sp.wait_ge(added, TT * half + c + 1)
                            cols = slice(half * HALF, (half + 1) * HALF)
                            sp.dma_start(out[c * P:(c + 1) * P, cols], h[:, c, cols]).then_inc(stored, 16)
                    sp.wait_ge(stored, 16 * 2 * TT)

            @block.tensor
            def _(pe):
                for half in range(2):
                    pe.wait_ge(loaded[half], 16)
                    for c in range(TT):
                        i = TT * half + c
                        if i >= 4:
                            pe.wait_ge(added, i - 3)
                        for k in range(n_in):
                            m = pe.matmul(banks[i % 4][:, :], xT[:, k, c * P:(c + 1) * P], wt[:, half, k, :],
                                          start=(k == 0), stop=(k == n_in - 1))
                        m.then_inc(ready, 1)

            @block.vector
            def _(dve):
                for half in range(2):
                    for c in range(TT):
                        i = TT * half + c
                        dve.wait_ge(ready, i + 1)
                        dst = h[:, c, half * HALF:(half + 1) * HALF]
                        dve.tensor_tensor(dst, banks[i % 4][:, :], dst, ALU.add).then_inc(added, 1)


def route(nc, A, const, h, xn_dram, list_dram, M):
    NL = NG + NE
    MADE = 10
    with Scope(nc) as s:
        sq = s.sb("ffn_sq", [P, D])
        ss = s.sb("ffn_ss", [P, TT])
        rs = s.sb("ffn_rstd", [P, TT])
        xg = s.sb("ffn_in", [P, TT, D])
        xT = s.sb("ffn_in_t", [P, KC, S])
        wr = s.sb("router_w", [P, KC, NL])
        br = s.sb("router_b", [P, NL])
        lg = s.sb("router_logits", [P, TT, NL])
        desc = s.sb("descending", [P, EPG])
        base = s.sb("list_base", [P, NE])
        steps = s.sb("round_limits", [P, EPG])
        ids = s.sb("token_ids", [P, 2, TT, 2], I32)
        empty = s.sb("empty_list", [P, NE * S // P, 2], I32)
        t4 = s.sb("t4", [P, TT, NG])
        grp = s.sb("group_hot", [P, TT, NG])
        ex4 = s.sb("group_exp", [P, TT, NG])
        gm = s.sb("group_max", [P, TT])
        a1 = s.sb("a1", [P, TT])
        gval = s.sb("group_prob", [P, TT])
        pick = s.sb("picked", [P, TT, NG, EPG])
        sel = s.sb("selected", [P, TT, EPG])
        t8 = s.sb("t8", [P, TT, EPG])
        hot = [s.sb(f"expert_hot{i}", [P, TT, EPG]) for i in range(2)]
        top = [s.sb(f"expert_top{i}", [P, TT]) for i in range(2)]
        p2 = s.sb("second_exp", [P, TT])
        full = [s.sb(f"expert_full{i}", [P, TT, NG, EPG]) for i in range(2)]
        both = s.sb("expert_both", [P, TT, NE])
        nboth = s.sb("expert_both_neg", [P, TT, NE])
        place = s.sb("places", [P, TT, NE])
        t32 = s.sb("t32", [P, TT, NE])
        slotf = s.sb("slots_float", [P, 2, TT])
        tot = s.sb("totals", [P, NE])
        most = s.sb("most", [P, 1])
        rf = s.sb("rounds_float", [P, 1])
        t_bank = [s.ps(f"ffn_ps{i}") for i in range(4)]
        l_bank = s.ps("logit_ps")
        r_bank = s.ps("rank_ps")
        squared, rstd, scaled = s.sem("ffn_squares"), s.sem("ffn_rstd_ready"), s.sem("ffn_scaled")
        turned, even_st, odd_st = s.sem("ffn_turned"), s.sem("ffn_even_stored"), s.sem("ffn_odd_stored")
        loaded, xn_st, zeroed, made = s.sem("router_loaded"), s.sem("ffn_in_stored"), s.sem("list_zeroed"), s.sem("router_constants")
        logits, ranks, dv, ac = s.sem("logits_ready"), s.sem("ranks_ready"), s.sem("route_step"), s.sem("route_exp")
        put = s.sem("ids_scattered")
        slots_ready = s.sem("slots_ready")
        with nc.Block() as block:

            @block.vector
            def _(dve):
                n = [0]

                def step(ins, name=None):
                    n[0] += 1
                    if name:
                        M[name] = n[0]
                    ins.then_inc(dv, 1)
                    dve.wait_ge(dv, n[0])

                def wide(x, k):
                    return x.unsqueeze(2).to_broadcast([P, TT, k])

                def row(x, k):
                    return x[:, 0:k].unsqueeze(1).to_broadcast([P, TT, k])

                def first_of_max(vals, best, tmp, hot_out, k):
                    step(dve.tensor_reduce(best, vals, AX_X, ALU.max))
                    step(dve.tensor_tensor(tmp, vals, wide(best, k), ALU.is_ge))
                    step(dve.tensor_tensor(tmp, tmp, row(desc, k), ALU.mult))
                    step(dve.tensor_reduce(a1[:, :], tmp, AX_X, ALU.max))
                    step(dve.tensor_tensor(hot_out, tmp, wide(a1[:, :], k), ALU.is_equal))

                dve.wait_ge(squared, TT)
                dve.tensor_scalar(ss[:, :], ss[:, :], 1.0 / D, EPS, ALU.mult, ALU.add).then_inc(rstd, 1)
                dve.wait_ge(rstd, 2)
                dve.reciprocal(rs[:, :], ss[:, :]).then_inc(rstd, 1)
                dve.wait_ge(rstd, 3)
                dve.wait_ge(const["row_params"], 32)
                for c in range(TT):
                    dve.scalar_tensor_tensor(out=xg[:, c, :], in0=h[:, c, :], scalar=rs[:, c:c + 1], in1=const["ffn_g"][:, :],
                                             op0=ALU.mult, op1=ALU.mult).then_inc(scaled, 1)
                for k in range(1, KC, 2):
                    dve.wait_ge(turned, k + 1)
                    dve.tensor_copy(xT[:, k, :], t_bank[k % 4][:, :]).then_inc(odd_st, 1)
                dve.wait_ge(logits, 1)
                dve.wait_ge(made, MADE)
                step(dve.tensor_tensor(lg[:, :, :], l_bank[:, 0:TT * NL].rearrange("p (c n) -> p c n", c=TT),
                                       br[:, :].unsqueeze(1).to_broadcast([P, TT, NL]), ALU.add))
                first_of_max(lg[:, :, 0:NG], gm[:, :], t4[:, :, :], grp[:, :, :], NG)
                step(dve.tensor_tensor(t4[:, :, :], lg[:, :, 0:NG], wide(gm[:, :], NG), ALU.subtract), "group_less")
                dve.wait_ge(ac, 1)
                step(dve.tensor_reduce(gval[:, :], ex4[:, :, :], AX_X, ALU.add))
                step(dve.reciprocal(gval[:, :], gval[:, :]))
                step(dve.tensor_tensor(pick[:, :, :, :], lg[:, :, NG:NL].rearrange("p c (g e) -> p c g e", g=NG),
                                       grp[:, :, :].unsqueeze(3).to_broadcast([P, TT, NG, EPG]), ALU.mult))
                step(dve.tensor_reduce(sel[:, :, :], pick[:, :, :, :].rearrange("p c g e -> p c e g"), AX_X, ALU.add))
                first_of_max(sel[:, :, :], top[0][:, :], t8[:, :, :], hot[0][:, :, :], EPG)
                step(dve.tensor_scalar(t8[:, :, :], hot[0][:, :, :], NEG, None, ALU.mult))
                step(dve.tensor_tensor(sel[:, :, :], sel[:, :, :], t8[:, :, :], ALU.add))
                first_of_max(sel[:, :, :], top[1][:, :], t8[:, :, :], hot[1][:, :, :], EPG)
                step(dve.tensor_tensor(p2[:, :], top[1][:, :], top[0][:, :], ALU.subtract), "top_less")
                for j in range(2):
                    step(dve.tensor_tensor(full[j][:, :, :, :], grp[:, :, :].unsqueeze(3).to_broadcast([P, TT, NG, EPG]),
                                           hot[j][:, :, :].unsqueeze(2).to_broadcast([P, TT, NG, EPG]), ALU.mult))
                flat = [full[j][:, :, :, :].rearrange("p c g e -> p c (g e)") for j in range(2)]
                step(dve.tensor_tensor(both[:, :, :], flat[0], flat[1], ALU.add))
                step(dve.tensor_scalar(nboth[:, :, :], both[:, :, :], -1.0, None, ALU.mult), "both")
                dve.wait_ge(ac, 2)
                step(dve.tensor_scalar(a1[:, :], p2[:, :], 1.0, None, ALU.add))
                step(dve.reciprocal(a1[:, :], a1[:, :]))
                step(dve.tensor_tensor(M["weights"][:, 0, :], gval[:, :], a1[:, :], ALU.mult))
                step(dve.tensor_tensor(M["weights"][:, 1, :], M["weights"][:, 0, :], p2[:, :], ALU.mult))
                dve.wait_ge(ranks, 1)
                step(dve.tensor_tensor(place[:, :, :], r_bank[:, 0:TT * NE].rearrange("p (c e) -> p c e", c=TT),
                                       base[:, :].unsqueeze(1).to_broadcast([P, TT, NE]), ALU.add))
                for j in range(2):
                    step(dve.tensor_tensor(t32[:, :, :], place[:, :, :], flat[j], ALU.mult))
                    step(dve.tensor_reduce(slotf[:, j, :], t32[:, :, :], AX_X, ALU.add))
                step(dve.tensor_copy(tot[:, :], r_bank[:, TT * NE:(TT + 1) * NE]))
                step(dve.tensor_reduce(most[:, :], tot[:, :], AX_X, ALU.max))
                step(dve.tensor_scalar(steps[:, :], steps[:, :], most[:, 0:1], None, ALU.is_lt))
                step(dve.tensor_reduce(rf[:, :], steps[:, :], AX_X, ALU.add))
                step(dve.tensor_copy(M["rounds"][:, 0:1], rf[:, :]))
                dve.tensor_copy(M["slots"][:, :, :], slotf[:, :, :]).then_inc(slots_ready, 1)

            @block.sync
            def _(sp):
                sp.dma_start(wr[:, :, 0:NG], A["router_grp_w"].rearrange("l (k p) n -> p (l k) n", p=P)).then_inc(loaded, 16)
                sp.dma_start(wr[:, :, NG:NL], A["router_exp_w"].rearrange("l (k p) n -> p (l k) n", p=P)).then_inc(loaded, 16)
                sp.dma_start(br[:, 0:NG], A["router_grp_b"].broadcast_to([P, NG])).then_inc(loaded, 16)
                sp.dma_start(br[:, NG:NL], A["router_exp_b"].broadcast_to([P, NE])).then_inc(loaded, 16)
                sp.wait_ge(made, MADE)
                sp.dma_start(list_dram.rearrange("(p n) a -> p (n a)", p=P),
                             empty[:, :, :].rearrange("p n a -> p (n a)")).then_inc(zeroed, 16)
                for c in range(TT):
                    sp.wait_ge(scaled, c + 1)
                    sp.dma_start(xn_dram[c * P:(c + 1) * P, :], xg[:, c, :]).then_inc(xn_st, 16)
                sp.wait_ge(xn_st, 16 * TT)

            @block.gpsimd
            def _(pool):
                pool.iota(desc[:, :], [[-1, EPG]], base=EPG, channel_multiplier=0, allow_small_or_imprecise_dtypes=True).then_inc(made, 1)
                pool.iota(base[:, :], [[S, NE]], base=0, channel_multiplier=0, allow_small_or_imprecise_dtypes=True).then_inc(made, 1)
                pool.iota(steps[:, :], [[CAP, EPG]], base=0, channel_multiplier=0, allow_small_or_imprecise_dtypes=True).then_inc(made, 1)
                for j in range(2):
                    pool.iota(ids[:, j, :, 0], [[P, TT]], base=0, channel_multiplier=1).then_inc(made, 1)
                    pool.iota(ids[:, j, :, 1], [[2 * P, TT]], base=j, channel_multiplier=2).then_inc(made, 1)
                pool.memset(empty[:, :, 0], 0).then_inc(made, 1)
                pool.iota(empty[:, :, 1], [[1, NE * S // P]], base=2 * S, channel_multiplier=NE * S // P).then_inc(made, 1)
                pool.memset(M["rounds"][:, :], 0).then_inc(made, 1)
                pool.wait_ge(zeroed, 16)
                pool.wait_ge(made, MADE)
                pool.wait_ge(slots_ready, 1)
                for j in range(2):
                    for c in range(TT):
                        pool.indirect_dma_start(out=list_dram, out_offset=bass.IndirectOffsetOnAxis(ap=M["slots"][:, j, c:c + 1], axis=0),
                                                in_=ids[:, j, c, :], in_offset=None).then_inc(put, 16)
                pool.wait_ge(put, 16 * 2 * TT)

            @block.scalar
            def _(act):
                for c in range(TT):
                    if c:
                        act.wait_ge(squared, c)
                    act.activation(sq[:, :], h[:, c, :], ACT.Square, accum_out=ss[:, c:c + 1]).then_inc(squared, 1)
                act.wait_ge(rstd, 1)
                act.activation(ss[:, :], ss[:, :], ACT.Sqrt).then_inc(rstd, 1)
                act.preload_act_table(ACT.Exp)
                for k in range(0, KC, 2):
                    act.wait_ge(turned, k + 1)
                    act.activation(xT[:, k, :], t_bank[k % 4][:, :], ACT.Copy).then_inc(even_st, 1)
                act.wait_ge(dv, M["group_less"])
                act.activation(ex4[:, :, :], t4[:, :, :], ACT.Exp).then_inc(ac, 1)
                act.wait_ge(dv, M["top_less"])
                act.activation(p2[:, :], p2[:, :], ACT.Exp).then_inc(ac, 1)

            @block.tensor
            def _(pe):
                for k in range(KC):
                    if k >= 4:
                        pe.wait_ge((even_st, odd_st)[k % 2], (k - 4) // 2 + 1)
                    for c in range(TT):
                        pe.wait_ge(scaled, c + 1)
                        t = pe.transpose(t_bank[k % 4][:, c * P:(c + 1) * P], xg[:, c, k * P:(k + 1) * P], const["ident"][:, :])
                    t.then_inc(turned, 1)
                pe.wait_ge(loaded, 64)
                pe.wait_ge(even_st, KC // 2)
                pe.wait_ge(odd_st, KC // 2)
                for c in range(TT):
                    for k in range(KC):
                        m = pe.matmul(l_bank[:, c * NL:(c + 1) * NL], xT[:, k, c * P:(c + 1) * P], wr[:, k, :],
                                      start=(k == 0), stop=(k == KC - 1))
                m.then_inc(logits, 1)
                pe.wait_ge(dv, M["both"])
                for c in range(TT + 1):
                    for b in range(min(c, TT - 1) + 1 if c < TT else TT):
                        same = b == c
                        m = pe.matmul(r_bank[:, c * NE:(c + 1) * NE], (const["causal"][:, 0, :] if same else const["minus_ones"][:, :]),
                                      (both if same else nboth)[:, b, :], start=(b == 0), stop=(b == min(c, TT - 1)))
                m.then_inc(ranks, 1)



def experts(nc, A, const, xn_dram, list_dram, y_dram, M):
    NB = 4
    FC = DE // P
    with Scope(nc) as s:
        wg = [s.sb(f"w_gate{j}", [P, KC, DE]) for j in range(NB)]
        wu = [s.sb(f"w_up{j}", [P, KC, DE]) for j in range(NB)]
        wd = [s.sb(f"w_down{j}", [P, FC, D]) for j in range(NB)]
        idx = [s.sb(f"token_index{j}", [CAP, 2], I32) for j in range(NB)]
        dst = [s.sb(f"result_row{j}", [CAP, 2], I32) for j in range(NB)]
        xg = [s.sb(f"gathered{j}", [CAP, D]) for j in range(NB)]
        xT = [s.sb(f"gathered_t{j}", [P, KC, CAP]) for j in range(2)]
        act_g = [s.sb(f"silu{j}", [P, FC * CAP]) for j in range(2)]
        hid = [s.sb(f"hidden{j}", [P, FC, CAP]) for j in range(2)]
        y = [s.sb(f"expert_out{j}", [CAP, D]) for j in range(NB)]
        t_bank = [s.ps(f"gathered_ps{j}") for j in range(2)]
        g_bank = [s.ps(f"hidden_ps{j}") for j in range(2)]
        y_bank = [s.ps(f"expert_ps{j}") for j in range(4)]
        idx_in = s.sems("index_loaded", NB)
        w_in = s.sems("expert_loaded", NB)
        x_in = s.sems("tokens_gathered", NB)
        turned = s.sems("gathered_turned", NB)
        t_st = s.sems("gathered_stored", NB)
        gu = s.sems("gate_up_ready", NB)
        silu = s.sems("silu_ready", NB)
        hid_r = s.sems("hidden_ready", NB)
        y_r = s.sems("expert_ready", NB)
        y_lo, y_hi = s.sems("expert_low_stored", NB), s.sems("expert_high_stored", NB)
        y_out = s.sems("expert_written", NB)
        dst_in = s.sems("result_rows_loaded", NB)
        spare, seen, seen_pe = s.sem("spare_rows_ready"), s.sem("waits_seen"), s.sem("gathers_seen")
        TURNS = NE // NB
        gate = A["exp_w_gate"].rearrange("l e (k p) n -> p (l e) k n", p=P)
        up = A["exp_w_up"].rearrange("l e (k p) n -> p (l e) k n", p=P)
        down = A["exp_w_down"].rearrange("l e (k p) n -> p (l e) k n", p=P)
        lists = list_dram.rearrange("(e r c) a -> c (e r) a", r=S // CAP, c=CAP)

        def turns(eng):
            rounds = eng.value_load(M["rounds"][0:1, 0:1], min_val=1, max_val=S // CAP)
            with eng.Fori(0, rounds) as rnd, eng.Fori(0, TURNS) as t:
                yield rnd, t, rnd * TURNS + t

        with nc.Block() as block:

            @block.sync
            def _(sp):
                for rnd, t, n in turns(sp):
                    for j in range(NB):
                        e = t * NB + j
                        sp.wait_ge(y_r[j], n + 1)
                        sp.dma_start(idx[j][:, :], lists[:, bass.ds(e * (S // CAP) + rnd, 1), :].rearrange("c a b -> c (a b)")).then_inc(idx_in[j], 16)
                        sp.dma_start(wg[j][:, :, :], gate[:, bass.ds(e, 1), :, :].rearrange("p a k n -> p (a k) n")).then_inc(w_in[j], 16)
                        sp.dma_start(wu[j][:, :, :], up[:, bass.ds(e, 1), :, :].rearrange("p a k n -> p (a k) n")).then_inc(w_in[j], 16)
                        sp.dma_start(wd[j][:, :, :], down[:, bass.ds(e, 1), :, :].rearrange("p a k n -> p (a k) n")).then_inc(w_in[j], 16)

            @block.gpsimd
            def _(pool):
                for j in range(NB):
                    pool.dma_start(dst[j][:, :], lists[:, 0:1, :].rearrange("c a b -> c (a b)")).then_inc(dst_in[j], 16)
                    pool.wait_ge(dst_in[j], 16)
                    pool.iota(dst[j][:, :], [[0, 2]], base=2 * S + NE * S + j * CAP, channel_multiplier=1).then_inc(spare, 1)
                    pool.memset(y[j][:, :], 0.0).then_inc(spare, 1)

                def write_rows(j, n):
                    pool.wait_ge(dst_in[j], n * 16 + 16)
                    pool.wait_ge(y_lo[j], n + 1)
                    pool.wait_ge(y_hi[j], n + 1)
                    pool.sem_inc(seen)
                    pool.indirect_dma_start(out=y_dram, out_offset=bass.IndirectOffsetOnAxis(ap=dst[j][:, 1:2], axis=0),
                                            in_=y[j][:, :], in_offset=None).then_inc(y_out[j], 16)

                pool.wait_ge(spare, 2 * NB)
                for rnd, t, n in turns(pool):
                    for j in range(NB):
                        pool.wait_ge(idx_in[j], n * 16 + 16)
                        pool.sem_inc(seen)
                        pool.indirect_dma_start(out=xg[j][:, :], out_offset=None, in_=xn_dram,
                                                in_offset=bass.IndirectOffsetOnAxis(ap=idx[j][:, 0:1], axis=0)).then_inc(x_in[j], 16)
                        write_rows(j, n)
                        pool.wait_ge(y_out[j], n * 16 + 16)
                        pool.dma_start(dst[j][:, :], lists[:, bass.ds((t * NB + j) * (S // CAP) + rnd, 1), :].rearrange("c a b -> c (a b)")).then_inc(dst_in[j], 16)
                total = pool.value_load(M["rounds"][0:1, 0:1], min_val=1, max_val=S // CAP) * TURNS
                for j in range(NB):
                    write_rows(j, total)
                for j in range(NB):
                    pool.wait_ge(y_out[j], total * 16 + 16)
                pool.sem_inc(seen)

            @block.tensor
            def _(pe):
                for j in range(NB):
                    pe.sem_inc(y_r[j])
                for rnd, t, n in turns(pe):
                    for j in range(NB):
                        b = j % 2
                        pe.wait_ge(x_in[j], n * 16 + 16)
                        pe.sem_inc(seen_pe)
                        for k in range(KC):
                            m = pe.transpose(t_bank[b][:, k * CAP:(k + 1) * CAP], xg[j][:, k * P:(k + 1) * P], const["ident"][0:CAP, 0:CAP])
                        m.then_inc(turned[j], 1)
                        pe.wait_ge(w_in[j], n * 48 + 48)
                        pe.wait_ge(t_st[j], n + 1)
                        for i, w in enumerate((wg[j], wu[j])):
                            for f in range(FC):
                                c0 = (i * FC + f) * CAP
                                for k in range(KC):
                                    m = pe.matmul(g_bank[b][:, c0:c0 + CAP], w[:, k, f * P:(f + 1) * P], xT[b][:, k, :],
                                                  start=(k == 0), stop=(k == KC - 1))
                        m.then_inc(gu[j], 1)
                        pe.wait_ge(hid_r[j], n + 1)
                        if j >= 2:
                            pe.wait_ge(y_lo[j - 2], n + 2)
                            pe.wait_ge(y_hi[j - 2], n + 2)
                        else:
                            pe.wait_ge(y_lo[j + 2], n + 1)
                            pe.wait_ge(y_hi[j + 2], n + 1)
                        for half in range(2):
                            for f in range(FC):
                                m = pe.matmul(y_bank[2 * b + half][0:CAP, :], hid[b][:, f, :], wd[j][:, f, half * 512:(half + 1) * 512],
                                              start=(f == 0), stop=(f == FC - 1))
                        m.then_inc(y_r[j], 1)

            @block.scalar
            def _(act):
                for j in range(NB):
                    act.sem_inc(y_hi[j])
                for rnd, t, n in turns(act):
                    for j in range(NB):
                        b = j % 2
                        act.wait_ge(turned[j], n + 1)
                        act.activation(xT[b][:, :, :].rearrange("p k c -> p (k c)"), t_bank[b][:, :], ACT.Copy).then_inc(t_st[j], 1)
                        act.wait_ge(gu[j], n + 1)
                        act.activation(act_g[b][:, :], g_bank[b][:, 0:FC * CAP], ACT.Silu).then_inc(silu[j], 1)
                        act.wait_ge(y_r[j], n + 2)
                        act.wait_ge(y_out[j], n * 16 + 16)
                        act.activation(y[j][:, 512:D], y_bank[2 * b + 1][0:CAP, :], ACT.Copy).then_inc(y_hi[j], 1)

            @block.vector
            def _(dve):
                for j in range(NB):
                    dve.sem_inc(y_lo[j])
                for rnd, t, n in turns(dve):
                    for j in range(NB):
                        b = j % 2
                        dve.wait_ge(silu[j], n + 1)
                        dve.tensor_tensor(hid[b][:, :, :].rearrange("p f c -> p (f c)"), g_bank[b][:, FC * CAP:2 * FC * CAP], act_g[b][:, :],
                                          ALU.mult).then_inc(hid_r[j], 1)
                        dve.wait_ge(y_r[j], n + 2)
                        dve.wait_ge(y_out[j], n * 16 + 16)
                        dve.tensor_copy(y[j][:, 0:512], y_bank[2 * b][0:CAP, :]).then_inc(y_lo[j], 1)


def combine(nc, const, h, y_dram, M):
    with Scope(nc) as s:
        yg = s.sb("expert_rows", [P, TT, 2, D])
        rows = y_dram[0:2 * S, :].rearrange("(c p k) d -> p c k d", p=P, k=2)
        sq = s.sb("fin_sq", [P, D])
        ss = s.sb("fin_ss", [P, TT])
        rs = s.sb("fin_rstd", [P, TT])
        got = s.sems("rows_gathered", 4)
        added = s.sem("rows_added")
        squared, rstd, scaled = s.sem("fin_squares"), s.sem("fin_rstd_ready"), s.sem("fin_scaled")
        with nc.Block() as block:

            @block.sync
            def _(sp):
                for c in range(TT):
                    sp.dma_start(yg[:, c, :, :], rows[:, c, :, :]).then_inc(got[c], 16)

            @block.vector
            def _(dve):
                for i in range(2 * TT):
                    c, j = i // 2, i % 2
                    dve.wait_ge(got[c], 16)
                    if j:
                        dve.wait_ge(added, i)
                    dve.scalar_tensor_tensor(out=h[:, c, :], in0=yg[:, c, j, :], scalar=M["weights"][:, j, c:c + 1], in1=h[:, c, :],
                                             op0=ALU.mult, op1=ALU.add).then_inc(added, 1)
                dve.wait_ge(squared, TT)
                dve.tensor_scalar(ss[:, :], ss[:, :], 1.0 / D, EPS, ALU.mult, ALU.add).then_inc(rstd, 1)
                dve.wait_ge(rstd, 2)
                dve.reciprocal(rs[:, :], ss[:, :]).then_inc(rstd, 1)
                dve.wait_ge(rstd, 3)
                for c in range(TT):
                    dve.scalar_tensor_tensor(out=h[:, c, :], in0=h[:, c, :], scalar=rs[:, c:c + 1], in1=const["fin_g"][:, :],
                                             op0=ALU.mult, op1=ALU.mult).then_inc(scaled, 1)

            @block.scalar
            def _(act):
                for c in range(TT):
                    act.wait_ge(added, 2 * c + 2)
                    if c:
                        act.wait_ge(squared, c)
                    act.activation(sq[:, :], h[:, c, :], ACT.Square, accum_out=ss[:, c:c + 1]).then_inc(squared, 1)
                act.wait_ge(rstd, 1)
                act.activation(ss[:, :], ss[:, :], ACT.Sqrt).then_inc(rstd, 1)


A_REL = 2 * 2 * P - 1
CLS = 4
BUCKETS = 32
SKEW = 16
COL = {"qa": 0, "ka": 512, "va": 640, "qb": 768, "kb": 2304, "vb": 3840, "ga": 5376, "gb": 5888, "mg": 6400}


def by_class(x):
    return x.rearrange("p (t c) -> p c t", c=CLS)


def bias_tables(nc, A, const, T):
    with Scope(nc) as s:
        hot = s.sb("bucket_hot", [BUCKETS, 3, 512])
        rel = s.sb("rel_bias", [BUCKETS, 32])
        win = s.sb("window", [NH, 4, 512])
        tab = s.sb("bias_rows", [NH, 4, 512])
        bank = [s.ps(f"bias_ps{i}") for i in range(4)]
        loaded, ready, added, stored, tiled = (s.sem("bias_" + n) for n in ("loaded", "ready", "added", "stored", "tiled"))
        dram = T["bias_dram"]
        with nc.Block() as block:

            @block.sync
            def _(sp):
                sp.dma_start(hot[:, :, :], A["const_bucket_hot"].rearrange("g b x -> b g x")).then_inc(loaded, 16)
                sp.dma_start(rel[:, :], A["rel_bias_2"]).then_inc(loaded, 16)
                sp.dma_start(win[:, :, :], A["const_window"].rearrange("g h x -> h g x")).then_inc(loaded, 16)
                sp.dma_start(T["sink"][:, :], A["sink_a_2"].broadcast_to([P, NH])).then_inc(loaded, 16)
                sp.wait_ge(added, 4)
                for g in range(4):
                    sp.dma_start(dram[g], tab[:, g:g + 1, :].broadcast_to([NH, SKEW, 512])).then_inc(stored, 16)
                sp.wait_ge(stored, 64)
                n = 0
                for g, tile, w in ((0, T["band"][0], 3 * P), (1, T["band"][1], 3 * P), (2, T["classes"][:, :, 0:P], P),
                                   (3, T["classes"][:, :, P:2 * P], P)):
                    for p in range(0, P, SKEW):
                        src = bass.AP(dram.tensor, dram.offset + g * NH * SKEW * 512 + P - 1 - p, [[511, SKEW], [SKEW * 512, NH], [1, w]])
                        sp.dma_start(tile[p:p + SKEW, :, :], src).then_inc(tiled, 16)
                        n += 1
                sp.wait_ge(tiled, 16 * n)

            @block.tensor
            def _(pe):
                pe.wait_ge(loaded, 64)
                for g in range(4):
                    pe.matmul(bank[g][0:NH, :], rel[:, g * NH:(g + 1) * NH], hot[:, max(g - 1, 0), :], start=True, stop=True).then_inc(ready, 1)

            @block.vector
            def _(dve):
                for g in range(4):
                    dve.wait_ge(ready, g + 1)
                    dve.tensor_tensor(tab[:, g, :], bank[g][0:NH, :], win[:, g, :], ALU.add).then_inc(added, 1)


def head_gain_columns(nc, const, T):
    with Scope(nc) as s:
        done = s.sem("head_gains_ready")
        with nc.Block() as block:

            @block.vector
            def _(dve):
                for i, name in enumerate(("q_norm_a_2", "k_norm_a_2", "q_norm_b_2", "k_norm_b_2")):
                    dve.tensor_scalar(T["head_gains"][:, i:i + 1], par_col(const, PARAM_AT[name]), HD ** -0.5 if i % 2 == 0 else 1.0,
                                      None, ALU.mult).then_inc(done, 1)
                dve.wait_ge(done, 4)


def project_second(nc, A, const, hT, T):
    UNIT, NSLOT, NBANK = 256, 3, 6
    w = A["w_in_2"].rearrange("l (k p) n -> p (l k) n", p=P)
    gains = T["head_gains"]
    jobs = []
    for u in range(21):
        col = u * UNIT
        if col < COL["ka"]:
            jobs += [(u, "qk", x, T["qa"][:, col // P + x, :], 0, False) for x in range(2)]
        elif col == COL["ka"]:
            jobs += [(u, "ka", x, T["ka"][:, x, :], 1, False) for x in range(2)]
            jobs += [(u, "va", 0, T["va"][:, :, :], None, False)]
        elif col < COL["vb"]:
            name = "qb" if col < COL["kb"] else "kb"
            for x in range(2):
                f = (col - COL[name]) // P + x
                jobs.append((u, "qk", x, T[name][:, f, :], 2 if name == "qb" else 3, f >= FT))
        else:
            g, half = divmod((col - COL["vb"]) // UNIT, 2)
            for pair in range(2):
                dst = T["v0"][:, :, half * UNIT:(half + 1) * UNIT] if g == 0 else \
                    T["v12"][:, :, (2 * (g - 1) + half) * UNIT:(2 * (g - 1) + half + 1) * UNIT]
                jobs.append((u, "vb", pair, dst[:, 2 * pair:2 * pair + 2, :], None, g > 0))
    last_job = {}
    for n, job in enumerate(jobs):
        last_job[job[0]] = n
    normed = [n for n, job in enumerate(jobs) if job[1] in ("qk", "ka")]
    plain = [n for n, job in enumerate(jobs) if job[1] not in ("qk", "ka")]
    with Scope(nc) as s:
        ring = s.sb("w_in_2_ring", [P, NSLOT, KC, UNIT])
        sq = s.sb("qk_sq", [P, 2, S])
        rs = s.sb("qk_rstd", [P, 2, S])
        bank = [s.ps(f"proj_ps{i}") for i in range(NBANK)]
        sums = [s.ps(f"qk_sum_ps{i}") for i in range(2)]
        loaded = s.sems("w_in_2_loaded", NSLOT)
        ready = s.sem("projected")
        v_st = s.sem("v2_stored")
        squared, summed, logged, rstd, gained, qk_st = (s.sem("head_norm_" + n) for n in ("squared", "summed", "logged", "rstd", "gained", "stored"))
        with nc.Block() as block:

            @block.sync
            def _(sp):
                for u in range(21):
                    if u >= NSLOT:
                        sp.wait_ge(ready, last_job[u - NSLOT] + 1)
                    sp.dma_start(ring[:, u % NSLOT, :, :], w[:, :, u * UNIT:(u + 1) * UNIT]).then_inc(loaded[u % NSLOT], 16)

            @block.tensor
            def _(pe):
                def head_sums(i):
                    pe.wait_ge(squared, i + 1)
                    if i >= 2:
                        pe.wait_ge(logged, i - 1)
                    pe.matmul(sums[i % 2][:, :], const["heads"][:, :], sq[:, i % 2, :], start=True, stop=True).then_inc(summed, 1)

                for n, (u, kind, x, dst, gain, perm) in enumerate(jobs):
                    pe.wait_ge(loaded[u % NSLOT], 16 * (u // NSLOT + 1))
                    if n >= NBANK:
                        o = n - NBANK
                        if o in normed:
                            pe.wait_ge(qk_st, normed.index(o) + 1)
                        else:
                            pe.wait_ge(v_st, plain.index(o) + 1)
                    wt = ring[:, u % NSLOT, :, :]
                    b = bank[n % NBANK]
                    if kind == "qk":
                        for k in range(KC):
                            m = pe.matmul(b[:, :], wt[:, k, x * P:(x + 1) * P], hT[:, k, :], start=(k == 0), stop=(k == KC - 1))
                    elif kind == "ka":
                        for half in range(2):
                            for k in range(KC):
                                m = pe.matmul(b[half * HD:(half + 1) * HD, :], wt[:, k, x * HD:(x + 1) * HD], hT[:, k, :],
                                              start=(k == 0), stop=(k == KC - 1))
                    else:
                        cols, nc_ = (slice(P, 2 * P), TT) if kind == "va" else (slice(0, UNIT), 2)
                        width = cols.stop - cols.start
                        for i in range(nc_):
                            c = i if kind == "va" else 2 * x + i
                            for k in range(KC):
                                t = by_class(hT[:, k, :])[:, c, :] if perm else hT[:, k, c * P:(c + 1) * P]
                                m = pe.matmul(b[:, i * width:(i + 1) * width], t, wt[:, k, cols], start=(k == 0), stop=(k == KC - 1))
                    m.then_inc(ready, 1)
                    if n >= 1 and n - 1 in normed:
                        head_sums(normed.index(n - 1))

            @block.scalar
            def _(act):
                act.preload_act_table_set("natural_log_exp_and_others")
                v = 0
                for n, (u, kind, x, dst, gain, perm) in enumerate(jobs):
                    if n in normed:
                        i = normed.index(n)
                        act.wait_ge(ready, n + 1)
                        if i >= 2:
                            act.wait_ge(summed, i - 1)
                        act.activation(sq[:, i % 2, :], bank[n % NBANK][:, :], ACT.Square).then_inc(squared, 1)
                        act.wait_ge(summed, i + 1)
                        if i >= 2:
                            act.wait_ge(qk_st, i - 1)
                        act.activation(rs[:, i % 2, :], sums[i % 2][:, :], ACT.Ln, scale=1.0 / HD, bias=const["eps"][:, :]).then_inc(logged, 1)
                        act.wait_ge(logged, i + 1)
                        act.activation(rs[:, i % 2, :], rs[:, i % 2, :], ACT.Exp, scale=-0.5).then_inc(rstd, 1)
                    else:
                        act.wait_ge(ready, n + 1)
                        width = P if kind == "va" else UNIT
                        act.activation(dst, bank[n % NBANK][:, :].rearrange("p (c w) -> p c w", w=width), ACT.Copy).then_inc(v_st, 1)

            @block.vector
            def _(dve):
                for i, n in enumerate(normed):
                    u, kind, x, dst, gain, perm = jobs[n]
                    dve.wait_ge(rstd, i + 1)
                    r = rs[:, i % 2, :]
                    dve.tensor_scalar(r, r, gains[:, gain:gain + 1], None, ALU.mult).then_inc(gained, 1)
                    dve.wait_ge(gained, i + 1)
                    src = bank[n % NBANK][:, :]
                    if perm:
                        o = dve.tensor_tensor(dst.rearrange("p (c t) -> p c t", c=CLS), by_class(src), by_class(r), ALU.mult)
                    else:
                        o = dve.tensor_tensor(dst, src, r, ALU.mult)
                    o.then_inc(qk_st, 1)


def windowed_attention(nc, const, T):
    HU = 4
    units = [(g, i, q) for g in range(3) for i in range(TT) for q in range(2)]
    NU = len(units)
    W = 3 * P
    with Scope(nc) as s:
        sc = s.sb("scores", [P, 2, HU, W])
        pt = s.sb("probs_t", [P, 3, W])
        mx = s.sb("row_max", [P, NU, HU])
        nm = s.sb("row_max_neg", [P, NU, HU])
        dn = s.sb("denominators", [P, NU, HU])
        ex = s.sb("sink_exp", [P, 2 * TT, HU])
        inv = s.sb("inverses", [P, 2, HU])
        s_bank = [s.ps(f"attn_score_ps{i}") for i in range(3)]
        t_bank = [s.ps(f"attn_turn_ps{i}") for i in range(2)]
        o_bank = [s.ps(f"attn_out_ps{i}") for i in range(2)]
        sc_ready, biased, p_ready, turned, pt_st, o_st = (
            s.sem("attn_" + n) for n in ("scores", "biased", "probs", "turned", "turned_stored", "stored"))
        used = s.sem("probs_t_used")
        negated, small, sunk = s.sem("row_max_negated"), s.sem("attn_small_step"), s.sem("sink_exp_ready")
        n_small = [0]
        small_at = {}

        def keys(g, i):
            if g == 2:
                return 0, [0, 1]
            b = [j for j in (i - 1, i, i + 1) if 0 <= j < TT]
            return (b[0] - i + 1) * P, b

        with nc.Block() as block:

            @block.vector
            def _(dve):
                def step(ins):
                    n_small[0] += 1
                    ins.then_inc(small, 1)
                    dve.wait_ge(small, n_small[0])

                def bias(u, h):
                    g, i, q = units[u]
                    c0, bl = keys(g, i)
                    w = len(bl) * P
                    n = HU * u + h
                    dve.wait_ge(sc_ready, n + 1)
                    tile = T["classes"][:, HU * q + h, 0:w] if g == 2 else T["band"][g][:, HU * q + h, c0:c0 + w]
                    dve.tensor_tensor(sc[:, u % 2, h, 0:w], s_bank[n % 3][:, 0:w], tile, ALU.add).then_inc(biased, 1)

                def row_max(u):
                    g, i, q = units[u]
                    w = len(keys(g, i)[1]) * P
                    dve.wait_ge(biased, HU * (u + 1))
                    m = mx[:, u, :]
                    step(dve.tensor_reduce(m, sc[:, u % 2, :, 0:w], AX_X, ALU.max))
                    if g == 0:
                        step(dve.tensor_tensor(m, m, T["sink"][:, HU * q:HU * (q + 1)], ALU.max))
                    dve.tensor_scalar(nm[:, u, :], m, -1.0, None, ALU.mult).then_inc(negated, 1)
                    if g == 0:
                        step(dve.tensor_tensor(ex[:, u, :], T["sink"][:, HU * q:HU * (q + 1)], m, ALU.subtract))
                        small_at[u] = n_small[0]

                def finish(u):
                    g, i, q = units[u]
                    dve.wait_ge(used, HU * (u + 1))
                    o = o_bank[u % 2][:, 0:HU * HD].rearrange("p (h d) -> p h d", h=HU)
                    if g == 0:
                        dve.wait_ge(sunk, u + 1)
                        dve.wait_ge(p_ready, HU * (u + 1))
                        step(dve.tensor_tensor(dn[:, u, :], dn[:, u, :], ex[:, u, :], ALU.add))
                        step(dve.reciprocal(inv[:, u % 2, :], dn[:, u, :]))
                        dve.tensor_tensor(T["ya"][:, i, HU * HD * q:HU * HD * (q + 1)].rearrange("p (h d) -> p h d", h=HU), o,
                                          inv[:, u % 2, :].unsqueeze(2).to_broadcast([P, HU, HD]), ALU.mult).then_inc(o_st, 1)
                    else:
                        dst = T["y0"] if g == 1 else T["y12"]
                        dve.wait_ge(p_ready, HU * (u + 1))
                        step(dve.tensor_copy(dst[:, i, HW + HU * q:HW + HU * (q + 1)], mx[:, u, :]))
                        step(dve.tensor_copy(dst[:, i, HW + NH + HU * q:HW + NH + HU * (q + 1)], dn[:, u, :]))
                        dve.tensor_copy(dst[:, i, HU * HD * q:HU * HD * (q + 1)], o_bank[u % 2][:, 0:HU * HD]).then_inc(o_st, 1)

                for h in range(HU):
                    bias(0, h)
                row_max(0)
                for u in range(NU):
                    w = len(keys(*units[u][0:2])[1]) * P
                    if u + 1 < NU and u >= 1:
                        dve.wait_ge(turned, HU * u)
                    for h in range(HU):
                        if u + 1 < NU:
                            bias(u + 1, h)
                        n = HU * u + h
                        dve.wait_ge(turned, n + 1)
                        if n >= 3:
                            dve.wait_ge(used, n - 2)
                        dve.tensor_copy(pt[:, n % 3, 0:w], t_bank[n % 2][:, 0:w]).then_inc(pt_st, 1)
                    if u + 1 < NU:
                        row_max(u + 1)
                    if u >= 1:
                        finish(u - 1)
                finish(NU - 1)

            @block.tensor
            def _(pe):
                def scores(u, h):
                    g, i, q = units[u]
                    n = HU * u + h
                    head = HU * q + h
                    f, b = head // 2, HD * (head % 2)
                    if n >= 3:
                        pe.wait_ge(biased, n - 2)
                    bank = s_bank[n % 3]
                    rows = slice(i * P, (i + 1) * P)
                    if g == 2:
                        for k in range(2):
                            m = pe.matmul(bank[:, k * P:(k + 1) * P], T["qb"][b:b + HD, (k + 1) * FT + f, rows],
                                          T["kb"][b:b + HD, (k + 1) * FT + f, rows], start=True, stop=True)
                    else:
                        bl = keys(g, i)[1]
                        kk = T["ka"][b:b + HD, head // 4, bl[0] * P:(bl[-1] + 1) * P] if g == 0 else \
                            T["kb"][b:b + HD, f, bl[0] * P:(bl[-1] + 1) * P]
                        qq = (T["qa"] if g == 0 else T["qb"])[b:b + HD, f, rows]
                        m = pe.matmul(bank[:, 0:len(bl) * P], qq, kk, start=True, stop=True)
                    m.then_inc(sc_ready, 1)

                def turn(u, h):
                    n = HU * u + h
                    nb = len(keys(*units[u][0:2])[1])
                    pe.wait_ge(p_ready, n + 1)
                    if n >= 2:
                        pe.wait_ge(pt_st, n - 1)
                    for j in range(nb):
                        m = pe.transpose(t_bank[n % 2][:, j * P:(j + 1) * P], sc[:, u % 2, h, j * P:(j + 1) * P], const["ident"][:, :])
                    m.then_inc(turned, 1)

                def values(u, h):
                    g, i, q = units[u]
                    n = HU * u + h
                    head = HU * q + h
                    pe.wait_ge(pt_st, n + 1)
                    if h == 0 and u >= 2:
                        pe.wait_ge(o_st, u - 1)
                    bl = keys(g, i)[1]
                    for j, b in enumerate(bl):
                        if g == 0:
                            v = T["va"][:, b, (head // 4) * HD:(head // 4 + 1) * HD]
                        elif g == 1:
                            v = T["v0"][:, b, head * HD:(head + 1) * HD]
                        else:
                            v = T["v12"][:, i, b * HW + head * HD:b * HW + (head + 1) * HD]
                        m = pe.matmul(o_bank[u % 2][:, h * HD:(h + 1) * HD], pt[:, n % 3, j * P:(j + 1) * P], v,
                                      start=(j == 0), stop=(j == len(bl) - 1))
                    m.then_inc(used, 1)

                for h in range(HU):
                    scores(0, h)
                for u in range(NU):
                    for h in range(HU):
                        if u + 1 < NU:
                            scores(u + 1, h)
                        turn(u, h)
                        if h:
                            values(u, h - 1)
                        elif u:
                            values(u - 1, HU - 1)
                values(NU - 1, HU - 1)

            @block.scalar
            def _(act):
                act.preload_act_table_set("natural_log_exp_and_others")
                for u in range(NU):
                    g, i, q = units[u]
                    w = len(keys(g, i)[1]) * P
                    act.wait_ge(negated, u + 1)
                    for h in range(HU):
                        act.activation(sc[:, u % 2, h, 0:w], sc[:, u % 2, h, 0:w], ACT.Exp, bias=nm[:, u, h:h + 1],
                                       accum_out=dn[:, u, h:h + 1]).then_inc(p_ready, 1)
                    if g == 0:
                        act.wait_ge(small, small_at[u])
                        act.activation(ex[:, u, :], ex[:, u, :], ACT.Exp).then_inc(sunk, 1)


def merge_groups(nc, const, T):
    W = HW + 2 * NH
    with Scope(nc) as s:
        m = s.sb("merged_max", [P, TT, NH])
        e = [s.sb(f"part_exp{i}", [P, TT, NH]) for i in range(2)]
        d = [s.sb(f"part_den{i}", [P, TT, NH]) for i in range(2)]
        out_st, back, st, ac = s.sem("classes_stored"), s.sem("classes_back"), s.sem("merge_step"), s.sem("merge_exp")
        dram = T["part_dram"]
        y = [T["y0"], T["y12"]]
        with nc.Block() as block:

            @block.sync
            def _(sp):
                for c in range(CLS):
                    sp.dma_start(dram.rearrange("(t c) w -> c t w", c=CLS)[c], y[1][:, c, :]).then_inc(out_st, 16)
                sp.wait_ge(out_st, 16 * CLS)
                sp.dma_start(y[1][:, :, :], dram.rearrange("(c p) w -> p c w", p=P)).then_inc(back, 16)

            @block.scalar
            def _(act):
                for j in range(2):
                    act.wait_ge(st, 3 + j)
                    act.activation(e[j][:, :, :], e[j][:, :, :], ACT.Exp).then_inc(ac, 1)

            @block.vector
            def _(dve):
                n = [0]

                def step(ins):
                    n[0] += 1
                    ins.then_inc(st, 1)
                    dve.wait_ge(st, n[0])

                mx = [x[:, :, HW:HW + NH] for x in y]
                den = [x[:, :, HW + NH:W] for x in y]
                dve.wait_ge(back, 16)
                step(dve.tensor_tensor(m[:, :, :], mx[0], mx[1], ALU.max))
                step(dve.tensor_copy(d[0][:, :, :], den[0]))
                for j in range(2):
                    step(dve.tensor_tensor(e[j][:, :, :], mx[j], m[:, :, :], ALU.subtract))
                for j in range(2):
                    dve.wait_ge(ac, j + 1)
                    step(dve.tensor_tensor(d[j][:, :, :], e[j][:, :, :], den[j], ALU.mult))
                step(dve.tensor_tensor(d[0][:, :, :], d[0][:, :, :], d[1][:, :, :], ALU.add))
                step(dve.reciprocal(d[0][:, :, :], d[0][:, :, :]))
                for j in range(2):
                    step(dve.tensor_tensor(e[j][:, :, :], e[j][:, :, :], d[0][:, :, :], ALU.mult))
                for c in range(TT):
                    for j in range(2):
                        o = y[j][:, c, 0:HW].rearrange("p (h d) -> p h d", h=NH)
                        step(dve.tensor_tensor(o, o, e[j][:, c, :].unsqueeze(2).to_broadcast([P, NH, HD]), ALU.mult))
                    step(dve.tensor_tensor(y[0][:, c, 0:HW], y[0][:, c, 0:HW], y[1][:, c, 0:HW], ALU.add))


def gate_and_merge(nc, A, const, hT, T, merged):
    UNIT, NSLOT, NBANK = 256, 3, 6
    w = A["w_in_2"].rearrange("l (k p) n -> p (l k) n", p=P)
    wa = A["w_branch_a_2"].rearrange("l (k p) n -> p (l k) n", p=P)
    wb = A["w_branch_b_2"].rearrange("l (k p) n -> p (l k) n", p=P)
    first = COL["ga"] // UNIT
    mg = COL["mg"] // UNIT
    units = list(range(first, mg))
    for j in range(4):
        units += [mg + j, mg + 4 + j]
    NGU = mg - first
    with Scope(nc) as s:
        ring = s.sb("gate_ring", [P, NSLOT, KC, UNIT])
        bw = [s.sb(f"branch_w{i}", [P, FT, D]) for i in range(2)]
        yT = s.sb("branches_t", [P, 2 * FT, S])
        sg = s.sb("gate_sigmoid", [P, 3, S])
        mix = s.sb("mix_part", [P, 2, S])
        bank = [s.ps(f"gate_ps{i}") for i in range(NBANK)]
        t_bank = [s.ps(f"turn_ps{i}") for i in range(2)]
        loaded, b_in = s.sems("gate_w_loaded", NSLOT), s.sem("branch_w_loaded")
        turned, t_st, ready, sig_r, gated, part, st = (
            s.sem("gm_" + n) for n in ("turned", "turned_stored", "ready", "sigmoid", "gated", "part", "stored"))
        y = [T["ya"], T["y0"]]
        with nc.Block() as block:

            @block.sync
            def _(sp):
                for i in range(2):
                    sp.dma_start(bw[i][:, :, :], (wa, wb)[i]).then_inc(b_in, 16)
                for n, u in enumerate(units):
                    if n >= NSLOT:
                        o = n - NSLOT
                        done = 2 * (o + 1) if o < NGU else 2 * NGU + 8 * ((o - NGU) // 2 + 1)
                        sp.wait_ge(ready, done)
                    sp.dma_start(ring[:, n % NSLOT, :, :], w[:, :, u * UNIT:(u + 1) * UNIT]).then_inc(loaded[n % NSLOT], 16)

            @block.tensor
            def _(pe):
                for f in range(2 * FT):
                    if f >= 2:
                        pe.wait_ge(t_st, f - 1)
                    for c in range(TT):
                        m = pe.transpose(t_bank[f % 2][:, c * P:(c + 1) * P], y[f // FT][:, c, (f % FT) * P:(f % FT + 1) * P], const["ident"][:, :])
                    m.then_inc(turned, 1)
                n = 0

                def tile(slot, half):
                    for k in range(KC):
                        m = pe.matmul(bank[n % NBANK][:, :], ring[:, slot, k, half * P:(half + 1) * P], hT[:, k, :],
                                      start=(k == 0), stop=(k == KC - 1))
                    m.then_inc(ready, 1)

                for i in range(NGU):
                    pe.wait_ge(loaded[i % NSLOT], 16 * (i // NSLOT + 1))
                    for half in range(2):
                        if n >= NBANK:
                            pe.wait_ge(gated, n - NBANK + 1)
                        tile(i % NSLOT, half)
                        n += 1
                pe.wait_ge(b_in, 32)
                for j in range(4):
                    for half in range(2):
                        for b in range(2):
                            i = NGU + 2 * j + b
                            if half == 0:
                                pe.wait_ge(loaded[i % NSLOT], 16 * (i // NSLOT + 1))
                            o = n - NBANK
                            if o < 2 * NGU:
                                pe.wait_ge(gated, o + 1)
                            else:
                                k, r = divmod(o - 2 * NGU, 4)
                                pe.wait_ge(sig_r, 2 * NGU + 2 * k + r + 1) if r < 2 else pe.wait_ge(part, 3 * k + r - 1)
                            tile(i % NSLOT, half)
                            n += 1
                        if j == 0 and half == 0:
                            pe.wait_ge(gated, 2 * NGU)
                        for b in range(2):
                            o = n - NBANK
                            if o < 2 * NGU:
                                pe.wait_ge(gated, o + 1)
                            else:
                                k, r = divmod(o - 2 * NGU, 4)
                                pe.wait_ge(sig_r, 2 * NGU + 2 * k + r + 1) if r < 2 else pe.wait_ge(part, 3 * k + r - 1)
                            t = 2 * j + half
                            for k in range(FT):
                                m = pe.matmul(bank[n % NBANK][:, :], bw[b][:, k, t * P:(t + 1) * P], yT[:, b * FT + k, :],
                                              start=(k == 0), stop=(k == FT - 1))
                            m.then_inc(ready, 1)
                            n += 1

            @block.scalar
            def _(act):
                for f in range(2 * NGU):
                    act.wait_ge(ready, f + 1)
                    if f >= 3:
                        act.wait_ge(gated, f - 2)
                    act.activation(sg[:, f % 3, :], bank[f % NBANK][:, :], ACT.Sigmoid).then_inc(sig_r, 1)
                for t in range(KC):
                    for b in range(2):
                        i = 2 * NGU + 2 * t + b
                        n = 2 * NGU + 4 * t + b
                        act.wait_ge(ready, n + 1)
                        o = i - 3
                        if o < 2 * NGU:
                            act.wait_ge(gated, o + 1)
                        else:
                            k, r = divmod(o - 2 * NGU, 2)
                            act.wait_ge(part, 3 * k + r + 1)
                        act.activation(sg[:, i % 3, :], bank[n % NBANK][:, :], ACT.Sigmoid,
                                       bias=par_col(const, PARAM_AT["b_merge_2"] + b * KC + t)).then_inc(sig_r, 1)

            @block.vector
            def _(dve):
                for f in range(2 * FT):
                    dve.wait_ge(turned, f + 1)
                    dve.tensor_copy(yT[:, f, :], t_bank[f % 2][:, :]).then_inc(t_st, 1)
                for f in range(2 * FT):
                    dve.wait_ge(sig_r, f + 1)
                    dve.wait_ge(t_st, 2 * FT)
                    dve.tensor_tensor(sg[:, f % 3, :], bank[f % NBANK][:, :], sg[:, f % 3, :], ALU.mult).then_inc(st, 1)
                    dve.wait_ge(st, f + 1)
                    dve.tensor_tensor(yT[:, f, :], yT[:, f, :], sg[:, f % 3, :], ALU.mult).then_inc(gated, 1)
                for t in range(KC):
                    for b in range(2):
                        n = 2 * NGU + 4 * t + 2 + b
                        i = 2 * NGU + 2 * t + b
                        dve.wait_ge(ready, n + 1)
                        dve.wait_ge(sig_r, i + 1)
                        if b == 0 and t:
                            dve.wait_ge(part, 3 * t)
                        dve.tensor_tensor(mix[:, b, :], bank[n % NBANK][:, :], sg[:, i % 3, :], ALU.mult).then_inc(part, 1)
                    dve.wait_ge(part, 3 * t + 2)
                    dve.tensor_tensor(merged[:, t, :], mix[:, 0, :], mix[:, 1, :], ALU.add).then_inc(part, 1)


def second_block(nc, A, const, out):
    with Scope(nc) as b2:
        recycle(nc)
        hT = b2.sb("block_in_t", [P, KC, S])
        T = {"ya": b2.sb("y_a", [P, TT, HW]), "y0": b2.sb("y_b0", [P, TT, HW + 2 * NH]),
             "head_gains": b2.sb("head_gains", [P, 4]), "sink": b2.sb("sink", [P, NH]),
             "bias_dram": nc.dram_tensor("bias_rows_dram", (4, NH, SKEW, 512), F32, kind="Internal").ap(),
             "part_dram": nc.dram_tensor("class_part_dram", (S, HW + 2 * NH), F32, kind="Internal").ap()}
        norm_to_features(nc, const["h"], PARAM_AT["norm_gain_2"], hT, const, "n2")
        head_gain_columns(nc, const, T)
        with Scope(nc) as s:
            T["band"] = [s.sb(f"band_bias{g_}", [P, NH, 3 * P]) for g_ in range(2)]
            T["classes"] = s.sb("class_bias", [P, NH, 2 * P])
            T["qa"], T["ka"] = s.sb("qa", [P, FT, S]), s.sb("ka", [P, 2, S])
            T["qb"], T["kb"] = s.sb("qb", [P, 3 * FT, S]), s.sb("kb", [P, 3 * FT, S])
            T["va"], T["v0"], T["v12"] = s.sb("va", [P, TT, P]), s.sb("vb0", [P, TT, HW]), s.sb("vb12", [P, TT, 2 * HW])
            bias_tables(nc, A, const, T)
            project_second(nc, A, const, hT, T)
            recycle(nc)
            T["y12"] = s.sb("y_b12", [P, TT, HW + 2 * NH])
            windowed_attention(nc, const, T)
            merge_groups(nc, const, T)
        merged = b2.sb("merged", [P, KC, S])
        gate_and_merge(nc, A, const, hT, T, merged)
        out_projection(nc, const, A["w_out_2"], merged, KC, const["h"], "wo2", out.rearrange("b t d -> (b t) d"))


def program(nc, A, out):
    Scope.ended = []
    with Scope(nc) as g:
        const = {"h": g.sb("h", [P, TT, D]), "ident": g.sb("ident", [P, P]), "par": g.sb("params", [P, P]),
                 "heads": g.sb("heads", [P, P]),
                 "eps": g.sb("eps", [P, 1]), "gn_eps": g.sb("gn_eps", [P, 1]), "log_shift": g.sb("log_shift", [P, 1]), "x_loaded": g.sem("x_loaded"), "row_params": g.sem("row_params_loaded")}
        once = g.stack.enter_context(Scope(nc))
        const.update({"causal": once.sb("causal", [P, 4, P]), "neg_causal": once.sb("neg_causal", [P, P]),
                      "minus_ones": once.sb("minus_ones", [P, P]), "suffix": once.sb("suffix", [P, P]),
                      "level": once.sb("level", [P, 7, P]),
                      "one_minus_mu": once.sb("one_minus_mu", [P, RT]), "one_minus_ka": once.sb("one_minus_ka", [P, FT]),
                      "ffn_g": once.sb("ffn_gain", [P, D]), "fin_g": once.sb("final_gain", [P, D])})
        setup_constants(nc, A, const)
        with Scope(nc) as b1:
            mixT = b1.sb("mixer_out", [P, KC, S])
            um = b1.sb("um", [P, RT, S])
            with Scope(nc) as sc:
                qk = sc.sb("qk", [P, 2 * FT, S])
                v = sc.sb("v", [P, TT, HW])
                with Scope(nc) as s:
                    xnT = s.sb("xnT", [P, KC, S])
                    norm_to_features(nc, const["h"], PARAM_AT["norm_mix_g"], xnT, const, "n1", const["x_loaded"])
                    project_first(nc, A, xnT, um, qk, v, const)
                stick_breaking(nc, const, qk, v, mixT)
            with Scope(nc) as rw:
                R = {"gate": rw.sb("gate", [P, FT, S]), "bonus": rw.sb("bonus", [P, FT, S]),
                     "kr": rw.sb("kk_r", [P, FT * NC, 2, CH]), "bh": rw.sb("b_hat", [P, FT, S]),
                     "kh": rw.sb("k_hat", [P, FT, S]), "mid": rw.sb("mid_decay", [P, FT * NC]),
                     "ends": rw.sb("chunk_sums", [P, FT * NC])}
                rwkv_features(nc, A, const, um, R)
                R["q"] = rw.sb("q_hat", [P, FT, S])
                R["o"] = rw.sb("rwkv_out", [P, FT, S])
                R["mn"] = rw.sb("m_n", [P, FT * NC, 2, HD])
                rwkv_chunks(nc, const, um, R)
                rwkv_output(nc, const, R, mixT)
            out_projection(nc, const, A["w_out"], mixT, KC, const["h"], "wo")
        with Scope(nc) as moe:
            M = {"slots": moe.sb("slots", [P, 2, TT], I32), "weights": moe.sb("route_weights", [P, 2, TT]),
                 "rounds": moe.sb("rounds", [P, 1], I32)}
            xn_dram = nc.dram_tensor("ffn_in_dram", (S, D), F32, kind="Internal").ap()
            list_dram = nc.dram_tensor("expert_lists", (NE * S, 2), I32, kind="Internal").ap()
            y_dram = nc.dram_tensor("expert_rows_dram", (2 * S + NE * S + 4 * CAP, D), F32, kind="Internal").ap()
            route(nc, A, const, const["h"], xn_dram, list_dram, M)
            recycle(nc)
            experts(nc, A, const, xn_dram, list_dram, y_dram, M)
            combine(nc, const, const["h"], y_dram, M)
        once.stack.close()
        second_block(nc, A, const, out)


def shape_constants():
    def bucket(rel):
        half, exact = BUCKETS // 2, BUCKETS // 4
        n = np.abs(rel)
        large = exact + (np.log(np.maximum(n, exact).astype(np.float32) / np.float32(exact)) / np.float32(np.log(1024 / exact))
                         * np.float32(half - exact)).astype(np.int32)
        return (rel > 0) * half + np.where(n < exact, n, np.minimum(large, half - 1))

    x = np.arange(512)
    band = np.minimum(x, A_REL - 1) - (2 * P - 1)
    apart = np.minimum(x, 2 * P - 2) - (P - 1)
    rels = [band, 4 * apart, 4 * apart]
    hot = np.stack([(bucket(r)[None, :] == np.arange(BUCKETS)[:, None]) for r in rels]).astype(np.float32)
    ok = [np.abs(band) <= 128, np.abs(band) <= 64, np.abs(apart) <= 64, apart % 4 == 0]
    window = np.stack([np.broadcast_to(np.where(o, 0.0, NEG), (NH, 512)) for o in ok]).astype(np.float32)
    return {"const_bucket_hot": np.ascontiguousarray(hot), "const_window": np.ascontiguousarray(window)}


def kernel(**inputs):
    import concourse.bacc as bacc
    from concourse.bass_utils import run_bass_kernel_spmd

    nc = bacc.Bacc("TRN2", target_bir_lowering=False, num_devices=1)
    arrays, A = {}, {}
    for name, a in {**inputs, **shape_constants()}.items():
        a = np.ascontiguousarray(a)
        arrays[name + "_dram"] = a
        A[name] = nc.dram_tensor(name + "_dram", a.shape, mybir.dt.from_np(a.dtype), kind="ExternalInput").ap()
    out = nc.dram_tensor("out_dram", (1, S, D), F32, kind="ExternalOutput").ap()
    program(nc, A, out)
    r = run_bass_kernel_spmd(nc, [arrays], core_ids=[0])
    return r.results[0]["out_dram"]
```

```python
from contextlib import ExitStack

import numpy as np

import concourse.bass as bass
from concourse import mybir

F32 = mybir.dt.float32
F32R = mybir.dt.float32r
I32 = mybir.dt.int32
U32 = mybir.dt.uint32
ALU = mybir.AluOpType
ACT = mybir.ActivationFunctionType
AX_X = mybir.AxisListType.X

P = 128
S = 512
TT = S // P
D = 1024
KC = D // P
NH = 8
HD = 64
HW = NH * HD
FT = HW // P
SB_IN = 3 * HW
RW_IN = 3 * HW + 64 + 64 + 128
RT = RW_IN // P
EPS = 1e-6
GN_EPS = 64e-5
DECAY = float(np.exp(-0.5))
NEG = -1e30
LOG_BITS = 30
CH = P
NC = S // CH

NG, EPG = 4, 8
NE = NG * EPG
DE = 256
CAP = 64
NB = 4
UNROLL = 8
LIST = NE * S + NB * CAP
FC = DE // P

PARAM_ROWS = [("norm_mix_g", 8), ("shift_mu", RT), ("sb_out_g", 4), ("rw_w0", 4), ("rw_a0", 4), ("rw_k_k", 4),
              ("rw_k_a", 4), ("rw_r_k", 4), ("rw_ln_w", 4), ("rw_ln_b", 4), ("norm_gain_2", 8), ("b_merge_2", 16),
              ("q_norm_a_2", 1), ("k_norm_a_2", 1), ("q_norm_b_2", 1), ("k_norm_b_2", 1)]
PARAM_AT = {}
_row = 0
for _name, _n in PARAM_ROWS:
    PARAM_AT[_name] = _row
    _row += _n
N_PARAMS = _row


class Scope:

    ended = []

    def __init__(self, nc):
        self.nc = nc
        self.stack = ExitStack()
        self.own = []

    def __enter__(self):
        return self

    def __exit__(self, *e):
        Scope.ended += self.own
        self.own = []
        return self.stack.__exit__(*e)

    def sb(self, name, shape, dt=F32):
        return self.stack.enter_context(self.nc.sbuf_tensor(name, shape, dt))

    def ps(self, name, n=512):
        return self.stack.enter_context(self.nc.psum_tensor(name, [P, n], F32))

    def sem(self, name):
        self.own.append(self.nc.alloc_semaphore(name))
        return self.own[-1]

    def sems(self, name, n):
        return [self.sem(f"{name}{i}") for i in range(n)]


def recycle(nc):
    nc.clear_and_free_semaphores(Scope.ended)
    Scope.ended = []
    nc.all_engine_barrier()


def setup_constants(nc, A, const):
    with Scope(nc) as s:
        rows = s.sb("param_rows", [P, P])
        pst = s.ps("param_ps")
        loaded = s.sem("params_loaded")
        padded = s.sem("param_rows_padded")
        turned = s.sem("params_turned")
        copied = s.sem("params_copied")
        made = s.sem("masks_made")
        ident, par = const["ident"], const["par"]
        n_loads = 0
        for name, n in PARAM_ROWS:
            n_loads += 2 if "_norm_" in name else 1
        with nc.Block() as block:

            @block.sync
            def _(sp):
                sp.dma_start(const["h"][:, :, :], A["x"].rearrange("b (c p) d -> p (b c) d", p=P)).then_inc(const["x_loaded"], 16)
                sp.wait_ge(padded, 1)
                for name, n in PARAM_ROWS:
                    r = PARAM_AT[name]
                    if "_norm_" in name:
                        for half in range(2):
                            sp.dma_start(rows[r:r + 1, half * HD:(half + 1) * HD], A[name]).then_inc(loaded, 16)
                    else:
                        src = A[name]
                        if len(src.shape) == 3:
                            src = src.rearrange("l a b -> l (a b)")
                        sp.dma_start(rows[r:r + n, :], src.rearrange("l (n p) -> (l n) p", p=P)).then_inc(loaded, 16)
                sp.dma_start(const["ffn_g"][:, :], A["norm_ffn_g"][0:1, :].broadcast_to([P, D])).then_inc(const["row_params"], 16)
                sp.dma_start(const["fin_g"][:, :], A["final_norm_g"].rearrange("(a d) -> a d", a=1).broadcast_to([P, D])).then_inc(const["row_params"], 16)

            @block.gpsimd
            def _(pool):
                n = [0]

                def step(ins):
                    n[0] += 1
                    ins.then_inc(made, 1)
                    pool.wait_ge(made, n[0])

                step(pool.memset(const["eps"][:, :], EPS))
                step(pool.memset(const["gn_eps"][:, :], GN_EPS))
                step(pool.memset(const["log_shift"][:, :], float(0.5 * LOG_BITS * np.log(2.0))))
                step(pool.memset(ident[:, :], 0.0))
                step(pool.affine_select(out=ident[:, :], in_=ident[:, :], compare_op=ALU.not_equal, fill=1.0, base=0,
                                        pattern=[[-1, P]], channel_multiplier=1))
                cm = const["causal"]
                step(pool.memset(cm[:, :, :], 1.0))
                for k in range(4):
                    step(pool.affine_select(out=cm[:, k, :], in_=cm[:, k, :], fill=0.0, base=0, pattern=[[1, P]],
                                            compare_op=(ALU.is_gt, ALU.is_ge)[k % 2], channel_multiplier=-1))
                step(pool.memset(const["neg_causal"][:, :], 0.0))
                step(pool.affine_select(out=const["neg_causal"][:, :], in_=const["neg_causal"][:, :], fill=NEG, base=0,
                                        pattern=[[1, P]], compare_op=ALU.is_gt, channel_multiplier=-1))
                step(pool.memset(const["minus_ones"][:, :], -1.0))
                step(pool.memset(const["suffix"][:, :], -1.0))
                step(pool.affine_select(out=const["suffix"][:, :], in_=const["suffix"][:, :], fill=0.0, base=0,
                                        pattern=[[-1, P]], compare_op=ALU.is_ge, channel_multiplier=1))
                step(pool.memset(const["heads"][:, :], 0.0))
                step(pool.memset(const["heads"][0:HD, 0:HD], 1.0))
                step(pool.memset(const["heads"][HD:P, HD:P], 1.0))
                for l in range(7):
                    m = 1 << l
                    lv = const["level"][:, l, :]
                    step(pool.memset(lv, 0.0))
                    v = lv.rearrange("p (b h x) -> p b h x", h=2, x=m)[:, :, 0, :]
                    step(pool.memset(v, 1.0))
                    nb = P // (2 * m)
                    step(pool.affine_select(out=v, in_=v, fill=0.0, base=-m, pattern=[[-2 * m, nb], [0, m]],
                                            compare_op=ALU.is_ge, channel_multiplier=1))
                    step(pool.affine_select(out=v, in_=v, fill=0.0, base=2 * m, pattern=[[2 * m, nb], [0, m]],
                                            compare_op=ALU.is_gt, channel_multiplier=-1))
                const["n_masks"] = n[0]

            @block.tensor
            def _(pe):
                pe.wait_ge(made, 5)
                pe.wait_ge(loaded, 16 * n_loads)
                pe.transpose(pst[:, 0:P], rows[:, :], ident[:, :]).then_inc(turned, 1)

            @block.vector
            def _(dve):
                dve.memset(rows[:, :], 0.0).then_inc(padded, 1)
                dve.wait_ge(turned, 1)
                dve.tensor_copy(par[:, :], pst[:, 0:N_PARAMS]).then_inc(copied, 1)
                mu = PARAM_AT["shift_mu"]
                dve.wait_ge(copied, 1)
                dve.tensor_scalar(const["one_minus_mu"][:, :], par[:, mu:mu + RT], -1.0, 1.0, ALU.mult, ALU.add).then_inc(copied, 1)
                ka = PARAM_AT["rw_k_a"]
                dve.tensor_scalar(const["one_minus_ka"][:, :], par[:, ka:ka + FT], -1.0, 1.0, ALU.mult, ALU.add).then_inc(copied, 1)
                dve.wait_ge(copied, 3)


def norm_to_features(nc, src, gain, dst, const, tag, x_loaded=None, low=None):
    with Scope(nc) as s:
        sq = s.sb(tag + "_sq", [P, D])
        xs = s.sb(tag + "_scaled", [P, TT, D])
        ss = s.sb(tag + "_ss", [P, TT])
        rs = s.sb(tag + "_rstd", [P, TT])
        banks = [s.ps(f"{tag}_ps{i}") for i in range(4)]
        squared = s.sem(tag + "_squares_summed")
        rstd = s.sem(tag + "_rstd_ready")
        scaled = s.sem(tag + "_tokens_scaled")
        turned = s.sem(tag + "_chunk_turned")
        even_st = s.sem(tag + "_even_chunk_stored")
        odd_st = s.sem(tag + "_odd_chunk_stored")
        ident, par = const["ident"], const["par"]
        with nc.Block() as block:

            @block.scalar
            def _(act):
                if x_loaded is not None:
                    act.wait_ge(x_loaded, 16)
                for c in range(TT):
                    if c:
                        act.wait_ge(squared, c)
                    act.activation(sq[:, :], src[:, c, :], ACT.Square, accum_out=ss[:, c:c + 1]).then_inc(squared, 1)
                act.wait_ge(rstd, 1)
                act.activation(ss[:, :], ss[:, :], ACT.Sqrt).then_inc(rstd, 1)
                for k in range(0, KC, 1 if low is not None else 2):
                    act.wait_ge(turned, k + 1)
                    act.activation(dst[:, k, :], banks[k % 4][:, :], ACT.Copy,
                                   scale=par[:, gain + k:gain + k + 1]).then_inc(even_st, 1)

            @block.vector
            def _(dve):
                dve.wait_ge(squared, TT)
                dve.tensor_scalar(ss[:, :], ss[:, :], 1.0 / D, EPS, ALU.mult, ALU.add).then_inc(rstd, 1)
                dve.wait_ge(rstd, 2)
                dve.reciprocal(rs[:, :], ss[:, :]).then_inc(rstd, 1)
                dve.wait_ge(rstd, 3)
                for c in range(TT):
                    dve.tensor_scalar(xs[:, c, :], src[:, c, :], rs[:, c:c + 1], None, ALU.mult).then_inc(scaled, 1)
                if low is not None:
                    for k in range(KC):
                        dve.wait_ge(even_st, k + 1)
                        dve.scalar_tensor_tensor(out=low[:, k, :], in0=banks[k % 4][:, :], scalar=par[:, gain + k:gain + k + 1],
                                                 in1=dst[:, k, :], op0=ALU.mult, op1=ALU.subtract).then_inc(odd_st, 1)
                    return
                for k in range(1, KC, 2):
                    dve.wait_ge(turned, k + 1)
                    dve.tensor_scalar(dst[:, k, :], banks[k % 4][:, :], par[:, gain + k:gain + k + 1], None,
                                      ALU.mult).then_inc(odd_st, 1)

            @block.tensor
            def _(pe):
                for k in range(KC):
                    if k >= 4 and low is not None:
                        pe.wait_ge(odd_st, k - 3)
                    elif k >= 4:
                        pe.wait_ge((even_st, odd_st)[k % 2], (k - 4) // 2 + 1)
                    for c in range(TT):
                        pe.wait_ge(scaled, c + 1)
                        t = pe.transpose(banks[k % 4][:, c * P:(c + 1) * P], xs[:, c, k * P:(k + 1) * P], ident[:, :])
                    t.then_inc(turned, 1)


def project_first(nc, A, xnT, um, qk, v, const):
    UNIT = 256
    NSLOT = 4
    NBANK = 6
    w = A["w_in"].rearrange("l (k p) n -> p (l k) n", p=P)
    units = [SB_IN + UNIT * i for i in range(RW_IN // UNIT)] + [UNIT * i for i in range(SB_IN // UNIT)]
    tiles = [(SB_IN + P * i) for i in range(RT)] + [P * i for i in range(2 * FT)]
    with Scope(nc) as s:
        ring = s.sb("w_in_ring", [P, NSLOT, KC, UNIT])
        shifted = s.sb("shifted", [P, 2, S])
        banks = [s.ps(f"u_ps{i}") for i in range(NBANK)]
        vbank = banks[0:4]
        loaded = s.sems("w_in_loaded", NSLOT)
        ready = s.sem("u_tile_ready")
        sh_zero = s.sem("shift_zeroed")
        sh = s.sem("u_shifted")
        mixed = s.sem("u_mixed")
        qk_st = s.sem("qk_stored")
        v_ready = s.sem("v_ready")
        v_st = s.sem("v_stored")
        with nc.Block() as block:

            @block.sync
            def _(sp):
                for i, col in enumerate(units):
                    if i >= NSLOT:
                        sp.wait_ge(ready, 2 * (i - NSLOT + 1))
                    sp.dma_start(ring[:, i % NSLOT, :, :], w[:, :, col:col + UNIT]).then_inc(loaded[i % NSLOT], 16)

            @block.tensor
            def _(pe):
                n = 0
                for i, col in enumerate(units):
                    pe.wait_ge(loaded[i % NSLOT], 16 * (i // NSLOT + 1))
                    if i < len(tiles) * P // UNIT:
                        for half in range(2):
                            if n >= NBANK:
                                done = n - NBANK + 1
                                pe.wait_ge(mixed, min(done, RT))
                                if done > RT:
                                    pe.wait_ge(qk_st, done - RT)
                            for k in range(KC):
                                m = pe.matmul(banks[n % NBANK][:, :], ring[:, i % NSLOT, k, half * P:(half + 1) * P],
                                              xnT[:, k, :], start=(k == 0), stop=(k == KC - 1))
                            m.then_inc(ready, 1)
                            n += 1
                    else:
                        part = i - len(tiles) * P // UNIT
                        if part == 0:
                            pe.wait_ge(qk_st, 2 * FT)
                        for c in range(TT):
                            for k in range(KC):
                                m = pe.matmul(vbank[c][:, part * UNIT:(part + 1) * UNIT], xnT[:, k, c * P:(c + 1) * P],
                                              ring[:, i % NSLOT, k, :], start=(k == 0), stop=(k == KC - 1))
                            if c == TT - 1 and part == 1:
                                m.then_inc(v_ready, 1)

            @block.scalar
            def _(act):
                mu = PARAM_AT["shift_mu"]
                act.wait_ge(sh_zero, 1)
                for j in range(RT):
                    act.wait_ge(ready, j + 1)
                    if j >= 2:
                        act.wait_ge(mixed, j - 1)
                    act.activation(shifted[:, j % 2, 1:S], banks[j % NBANK][:, 0:S - 1], ACT.Copy,
                                   scale=par_col(const, mu + j)).then_inc(sh, 1)
                for j in range(2 * FT):
                    n = RT + j
                    act.wait_ge(ready, n + 1)
                    act.activation(qk[:, j, :], banks[n % NBANK][:, :], ACT.Copy,
                                   scale=HD ** -0.5 if j < FT else 1.0).then_inc(qk_st, 1)

            @block.vector
            def _(dve):
                dve.memset(shifted[:, :, 0:1], 0.0).then_inc(sh_zero, 1)
                for j in range(RT):
                    dve.wait_ge(sh, j + 1)
                    dve.scalar_tensor_tensor(out=um[:, j, :], in0=banks[j % NBANK][:, :],
                                             scalar=const["one_minus_mu"][:, j:j + 1], in1=shifted[:, j % 2, :],
                                             op0=ALU.mult, op1=ALU.add).then_inc(mixed, 1)
                dve.wait_ge(v_ready, 1)
                for c in range(TT):
                    dve.tensor_copy(v[:, c, :], vbank[c][:, :]).then_inc(v_st, 1)


def split_product(pe, out, a, b, n):
    for k in range(n):
        for i, j in ((0, 0), (0, 1), (1, 0)):
            m = pe.matmul(out, a(k)[i], b(k)[j], start=(k == 0 and i + j == 0), stop=(k == n - 1 and i == 1))
    return m


class SplitWeights:

    def __init__(self, s, tag, w, cols, unit, used):
        self.w, self.cols, self.unit, self.used = w, cols, unit, used
        self.raw = s.sb(tag + "_raw", [P, 2, KC, unit])
        self.part = [s.sb(tag + "_high", [P, 2, KC, unit], F32R), s.sb(tag + "_low", [P, 2, KC, unit], F32R)]
        self.loaded = s.sems(tag + "_loaded", 2)
        self.high, self.low = s.sem(tag + "_high_ready"), s.sem(tag + "_low_ready")

    def load(self, sp, n):
        if n >= 2:
            sp.wait_ge(self.low, n - 1)
        sp.dma_start(self.raw[:, n % 2, :, :], self.w[:, :, self.cols[n]:self.cols[n] + self.unit]).then_inc(self.loaded[n % 2], 16)

    def split_high(self, act, n):
        if n >= len(self.cols):
            return
        if n >= 2:
            act.wait_ge(*self.used(n - 2))
        act.wait_ge(self.loaded[n % 2], 16 * (n // 2 + 1))
        act.activation(self.part[0][:, n % 2, :, :], self.raw[:, n % 2, :, :], ACT.Copy).then_inc(self.high, 1)

    def split_low(self, dve, n):
        if n >= len(self.cols):
            return
        if n >= 2:
            dve.wait_ge(*self.used(n - 2))
        dve.wait_ge(self.high, n + 1)
        dve.tensor_tensor(self.part[1][:, n % 2, :, :], self.raw[:, n % 2, :, :], self.part[0][:, n % 2, :, :],
                          ALU.subtract).then_inc(self.low, 1)

    def wait(self, pe, n):
        pe.wait_ge(self.low, n + 1)

    def parts(self, n, k, cols):
        return [p[:, n % 2, k, cols] for p in self.part]


def par_col(const, i):
    return const["par"][:, i:i + 1]


def normalize_heads(nc, const, tiles, tag):
    with Scope(nc) as s:
        sq = s.sb(tag + "_sq", [P, 2, S])
        rs = s.sb(tag + "_rstd", [P, 2, S])
        banks = [s.ps(f"{tag}_ps{i}") for i in range(2)]
        squared = s.sem("head_squares")
        summed = s.sem("head_sums")
        logged = s.sem("head_logs")
        rstd = s.sem("head_rstd")
        scaled = s.sem("head_scaled")
        n = len(tiles)
        with nc.Block() as block:

            @block.scalar
            def _(act):
                act.preload_act_table_set("natural_log_exp_and_others")
                for j in range(n + 1):
                    if j < n:
                        if j >= 2:
                            act.wait_ge(summed, j - 1)
                        act.activation(sq[:, j % 2, :], tiles[j][0], ACT.Square).then_inc(squared, 1)
                    if j >= 1:
                        i = j - 1
                        act.wait_ge(summed, i + 1)
                        if i >= 2:
                            act.wait_ge(scaled, i - 1)
                        act.activation(rs[:, i % 2, :], banks[i % 2][:, :], ACT.Ln, scale=1.0 / HD,
                                       bias=const["eps"][:, :]).then_inc(logged, 1)
                        act.wait_ge(logged, i + 1)
                        act.activation(rs[:, i % 2, :], rs[:, i % 2, :], ACT.Exp, scale=-0.5).then_inc(rstd, 1)

            @block.tensor
            def _(pe):
                for j in range(n):
                    pe.wait_ge(squared, j + 1)
                    if j >= 2:
                        pe.wait_ge(logged, j - 1)
                    pe.matmul(banks[j % 2][:, :], const["heads"][:, :], sq[:, j % 2, :], start=True, stop=True).then_inc(summed, 1)

            @block.vector
            def _(dve):
                for j in range(n):
                    src, gain, dst = tiles[j]
                    dve.wait_ge(rstd, j + 1)
                    dve.scalar_tensor_tensor(out=dst, in0=src, scalar=gain, in1=rs[:, j % 2, :],
                                             op0=ALU.mult, op1=ALU.mult).then_inc(scaled, 1)


def stick_breaking(nc, const, qk, v, mixT):
    OFF = [0, 512, 1024, 896]
    N = 1280
    with Scope(nc) as outer, Scope(nc) as s:
        raw = outer.sb("stick_out", [P, FT, S])
        zt = [s.stack.enter_context(nc.psum_tensor(f"z_ps{i}", [P, 3 * 512], F32)) for i in range(2)]
        avt = [s.ps(f"av_ps{i}") for i in range(2)]
        ln = s.sb("ln_rest", [P, 2, N])
        spl = s.sb("softplus", [P, 2, N])
        wt = s.sb("stick_weights", [P, 2, N])
        z_ready = s.sem("z_ready")
        abs_ready = s.sem("abs_ready")
        e_ready = s.sem("exp_ready")
        l_ready = s.sem("log_ready")
        sp_ready = s.sem("softplus_ready")
        masked = s.sem("softplus_masked")
        suf_ready = s.sem("suffix_ready")
        neg_ready = s.sem("diagonal_masked")
        w_ready = s.sem("stick_weights_ready")
        av_ready = s.sem("stick_av_ready")
        raw_ready = s.sem("stick_out_ready")

        def blk(t, i, t0=None):
            t0 = i if t0 is None else t0
            return t[:, OFF[i] + (t0 - i) * P:OFF[i] + (TT - i) * P]

        with nc.Block() as block:

            @block.tensor
            def _(pe):
                def scores(h):
                    f, b = h // 2, HD * (h % 2)
                    if h >= 2:
                        pe.wait_ge(w_ready, h - 1)
                    for i in (0, 1, 3, 2):
                        m = pe.matmul(blk(zt[h % 2], i), qk[b:b + HD, FT + f, i * P:(i + 1) * P], qk[b:b + HD, f, i * P:S],
                                      start=(i != 3), stop=True, skip_group_check=True)
                    m.then_inc(z_ready, 1)

                def suffix(h):
                    pe.wait_ge(masked, 4 * (h + 1))
                    for i in range(TT):
                        for j in range(i, TT):
                            m = pe.matmul(blk(zt[h % 2], i, j), const["suffix" if j == i else "minus_ones"][:, :],
                                          blk(spl[:, h % 2, :], j), start=False, stop=True, skip_group_check=True)
                    m.then_inc(suf_ready, 1)

                def values(h):
                    b = HD * (h % 2)
                    pe.wait_ge(w_ready, h + 1)
                    if h >= 4:
                        pe.wait_ge(raw_ready, h // 2 - 1)
                    for i in range(TT):
                        m = pe.matmul(avt[h // 2 % 2][b:b + HD, i * P:S], v[:, i, h * HD:(h + 1) * HD],
                                      blk(wt[:, h % 2, :], i), start=(i == 0), stop=(i == TT - 1))
                    m.then_inc(av_ready, 1)

                scores(0)
                scores(1)
                for h in range(NH):
                    suffix(h)
                    if h >= 1:
                        values(h - 1)
                    if h + 2 < NH:
                        scores(h + 2)
                values(NH - 1)

            @block.vector
            def _(dve):
                def softplus(h):
                    dve.wait_ge(l_ready, h + 1)
                    if h >= 2:
                        dve.wait_ge(suf_ready, h - 1)
                    dve.scalar_tensor_tensor(out=spl[:, h % 2, :], in0=zt[h % 2][:, 0:N], scalar=0.0, in1=ln[:, h % 2, :],
                                             op0=ALU.max, op1=ALU.add).then_inc(sp_ready, 1)

                def mask(h):
                    dve.wait_ge(suf_ready, h + 1)
                    for i in range(TT):
                        d = zt[h % 2][:, OFF[i]:OFF[i] + P]
                        dve.tensor_tensor(d, d, const["neg_causal"][:, :], ALU.add).then_inc(neg_ready, 1)

                softplus(0)
                for h in range(NH):
                    if h + 1 < NH:
                        softplus(h + 1)
                    mask(h)

            @block.gpsimd
            def _(pool):
                for h in range(NH):
                    pool.wait_ge(sp_ready, h + 1)
                    for i in range(TT):
                        d = spl[:, h % 2, OFF[i]:OFF[i] + P]
                        pool.tensor_tensor(d, d, const["causal"][:, 0, :], ALU.mult).then_inc(masked, 1)

            @block.scalar
            def _(act):
                def log_rest(h):
                    x = ln[:, h % 2, :]
                    act.wait_ge(z_ready, h + 1)
                    if h >= 2:
                        act.wait_ge(sp_ready, h - 1)
                    act.activation(x, zt[h % 2][:, 0:N], ACT.Abs).then_inc(abs_ready, 1)
                    act.wait_ge(abs_ready, h + 1)
                    act.activation(x, x, ACT.Exp, scale=-1.0).then_inc(e_ready, 1)
                    act.wait_ge(e_ready, h + 1)
                    act.activation(x, x, ACT.Ln, bias=1.0).then_inc(l_ready, 1)

                def weights(h):
                    act.wait_ge(neg_ready, 4 * (h + 1))
                    if h >= 2:
                        act.wait_ge(av_ready, h - 1)
                    act.activation(wt[:, h % 2, :], zt[h % 2][:, 0:N], ACT.Exp).then_inc(w_ready, 1)

                act.preload_act_table_set("natural_log_exp_and_others")
                log_rest(0)
                for h in range(NH):
                    if h + 1 < NH:
                        log_rest(h + 1)
                    weights(h)
                    if h % 2 == 0 and h >= 2:
                        f = h // 2 - 1
                        act.wait_ge(av_ready, h)
                        act.activation(raw[:, f, :], avt[f % 2][:, :], ACT.Copy).then_inc(raw_ready, 1)
                act.wait_ge(av_ready, NH)
                act.activation(raw[:, FT - 1, :], avt[(FT - 1) % 2][:, :], ACT.Copy).then_inc(raw_ready, 1)

        s.stack.close()
        g = PARAM_AT["sb_out_g"]
        normalize_heads(nc, const, [(raw[:, f, :], par_col(const, g + f), mixT[:, f, :]) for f in range(FT)],
                        "sbn")


def rwkv_features(nc, A, const, um, R):
    r, k, vv = um[:, 0:FT, :], um[:, FT:2 * FT, :], um[:, 2 * FT:3 * FT, :]
    with Scope(nc) as s:
        wa2 = s.sb("lora_w2_a2", [P, HW])
        g2 = s.sb("lora_g2", [P, HW])
        lora = s.sb("lora_in", [P, 2, S])
        sig = s.sb("decay_sigmoid", [P, FT, S])
        rate = s.sb("rate", [P, FT, S])
        kkn = s.sb("kkn", [P, FT, S])
        cum = s.sb("decay_sums", [P, FT, S])
        e1 = s.sb("e1", [P, FT, S])
        e2 = s.sb("e2", [P, FT, S])
        ones0 = s.sb("chunk_starts", [P, S])
        banks = [s.ps(f"lora_ps{i}") for i in range(8)]
        loaded = s.sem("lora_loaded")
        lora_in = s.sem("lora_in_ready")
        prod = s.sem("lora_product")
        act_st = s.sem("lora_act_stored")
        gate_st = s.sem("gate_stored")
        sq_r = s.sem("kk_squared")
        ss_r = s.sem("kk_summed")
        mx = s.sem("kk_sum_bounded")
        rs_l = s.sem("kk_log")
        rs_r = s.sem("kk_rstd")
        dv = s.sem("rwkv_vector_step")
        ex = s.sem("decay_exp_ready")
        bz = s.sem("bonus_summed")
        start = s.sem("chunk_starts_ready")
        names = {}
        kk_col = PARAM_AT["rw_k_k"]
        with nc.Block() as block:

            @block.sync
            def _(sp):
                sp.dma_start(wa2[0:64, :], A["rw_w2"][0]).then_inc(loaded, 16)
                sp.dma_start(wa2[64:128, :], A["rw_a2"][0]).then_inc(loaded, 16)
                sp.dma_start(g2[:, :], A["rw_g2"][0]).then_inc(loaded, 16)

            @block.gpsimd
            def _(pool):
                pool.memset(ones0[:, :], 1.0).then_inc(start, 1)
                pool.wait_ge(start, 1)
                pool.memset(ones0[:, 0:S:CH], 0.0).then_inc(start, 1)

            @block.vector
            def _(dve):
                n = [0]

                def step(name, ins):
                    n[0] += 1
                    names[name] = n[0]
                    ins.then_inc(dv, 1)
                    return n[0]

                for f in range(FT):
                    dve.wait_ge(ss_r, f + 1)
                    dve.tensor_scalar(e2[:, f, :], banks[f][:, :], 1e-24, None, ALU.max).then_inc(mx, 1)
                dve.wait_ge(start, 2)
                for f in range(FT):
                    dve.wait_ge(act_st, f + 1)
                    a = step("cum", dve.tensor_tensor_scan(cum[:, f, :], ones0[:, :], sig[:, f, :], 0.0, ALU.mult, ALU.add))
                dve.wait_ge(dv, a)
                cum3 = cum[:, :, :].rearrange("p f (c t) -> p (f c) t", t=CH)
                sig3 = sig[:, :, :].rearrange("p f (c t) -> p (f c) t", t=CH)
                a = step("ends", dve.tensor_copy(R["ends"][:, :], cum3[:, :, CH - 1]))
                dve.wait_ge(dv, a)
                ends = R["ends"][:, :].unsqueeze(2).to_broadcast([P, FT * NC, CH])
                a = step("csc", dve.scalar_tensor_tensor(out=cum3, in0=ends, scalar=-0.5, in1=cum3, op0=ALU.mult, op1=ALU.add))
                dve.wait_ge(dv, a)
                step("csx", dve.tensor_tensor(sig3, cum3, sig3, ALU.subtract))
                dve.wait_ge(rs_r, 1)
                for f in range(FT):
                    a = step("kkn", dve.scalar_tensor_tensor(out=kkn[:, f, :], in0=k[:, f, :], scalar=par_col(const, kk_col + f),
                                                             in1=e2[:, f, :], op0=ALU.mult, op1=ALU.mult))
                dve.wait_ge(act_st, 2 * FT)
                for f in range(FT):
                    b = step("fac", dve.tensor_scalar(e1[:, f, :], rate[:, f, :], par_col(const, PARAM_AT["rw_k_a"] + f),
                                                      const["one_minus_ka"][:, f:f + 1], ALU.mult, ALU.add))
                dve.wait_ge(dv, b)
                a = step("k2", dve.tensor_tensor(k, k, e1[:, :, :], ALU.mult))
                a = step("b", dve.tensor_tensor(rate[:, :, :], kkn[:, :, :], rate[:, :, :], ALU.mult))
                dve.wait_ge(dv, a)
                names["kkn"] = a
                c4 = lambda x: x.rearrange("p f (c t) -> p (f c) t", t=CH)
                KR = R["kr"]
                dve.wait_ge(ex, 1)
                step("krk", dve.tensor_tensor(KR[:, :, 0, :], c4(kkn[:, :, :]), sig3, ALU.mult))
                dve.wait_ge(ex, 3)
                step("krr", dve.tensor_tensor(KR[:, :, 1, :], c4(r), c4(e1[:, :, :]), ALU.mult))
                step("bh", dve.tensor_tensor(R["bh"][:, :, :], rate[:, :, :], e2[:, :, :], ALU.mult))
                a = step("kh", dve.tensor_tensor(R["kh"][:, :, :], k, e2[:, :, :], ALU.mult))
                dve.wait_ge(dv, a)
                for f in range(FT):
                    step("rk", dve.scalar_tensor_tensor(out=rate[:, f, :], in0=r[:, f, :], scalar=par_col(const, PARAM_AT["rw_r_k"] + f),
                                                        in1=k[:, f, :], op0=ALU.mult, op1=ALU.mult))
                for f in range(FT):
                    dve.wait_ge(bz, f + 1)
                    step("bonus", dve.tensor_tensor(R["bonus"][:, f, :], banks[f][:, :], vv[:, f, :], ALU.mult))

            @block.tensor
            def _(pe):
                pe.wait_ge(sq_r, FT)
                for f in range(FT):
                    pe.matmul(banks[f][:, :], const["heads"][:, :], e1[:, f, :], start=True, stop=True).then_inc(ss_r, 1)
                pe.wait_ge(loaded, 48)
                pe.wait_ge(lora_in, 3)
                for f in range(FT):
                    cols = slice(f * P, (f + 1) * P)
                    pe.matmul(banks[4 + f][:, :], wa2[0:64, cols], lora[0:64, 0, :], start=True, stop=True).then_inc(prod, 1)
                for f in range(FT):
                    cols = slice(f * P, (f + 1) * P)
                    pe.wait_ge(mx, f + 1)
                    pe.matmul(banks[f][:, :], wa2[64:128, cols], lora[64:128, 0, :], start=True, stop=True).then_inc(prod, 1)
                for f in range(FT):
                    cols = slice(f * P, (f + 1) * P)
                    pe.wait_ge(act_st, f + 1)
                    pe.matmul(banks[4 + f][:, :], g2[:, cols], lora[:, 1, :], start=True, stop=True).then_inc(prod, 1)
                pe.wait_ge(dv, names["rk"])
                for f in range(FT):
                    pe.wait_ge(act_st, 4 + f + 1)
                    pe.matmul(banks[f][:, :], const["heads"][:, :], rate[:, f, :], start=True, stop=True).then_inc(bz, 1)

            @block.scalar
            def _(act):
                for f in range(FT):
                    act.activation(e1[:, f, :], k[:, f, :], ACT.Square, scale=par_col(const, kk_col + f)).then_inc(sq_r, 1)
                act.activation(lora[0:64, 0, :], um[0:64, 3 * FT, :], ACT.Tanh).then_inc(lora_in, 1)
                act.activation(lora[64:128, 0, :], um[64:128, 3 * FT, :], ACT.Copy).then_inc(lora_in, 1)
                act.activation(lora[:, 1, :], um[:, 3 * FT + 1, :], ACT.Sigmoid).then_inc(lora_in, 1)
                for f in range(FT):
                    act.wait_ge(prod, f + 1)
                    act.activation(sig[:, f, :], banks[4 + f][:, :], ACT.Sigmoid,
                                   bias=par_col(const, PARAM_AT["rw_w0"] + f)).then_inc(act_st, 1)
                for f in range(FT):
                    act.wait_ge(prod, 4 + f + 1)
                    act.activation(rate[:, f, :], banks[f][:, :], ACT.Sigmoid,
                                   bias=par_col(const, PARAM_AT["rw_a0"] + f)).then_inc(act_st, 1)
                act.preload_act_table_set("natural_log_exp_and_others")
                act.wait_ge(mx, FT)
                act.activation(e2[:, :, :], e2[:, :, :], ACT.Ln, scale=float(2.0 ** LOG_BITS)).then_inc(rs_l, 1)
                act.wait_ge(rs_l, 1)
                act.activation(e2[:, :, :], e2[:, :, :], ACT.Exp, scale=-0.5, bias=const["log_shift"][:, :]).then_inc(rs_r, 1)
                for f in range(FT):
                    act.wait_ge(prod, 8 + f + 1)
                    act.activation(R["gate"][:, f, :], banks[4 + f][:, :], ACT.Copy).then_inc(gate_st, 1)
                act.wait_ge(dv, names["csx"])
                act.activation(sig[:, :, :], sig[:, :, :], ACT.Exp, scale=-DECAY).then_inc(ex, 1)
                act.wait_ge(dv, names["kkn"])
                act.activation(e1[:, :, :], cum[:, :, :], ACT.Exp, scale=-DECAY).then_inc(ex, 1)
                act.activation(e2[:, :, :], cum[:, :, :], ACT.Exp, scale=DECAY).then_inc(ex, 1)
                act.activation(R["mid"][:, :], R["ends"][:, :], ACT.Exp, scale=-0.5 * DECAY).then_inc(ex, 1)


def rwkv_chunks(nc, const, um, R):
    LEVELS = 7
    G = 2 * NC
    vT = um[:, 2 * FT:3 * FT, :]
    with Scope(nc) as s:
        tok = s.sb("token_side", [P, 2, NC, 5, P])
        KK, BV, V, B, K = range(5)
        sc = s.sb("chunk_scores", [P, G, 4, CH])
        x = s.sb("inverse", [P, G, CH])
        xt = s.sb("inverse_t", [P, G, CH])
        u = s.sb("level_product", [P, G, CH])
        gh = s.sb("g_h", [P, G, 2, HD])
        s_bank = [s.ps(f"score_ps{i}") for i in range(2)]
        l_bank = [[s.ps(f"level_ps{q}{i}") for i in range(2)] for q in range(2)]
        f_bank = [s.ps(f"final_ps{i}") for i in range(2)]
        kk_st = s.sem("kk_tokens_stored")
        tok_ready, tok_st = s.sem("tokens_turned"), s.sem("tokens_stored")
        sc_ready, sc_st = s.sem("scores_ready"), s.sem("scores_stored")
        bv_ready, bv_st = s.sem("bv_ready"), s.sem("bv_stored")
        u_ready, u_st = s.sems("u_ready", 2), s.sems("u_stored", 2)
        xu_ready, ux_ready = s.sems("xu_ready", 2), s.sems("ux_ready", 2)
        x_st, xt_st = s.sems("x_stored", 2), s.sems("xt_stored", 2)
        gh_ready, gh_st = s.sem("gh_ready"), s.sem("gh_stored")
        qo_ready, mn_ready = s.sem("q_o_ready"), s.sem("m_n_ready")
        q_st, o_st, mn_st = s.sem("q_stored"), s.sem("o_stored"), s.sem("m_n_stored")
        ident = const["ident"][:, :]
        with nc.Block() as block:

            @block.tensor
            def _(pe):
                for f in range(FT):
                    t = tok[:, f % 2]
                    for c in range(NC):
                        i = NC * f + c
                        bank = f_bank[c % 2]
                        if c >= 2:
                            pe.wait_ge(tok_st, i - 1)
                        elif f:
                            pe.wait_ge(gh_st, 2 * f)
                            pe.wait_ge(q_st, 2 * f)
                            pe.wait_ge(o_st, 2 * f)
                        cs = slice(c * CH, (c + 1) * CH)
                        for j, src in enumerate((R["kr"][:, i, 0, :], vT[:, f, cs], R["bh"][:, f, cs], R["kh"][:, f, cs])):
                            m = pe.transpose(bank[:, j * P:(j + 1) * P], src, ident)
                        m.then_inc(tok_ready, 1)
                    if f:
                        pe.wait_ge(bv_st, f)
                        pe.wait_ge(mn_st, 2 * f)
                    for g in range(G):
                        c, b = g // 2, HD * (g % 2)
                        i = G * f + g
                        if g >= 2:
                            pe.wait_ge(sc_st, i - 1)
                        cs = slice(c * CH, (c + 1) * CH)
                        kr = R["kr"][b:b + HD, NC * f + c, :, :]
                        pe.matmul(s_bank[g % 2][:, 0:2 * CH], R["bh"][b:b + HD, f, cs], kr, start=True, stop=True)
                        pe.matmul(s_bank[g % 2][:, 2 * CH:4 * CH], R["kh"][b:b + HD, f, cs], kr, start=True, stop=True).then_inc(sc_ready, 1)
                    pe.wait_ge(sc_st, G * (f + 1))
                    pe.wait_ge(kk_st, NC * (f + 1))
                    pe.wait_ge(tok_st, NC * (f + 1))
                    for g in range(G):
                        m = pe.matmul(s_bank[0][:, g * HD:(g + 1) * HD], sc[:, g, 2, :], t[:, g // 2, V, (g % 2) * HD:(g % 2 + 1) * HD],
                                      start=True, stop=True)
                    m.then_inc(bv_ready, 1)
                    for l in range(LEVELS):
                        for q in range(2):
                            if l:
                                pe.wait_ge(x_st[q], 6 * f + l)
                            for g in range(4 * q, 4 * q + 4):
                                cols = slice((g % 4) * CH, (g % 4 + 1) * CH)
                                m = pe.matmul(l_bank[q][0][:, cols], sc[:, g, 0, :], x[:, g, :] if l else ident, start=True, stop=True)
                            m.then_inc(u_ready[q], 1)
                        for q in range(2):
                            pe.wait_ge(u_st[q], LEVELS * f + l + 1)
                            if l:
                                pe.wait_ge(xt_st[q], LEVELS * f + l)
                            if 0 < l < LEVELS - 1:
                                for g in range(4 * q, 4 * q + 4):
                                    cols = slice((g % 4) * CH, (g % 4 + 1) * CH)
                                    m = pe.matmul(l_bank[q][0][:, cols], xt[:, g, :], u[:, g, :], start=True, stop=True)
                                m.then_inc(xu_ready[q], 1)
                            for g in range(4 * q, 4 * q + 4):
                                cols = slice((g % 4) * CH, (g % 4 + 1) * CH)
                                m = pe.matmul(l_bank[q][1][:, cols], u[:, g, :], xt[:, g, :] if l else ident, start=True, stop=True)
                            m.then_inc(ux_ready[q], 1)
                    for q in range(2):
                        pe.wait_ge(xt_st[q], LEVELS * (f + 1))
                        pe.wait_ge(bv_st, f + 1)
                        if q:
                            pe.wait_ge(gh_st, 2 * f + q)
                        for g in range(4 * q, 4 * q + 4):
                            b = HD * (g % 2)
                            m = pe.matmul(f_bank[0][:, (g % 4) * P:(g % 4 + 1) * P], xt[:, g, :], t[:, g // 2, KK:BV + 1, b:b + HD],
                                          start=True, stop=True)
                        m.then_inc(gh_ready, 1)
                        pe.wait_ge(gh_st, 2 * f + q + 1)
                        if q:
                            pe.wait_ge(q_st, 2 * f + q)
                            pe.wait_ge(o_st, 2 * f + q)
                            pe.wait_ge(mn_st, 2 * f + q)
                        for g in range(4 * q, 4 * q + 4):
                            c, b = g // 2, HD * (g % 2)
                            qo = f_bank[1][b:b + HD, (c % 2) * 2 * CH:(c % 2 + 1) * 2 * CH]
                            pe.matmul(qo[:, 0:CH], gh[:, g, 0, :], sc[:, g, 1, :], start=True, stop=True)
                            pe.matmul(qo[:, CH:2 * CH], gh[:, g, 1, :], sc[:, g, 1, :], start=True, stop=False)
                            m = pe.matmul(qo[:, CH:2 * CH], t[:, c, V, b:b + HD], sc[:, g, 3, :], start=False, stop=True)
                        m.then_inc(qo_ready, 1)
                        for g in range(4 * q, 4 * q + 4):
                            c, b = g // 2, HD * (g % 2)
                            mn = s_bank[1][b:b + HD, (c % 2) * 2 * HD:(c % 2 + 1) * 2 * HD]
                            pe.matmul(mn[:, 0:HD], gh[:, g, 0, :], t[:, c, B, b:b + HD], start=True, stop=True)
                            pe.matmul(mn[:, HD:2 * HD], t[:, c, B, b:b + HD], gh[:, g, 1, :], start=True, stop=False)
                            m = pe.matmul(mn[:, HD:2 * HD], t[:, c, K, b:b + HD], t[:, c, V, b:b + HD], start=False, stop=True)
                        m.then_inc(mn_ready, 1)

            @block.scalar
            def _(act):
                for f in range(FT):
                    for c in range(NC):
                        i = NC * f + c
                        act.wait_ge(tok_ready, i + 1)
                        bank = f_bank[c % 2][:, :].rearrange("p (j n) -> p j n", j=4)
                        act.activation(tok[:, f % 2, c, KK, :], bank[:, 0, :], ACT.Copy).then_inc(kk_st, 1)
                        act.activation(tok[:, f % 2, c, V:K + 1, :], bank[:, 1:4, :], ACT.Copy).then_inc(tok_st, 1)
                    act.wait_ge(bv_ready, f + 1)
                    act.activation(tok[:, f % 2, :, BV, :], s_bank[0][:, :].rearrange("p (c n) -> p c n", c=NC), ACT.Copy).then_inc(bv_st, 1)
                    for q in range(2):
                        act.wait_ge(gh_ready, 2 * f + q + 1)
                        act.activation(gh[:, 4 * q:4 * q + 4, :, :].rearrange("p g k n -> p (g k n)"), f_bank[0][:, :], ACT.Copy,
                                       scale=-1.0).then_inc(gh_st, 1)
                        act.wait_ge(q_st, 2 * f + q + 1)
                        qo = f_bank[1][:, :].rearrange("p (c k t) -> p c k t", c=2, k=2)
                        act.activation(R["o"][:, f, 2 * q * CH:2 * (q + 1) * CH].rearrange("p (c t) -> p c t", c=2), qo[:, :, 1, :],
                                       ACT.Copy).then_inc(o_st, 1)
                        act.wait_ge(mn_ready, 2 * f + q + 1)
                        i = NC * f + 2 * q
                        act.activation(R["mn"][:, i:i + 2, :, :].rearrange("p c k n -> p (c k n)"), s_bank[1][:, 0:4 * HD], ACT.Copy).then_inc(mn_st, 1)

            @block.vector
            def _(dve):
                for f in range(FT):
                    if f:
                        dve.wait_ge(mn_ready, 2 * f)
                        dve.wait_ge(qo_ready, 2 * f)
                    for g in range(G):
                        dve.wait_ge(sc_ready, G * f + g + 1)
                        dve.tensor_tensor(sc[:, g, :, :].rearrange("p k t -> p (k t)"), s_bank[g % 2][:, :],
                                          const["causal"][:, :, :].rearrange("p k t -> p (k t)"), ALU.mult).then_inc(sc_st, 1)
                    ids = const["ident"][:, :].unsqueeze(1).to_broadcast([P, 4, CH])
                    for l in range(LEVELS):
                        lv = const["level"][:, l, :].unsqueeze(1).to_broadcast([P, 4, CH])
                        for q in range(2):
                            gs = slice(4 * q, 4 * q + 4)
                            bank = [l_bank[q][j][:, :].rearrange("p (g t) -> p g t", g=4) for j in range(2)]
                            dve.wait_ge(u_ready[q], LEVELS * f + l + 1)
                            if l:
                                dve.wait_ge(ux_ready[q], LEVELS * f + l)
                            dve.tensor_tensor(u[:, gs, :], bank[0], lv, ALU.mult).then_inc(u_st[q], 1)
                        for q in range(2):
                            gs = slice(4 * q, 4 * q + 4)
                            bank = [l_bank[q][j][:, :].rearrange("p (g t) -> p g t", g=4) for j in range(2)]
                            if l == 0:
                                dve.wait_ge(u_st[q], LEVELS * f + 1)
                                dve.tensor_tensor(x[:, gs, :], ids, u[:, gs, :], ALU.subtract).then_inc(x_st[q], 1)
                            elif l < LEVELS - 1:
                                dve.wait_ge(xu_ready[q], 5 * f + l)
                                dve.tensor_tensor(x[:, gs, :], x[:, gs, :], bank[0], ALU.subtract).then_inc(x_st[q], 1)
                            dve.wait_ge(ux_ready[q], LEVELS * f + l + 1)
                            dve.tensor_tensor(xt[:, gs, :], xt[:, gs, :] if l else ids, bank[1], ALU.subtract).then_inc(xt_st[q], 1)
                    for q in range(2):
                        dve.wait_ge(qo_ready, 2 * f + q + 1)
                        qo = f_bank[1][:, :].rearrange("p (c k t) -> p c k t", c=2, k=2)
                        i = NC * f + 2 * q
                        dve.tensor_tensor(R["q"][:, f, 2 * q * CH:2 * (q + 1) * CH].rearrange("p (c t) -> p c t", c=2), qo[:, :, 0, :],
                                          R["kr"][:, i:i + 2, 1, :], ALU.add).then_inc(q_st, 1)


def rwkv_output(nc, const, R, mixT):
    with Scope(nc) as s:
        st = s.sb("chunk_state", [P, NC, FT, HD])
        z = s.sb("state_sum", [P, FT, HD])
        mm = s.sb("mid_products", [P, FT, NC])
        xc = s.sb("centred", [P, 2, S])
        sq = s.sb("centred_sq", [P, 2, S])
        rs = s.sb("group_rstd", [P, 2, S])
        z_bank = s.ps("state_ps")
        o_bank = [s.ps(f"out_ps{i}") for i in range(2)]
        m_bank = [s.ps(f"mean_ps{i}") for i in range(2)]
        v_bank = [s.ps(f"var_ps{i}") for i in range(2)]
        step_ready = s.sem("state_product_ready")
        zs = s.sem("state_step")
        o_ready, o_st = s.sem("out_ready"), s.sem("out_stored")
        mean, cent, sqd, var, lg, rstd, fin = (s.sem("group_" + n) for n in ("mean", "centred", "squared", "var", "log", "rstd", "done"))
        mid = R["mid"][:, :].rearrange("p (f c) -> p f c", c=NC)
        mn = R["mn"][:, :, :, :].rearrange("p (f c) k n -> p f c k n", c=NC)
        with nc.Block() as block:

            @block.tensor
            def _(pe):
                for c in range(1, NC - 1):
                    pe.wait_ge(zs, 1 + 3 * (c - 1) + 1)
                    for f in range(FT):
                        for b in (0, HD):
                            m = pe.matmul(z_bank[b:b + HD, f * HD:(f + 1) * HD], R["mn"][b:b + HD, f * NC + c, 0, :],
                                          st[b:b + HD, c, f, :], start=True, stop=True)
                    m.then_inc(step_ready, 1)
                pe.wait_ge(zs, 1 + 3 * (NC - 2) + 1)
                for j in range(FT + 2):
                    if j < FT:
                        if j >= 2:
                            pe.wait_ge(o_st, j - 1)
                        for c in range(1, NC):
                            for b in (0, HD):
                                m = pe.matmul(o_bank[j % 2][b:b + HD, c * CH:(c + 1) * CH], st[b:b + HD, c, j, :],
                                              R["q"][b:b + HD, j, c * CH:(c + 1) * CH], start=True, stop=True)
                        m.then_inc(o_ready, 1)
                    if 0 <= j - 1 < FT:
                        i = j - 1
                        pe.wait_ge(o_st, i + 1)
                        if i >= 2:
                            pe.wait_ge(cent, i - 1)
                        pe.matmul(m_bank[i % 2][:, :], const["heads"][:, :], R["o"][:, i, :], start=True, stop=True).then_inc(mean, 1)
                    if 0 <= j - 2 < FT:
                        i = j - 2
                        pe.wait_ge(sqd, i + 1)
                        if i >= 2:
                            pe.wait_ge(lg, i - 1)
                        pe.matmul(v_bank[i % 2][:, :], const["heads"][:, :], sq[:, i % 2, :], start=True, stop=True).then_inc(var, 1)

            @block.vector
            def _(dve):
                def bc(f3):
                    return f3.unsqueeze(2).to_broadcast([P, FT, HD])

                dve.tensor_tensor(mm[:, :, 0:NC - 1], mid[:, :, 0:NC - 1], mid[:, :, 1:NC], ALU.mult).then_inc(zs, 1)
                dve.wait_ge(zs, 1)
                dve.tensor_tensor(st[:, 1, :, :], mn[:, :, 0, 1, :], bc(mm[:, :, 0]), ALU.mult).then_inc(zs, 1)
                n = 2
                for c in range(1, NC - 1):
                    dve.wait_ge(zs, n)
                    dve.wait_ge(step_ready, c)
                    dve.tensor_tensor(z[:, :, :], z_bank[:, 0:FT * HD].rearrange("p (f n) -> p f n", f=FT), st[:, c, :, :], ALU.add).then_inc(zs, 1)
                    dve.wait_ge(zs, n + 1)
                    dve.tensor_tensor(z[:, :, :], z[:, :, :], mn[:, :, c, 1, :], ALU.add).then_inc(zs, 1)
                    dve.wait_ge(zs, n + 2)
                    dve.tensor_tensor(st[:, c + 1, :, :], z[:, :, :], bc(mm[:, :, c]), ALU.mult).then_inc(zs, 1)
                    n += 3
                w, bcol = PARAM_AT["rw_ln_w"], PARAM_AT["rw_ln_b"]
                for j in range(FT + 2):
                    if j < FT:
                        dve.wait_ge(o_ready, j + 1)
                        o = R["o"][:, j, CH:S]
                        dve.tensor_tensor(o, o_bank[j % 2][:, CH:S], o, ALU.add).then_inc(o_st, 1)
                    if 0 <= j - 1 < FT:
                        i = j - 1
                        dve.wait_ge(mean, i + 1)
                        if i >= 2:
                            dve.wait_ge(fin, 3 * (i - 1))
                            dve.wait_ge(sqd, i - 1)
                        dve.scalar_tensor_tensor(out=xc[:, i % 2, :], in0=m_bank[i % 2][:, :], scalar=-1.0 / HD,
                                                 in1=R["o"][:, i, :], op0=ALU.mult, op1=ALU.add).then_inc(cent, 1)
                    if 0 <= j - 2 < FT:
                        i = j - 2
                        dve.wait_ge(rstd, i + 1)
                        dve.wait_ge(cent, i + 1)
                        y = xc[:, i % 2, :]
                        dve.scalar_tensor_tensor(out=y, in0=y, scalar=par_col(const, w + i), in1=rs[:, i % 2, :],
                                                 op0=ALU.mult, op1=ALU.mult).then_inc(fin, 1)
                        dve.wait_ge(fin, 3 * i + 1)
                        dve.scalar_tensor_tensor(out=y, in0=y, scalar=par_col(const, bcol + i), in1=R["bonus"][:, i, :],
                                                 op0=ALU.add, op1=ALU.add).then_inc(fin, 1)
                        dve.wait_ge(fin, 3 * i + 2)
                        dve.tensor_tensor(mixT[:, FT + i, :], y, R["gate"][:, i, :], ALU.mult).then_inc(fin, 1)

            @block.scalar
            def _(act):
                act.preload_act_table_set("natural_log_exp_and_others")
                for i in range(FT):
                    act.wait_ge(cent, i + 1)
                    if i >= 2:
                        act.wait_ge(var, i - 1)
                    act.activation(sq[:, i % 2, :], xc[:, i % 2, :], ACT.Square).then_inc(sqd, 1)
                    act.wait_ge(var, i + 1)
                    if i >= 2:
                        act.wait_ge(fin, 3 * (i - 2) + 1)
                    act.activation(rs[:, i % 2, :], v_bank[i % 2][:, :], ACT.Ln, scale=1.0 / HD, bias=const["gn_eps"][:, :]).then_inc(lg, 1)
                    act.wait_ge(lg, i + 1)
                    act.activation(rs[:, i % 2, :], rs[:, i % 2, :], ACT.Exp, scale=-0.5).then_inc(rstd, 1)


def out_projection(nc, const, w, xT, n_in, h, tag, out=None):
    HALF = D // 2
    with Scope(nc) as s:
        wt = s.sb(tag + "_w", [P, 2, n_in, HALF])
        banks = [s.ps(f"{tag}_ps{i}") for i in range(4)]
        loaded = s.sems(tag + "_loaded", 2)
        ready = s.sem(tag + "_ready")
        added = s.sem(tag + "_added")
        stored = s.sem(tag + "_stored")
        wv = w.rearrange("l (k p) n -> p (l k) n", p=P)
        with nc.Block() as block:

            @block.sync
            def _(sp):
                for half in range(2):
                    sp.dma_start(wt[:, half, :, :], wv[:, :, half * HALF:(half + 1) * HALF]).then_inc(loaded[half], 16)
                if out is not None:
                    for half in range(2):
                        for c in range(TT):
                            sp.wait_ge(added, TT * half + c + 1)
                            cols = slice(half * HALF, (half + 1) * HALF)
                            sp.dma_start(out[c * P:(c + 1) * P, cols], h[:, c, cols]).then_inc(stored, 16)
                    sp.wait_ge(stored, 16 * 2 * TT)

            @block.tensor
            def _(pe):
                for half in range(2):
                    pe.wait_ge(loaded[half], 16)
                    for c in range(TT):
                        i = TT * half + c
                        if i >= 4:
                            pe.wait_ge(added, i - 3)
                        for k in range(n_in):
                            m = pe.matmul(banks[i % 4][:, :], xT[:, k, c * P:(c + 1) * P], wt[:, half, k, :],
                                          start=(k == 0), stop=(k == n_in - 1))
                        m.then_inc(ready, 1)

            @block.vector
            def _(dve):
                for half in range(2):
                    for c in range(TT):
                        i = TT * half + c
                        dve.wait_ge(ready, i + 1)
                        dst = h[:, c, half * HALF:(half + 1) * HALF]
                        dve.tensor_tensor(dst, banks[i % 4][:, :], dst, ALU.add).then_inc(added, 1)


def route(nc, A, const, h, xn_dram, list_dram, M):
    NL = NG + NE
    MADE = 10
    with Scope(nc) as s:
        sq = s.sb("ffn_sq", [P, D])
        ss = s.sb("ffn_ss", [P, TT])
        rs = s.sb("ffn_rstd", [P, TT])
        xg = s.sb("ffn_in", [P, TT, D])
        xT = s.sb("ffn_in_t", [P, KC, S])
        wr = s.sb("router_w", [P, KC, NL])
        br = s.sb("router_b", [P, NL])
        lg = s.sb("router_logits", [P, TT, NL])
        desc = s.sb("descending", [P, EPG])
        base = s.sb("list_base", [P, NE])
        steps = s.sb("round_limits", [P, S // CAP])
        ids = s.sb("token_ids", [P, 2, TT, 2], I32)
        empty = s.sb("empty_list", [P, LIST // P, 2], I32)
        t4 = s.sb("t4", [P, TT, NG])
        grp = s.sb("group_hot", [P, TT, NG])
        ex4 = s.sb("group_exp", [P, TT, NG])
        gm = s.sb("group_max", [P, TT])
        a1 = s.sb("a1", [P, TT])
        gval = s.sb("group_prob", [P, TT])
        pick = s.sb("picked", [P, TT, NG, EPG])
        sel = s.sb("selected", [P, TT, EPG])
        t8 = s.sb("t8", [P, TT, EPG])
        hot = [s.sb(f"expert_hot{i}", [P, TT, EPG]) for i in range(2)]
        top = [s.sb(f"expert_top{i}", [P, TT]) for i in range(2)]
        p2 = s.sb("second_exp", [P, TT])
        full = [s.sb(f"expert_full{i}", [P, TT, NG, EPG]) for i in range(2)]
        both = s.sb("expert_both", [P, TT, NE])
        nboth = s.sb("expert_both_neg", [P, TT, NE])
        places = s.sb("places", [P, 2, TT])
        reached = s.sb("rounds_reached", [P, 2 * TT, S // CAP])
        t32 = s.sb("t32", [P, TT, NE])
        slotf = s.sb("slots_float", [P, 2, TT])
        tot = s.sb("totals", [P, NE])
        most = s.sb("most", [P, 1])
        rf = s.sb("rounds_float", [P, 1])
        t_bank = [s.ps(f"ffn_ps{i}") for i in range(4)]
        l_bank = s.ps("logit_ps")
        r_bank = s.ps("rank_ps")
        squared, rstd, scaled = s.sem("ffn_squares"), s.sem("ffn_rstd_ready"), s.sem("ffn_scaled")
        turned, even_st, odd_st = s.sem("ffn_turned"), s.sem("ffn_even_stored"), s.sem("ffn_odd_stored")
        loaded, xn_st, zeroed, made = s.sem("router_loaded"), s.sem("ffn_in_stored"), s.sem("list_zeroed"), s.sem("router_constants")
        logits, ranks, dv, ac = s.sem("logits_ready"), s.sem("ranks_ready"), s.sem("route_step"), s.sem("route_exp")
        put = s.sem("ids_scattered")
        slots_ready = s.sem("slots_ready")
        with nc.Block() as block:

            @block.vector
            def _(dve):
                n = [0]

                def step(ins, name=None):
                    n[0] += 1
                    if name:
                        M[name] = n[0]
                    ins.then_inc(dv, 1)
                    dve.wait_ge(dv, n[0])

                def wide(x, k):
                    return x.unsqueeze(2).to_broadcast([P, TT, k])

                def row(x, k):
                    return x[:, 0:k].unsqueeze(1).to_broadcast([P, TT, k])

                def first_of_max(vals, best, tmp, hot_out, k):
                    step(dve.tensor_reduce(best, vals, AX_X, ALU.max))
                    step(dve.tensor_tensor(tmp, vals, wide(best, k), ALU.is_ge))
                    step(dve.tensor_tensor(tmp, tmp, row(desc, k), ALU.mult))
                    step(dve.tensor_reduce(a1[:, :], tmp, AX_X, ALU.max))
                    step(dve.tensor_tensor(hot_out, tmp, wide(a1[:, :], k), ALU.is_equal))

                dve.wait_ge(squared, TT)
                dve.tensor_scalar(ss[:, :], ss[:, :], 1.0 / D, EPS, ALU.mult, ALU.add).then_inc(rstd, 1)
                dve.wait_ge(rstd, 2)
                dve.reciprocal(rs[:, :], ss[:, :]).then_inc(rstd, 1)
                dve.wait_ge(rstd, 3)
                dve.wait_ge(const["row_params"], 32)
                for c in range(TT):
                    dve.scalar_tensor_tensor(out=xg[:, c, :], in0=h[:, c, :], scalar=rs[:, c:c + 1], in1=const["ffn_g"][:, :],
                                             op0=ALU.mult, op1=ALU.mult).then_inc(scaled, 1)
                for k in range(1, KC, 2):
                    dve.wait_ge(turned, k + 1)
                    dve.tensor_copy(xT[:, k, :], t_bank[k % 4][:, :]).then_inc(odd_st, 1)
                dve.wait_ge(logits, 1)
                dve.wait_ge(made, MADE)
                step(dve.tensor_tensor(lg[:, :, :], l_bank[:, 0:TT * NL].rearrange("p (c n) -> p c n", c=TT),
                                       br[:, :].unsqueeze(1).to_broadcast([P, TT, NL]), ALU.add))
                first_of_max(lg[:, :, 0:NG], gm[:, :], t4[:, :, :], grp[:, :, :], NG)
                step(dve.tensor_tensor(t4[:, :, :], lg[:, :, 0:NG], wide(gm[:, :], NG), ALU.subtract), "group_less")
                dve.wait_ge(ac, 1)
                step(dve.tensor_reduce(gval[:, :], ex4[:, :, :], AX_X, ALU.add))
                step(dve.reciprocal(gval[:, :], gval[:, :]))
                step(dve.tensor_tensor(pick[:, :, :, :], lg[:, :, NG:NL].rearrange("p c (g e) -> p c g e", g=NG),
                                       grp[:, :, :].unsqueeze(3).to_broadcast([P, TT, NG, EPG]), ALU.mult))
                step(dve.tensor_reduce(sel[:, :, :], pick[:, :, :, :].rearrange("p c g e -> p c e g"), AX_X, ALU.add))
                first_of_max(sel[:, :, :], top[0][:, :], t8[:, :, :], hot[0][:, :, :], EPG)
                step(dve.tensor_scalar(t8[:, :, :], hot[0][:, :, :], NEG, None, ALU.mult))
                step(dve.tensor_tensor(sel[:, :, :], sel[:, :, :], t8[:, :, :], ALU.add))
                first_of_max(sel[:, :, :], top[1][:, :], t8[:, :, :], hot[1][:, :, :], EPG)
                step(dve.tensor_tensor(p2[:, :], top[1][:, :], top[0][:, :], ALU.subtract), "top_less")
                for j in range(2):
                    step(dve.tensor_tensor(full[j][:, :, :, :], grp[:, :, :].unsqueeze(3).to_broadcast([P, TT, NG, EPG]),
                                           hot[j][:, :, :].unsqueeze(2).to_broadcast([P, TT, NG, EPG]), ALU.mult))
                flat = [full[j][:, :, :, :].rearrange("p c g e -> p c (g e)") for j in range(2)]
                step(dve.tensor_tensor(both[:, :, :], flat[0], flat[1], ALU.add))
                step(dve.tensor_scalar(nboth[:, :, :], both[:, :, :], -1.0, None, ALU.mult), "both")
                dve.wait_ge(ac, 2)
                step(dve.tensor_scalar(a1[:, :], p2[:, :], 1.0, None, ALU.add))
                step(dve.reciprocal(a1[:, :], a1[:, :]))
                step(dve.tensor_tensor(M["weights"][:, 0, :], gval[:, :], a1[:, :], ALU.mult))
                step(dve.tensor_tensor(M["weights"][:, 1, :], M["weights"][:, 0, :], p2[:, :], ALU.mult))
                dve.wait_ge(ranks, 1)
                rank = r_bank[:, 0:TT * NE].rearrange("p (c e) -> p c e", c=TT)
                for j in range(2):
                    step(dve.tensor_tensor(t32[:, :, :], rank, flat[j], ALU.mult))
                    step(dve.tensor_reduce(places[:, j, :], t32[:, :, :], AX_X, ALU.add))
                    step(dve.tensor_tensor(t32[:, :, :], base[:, :].unsqueeze(1).to_broadcast([P, TT, NE]), flat[j], ALU.mult))
                    step(dve.tensor_reduce(slotf[:, j, :], t32[:, :, :], AX_X, ALU.add))
                step(dve.tensor_tensor(slotf[:, :, :], slotf[:, :, :], places[:, :, :], ALU.add))
                pl = places[:, :, :].rearrange("p j c -> p (j c)")
                step(dve.tensor_tensor(reached[:, :, :], pl.unsqueeze(2).to_broadcast([P, 2 * TT, S // CAP]),
                                       steps[:, :].unsqueeze(1).to_broadcast([P, 2 * TT, S // CAP]), ALU.is_ge))
                step(dve.tensor_reduce(pl, reached[:, :, :], AX_X, ALU.add))
                step(dve.scalar_tensor_tensor(out=slotf[:, :, :].rearrange("p j c -> p (j c)"), in0=pl, scalar=float((NE - 1) * CAP),
                                              in1=slotf[:, :, :].rearrange("p j c -> p (j c)"), op0=ALU.mult, op1=ALU.add))
                step(dve.tensor_copy(tot[:, :], r_bank[:, TT * NE:(TT + 1) * NE]))
                step(dve.tensor_reduce(most[:, :], tot[:, :], AX_X, ALU.max))
                step(dve.tensor_scalar(steps[:, :], steps[:, :], most[:, 0:1], None, ALU.is_lt))
                step(dve.tensor_reduce(rf[:, :], steps[:, :], AX_X, ALU.add))
                step(dve.tensor_copy(M["rounds"][:, 0:1], rf[:, :]))
                dve.tensor_copy(M["slots"][:, :, :], slotf[:, :, :]).then_inc(slots_ready, 1)

            @block.sync
            def _(sp):
                sp.dma_start(wr[:, :, 0:NG], A["router_grp_w"].rearrange("l (k p) n -> p (l k) n", p=P)).then_inc(loaded, 16)
                sp.dma_start(wr[:, :, NG:NL], A["router_exp_w"].rearrange("l (k p) n -> p (l k) n", p=P)).then_inc(loaded, 16)
                sp.dma_start(br[:, 0:NG], A["router_grp_b"].broadcast_to([P, NG])).then_inc(loaded, 16)
                sp.dma_start(br[:, NG:NL], A["router_exp_b"].broadcast_to([P, NE])).then_inc(loaded, 16)
                for j in range(NB):
                    load_expert(sp, A, M, j, j)
                sp.wait_ge(made, MADE)
                sp.dma_start(list_dram.rearrange("(p n) a -> p (n a)", p=P),
                             empty[:, :, :].rearrange("p n a -> p (n a)")).then_inc(zeroed, 16)
                for c in range(TT):
                    sp.wait_ge(scaled, c + 1)
                    sp.dma_start(xn_dram[c * P:(c + 1) * P, :], xg[:, c, :]).then_inc(xn_st, 16)
                sp.wait_ge(xn_st, 16 * TT)

            @block.gpsimd
            def _(pool):
                pool.iota(desc[:, :], [[-1, EPG]], base=EPG, channel_multiplier=0, allow_small_or_imprecise_dtypes=True).then_inc(made, 1)
                pool.iota(base[:, :], [[CAP, NE]], base=-(NE - 1) * CAP, channel_multiplier=0, allow_small_or_imprecise_dtypes=True).then_inc(made, 1)
                pool.iota(steps[:, :], [[CAP, S // CAP]], base=0, channel_multiplier=0, allow_small_or_imprecise_dtypes=True).then_inc(made, 1)
                for j in range(2):
                    pool.iota(ids[:, j, :, 0], [[P, TT]], base=0, channel_multiplier=1).then_inc(made, 1)
                    pool.iota(ids[:, j, :, 1], [[2 * P, TT]], base=j, channel_multiplier=2).then_inc(made, 1)
                pool.memset(empty[:, :, 0], 0).then_inc(made, 1)
                pool.iota(empty[:, :, 1], [[1, LIST // P]], base=2 * S, channel_multiplier=LIST // P).then_inc(made, 1)
                pool.memset(M["rounds"][:, :], 0).then_inc(made, 1)
                pool.wait_ge(zeroed, 16)
                pool.wait_ge(made, MADE)
                pool.wait_ge(slots_ready, 1)
                for j in range(2):
                    for c in range(TT):
                        pool.indirect_dma_start(out=list_dram, out_offset=bass.IndirectOffsetOnAxis(ap=M["slots"][:, j, c:c + 1], axis=0),
                                                in_=ids[:, j, c, :], in_offset=None).then_inc(put, 16)
                pool.wait_ge(put, 16 * 2 * TT)

            @block.scalar
            def _(act):
                for c in range(TT):
                    if c:
                        act.wait_ge(squared, c)
                    act.activation(sq[:, :], h[:, c, :], ACT.Square, accum_out=ss[:, c:c + 1]).then_inc(squared, 1)
                act.wait_ge(rstd, 1)
                act.activation(ss[:, :], ss[:, :], ACT.Sqrt).then_inc(rstd, 1)
                act.preload_act_table(ACT.Exp)
                for k in range(0, KC, 2):
                    act.wait_ge(turned, k + 1)
                    act.activation(xT[:, k, :], t_bank[k % 4][:, :], ACT.Copy).then_inc(even_st, 1)
                act.wait_ge(dv, M["group_less"])
                act.activation(ex4[:, :, :], t4[:, :, :], ACT.Exp).then_inc(ac, 1)
                act.wait_ge(dv, M["top_less"])
                act.activation(p2[:, :], p2[:, :], ACT.Exp).then_inc(ac, 1)

            @block.tensor
            def _(pe):
                for k in range(KC):
                    if k >= 4:
                        pe.wait_ge((even_st, odd_st)[k % 2], (k - 4) // 2 + 1)
                    for c in range(TT):
                        pe.wait_ge(scaled, c + 1)
                        t = pe.transpose(t_bank[k % 4][:, c * P:(c + 1) * P], xg[:, c, k * P:(k + 1) * P], const["ident"][:, :])
                    t.then_inc(turned, 1)
                pe.wait_ge(loaded, 64)
                pe.wait_ge(even_st, KC // 2)
                pe.wait_ge(odd_st, KC // 2)
                for c in range(TT):
                    for k in range(KC):
                        m = pe.matmul(l_bank[:, c * NL:(c + 1) * NL], xT[:, k, c * P:(c + 1) * P], wr[:, k, :],
                                      start=(k == 0), stop=(k == KC - 1))
                m.then_inc(logits, 1)
                pe.wait_ge(dv, M["both"])
                for c in range(TT + 1):
                    for b in range(min(c, TT - 1) + 1 if c < TT else TT):
                        same = b == c
                        m = pe.matmul(r_bank[:, c * NE:(c + 1) * NE], (const["causal"][:, 0, :] if same else const["minus_ones"][:, :]),
                                      (both if same else nboth)[:, b, :], start=(b == 0), stop=(b == min(c, TT - 1)))
                m.then_inc(ranks, 1)



def load_expert(sp, A, M, j, e):
    for name, slot in (("exp_w_gate", M["gate"][j]), ("exp_w_up", M["up"][j]), ("exp_w_down", M["down"][j])):
        w = A[name].rearrange("l e (k p) n -> p (l e) k n", p=P)
        sp.dma_start(slot[:, :, :], w[:, bass.ds(e, 1), :, :].rearrange("p a k n -> p (a k) n")).then_inc(M["weights_in"][j], 16)


def experts(nc, A, const, xn_dram, list_dram, y_dram, M):
    with Scope(nc) as s:
        wg, wu, wd, w_in = M["gate"], M["up"], M["down"], M["weights_in"]
        idx = [s.sb(f"list_places{i}", [CAP, 2], I32) for i in range(UNROLL)]
        xg = [s.sb(f"gathered{j}", [CAP, D]) for j in range(NB)]
        xT = [s.sb(f"gathered_t{j}", [P, KC, CAP]) for j in range(2)]
        act_g = [s.sb(f"silu{j}", [P, DE]) for j in range(2)]
        hid_t = [s.sb(f"hidden_t{j}", [P, DE]) for j in range(2)]
        hid = [s.sb(f"hidden{j}", [P, FC, CAP]) for j in range(2)]
        y = [s.sb(f"expert_out{j}", [CAP, D]) for j in range(NB)]
        t_bank = [s.ps(f"gathered_ps{j}") for j in range(2)]
        g_bank = [s.ps(f"hidden_ps{j}") for j in range(2)]
        h_bank = [s.ps(f"hidden_turned_ps{j}") for j in range(2)]
        y_bank = [s.ps(f"expert_ps{j}") for j in range(2)]
        idx_in = s.sems("index_loaded", UNROLL)
        x_in = s.sems("tokens_gathered", NB)
        turned = s.sems("gathered_turned", NB)
        t_st = s.sems("gathered_stored", NB)
        gu = s.sems("gate_up_ready", NB)
        silu = s.sems("silu_ready", NB)
        mul_r = s.sems("hidden_multiplied", NB)
        h_turned = s.sems("hidden_turned", NB)
        hid_r = s.sems("hidden_ready", NB)
        y_r = s.sems("expert_ready", NB)
        y_lo, y_hi = s.sems("expert_low_stored", NB), s.sems("expert_high_stored", NB)
        y_out = s.sems("expert_written", NB)
        spare, seen, seen_sp, seen_pe = s.sem("spare_rows_ready"), s.sem("waits_seen"), s.sem("slots_seen"), s.sem("gathers_seen")
        TURNS = NE // UNROLL
        lists = list_dram.rearrange("(l c) a -> c l a", c=CAP)

        def use(i, n):
            return i % NB, n * (UNROLL // NB) + i // NB

        def turns(eng):
            rounds = eng.value_load(M["rounds"][0:1, 0:1], min_val=1, max_val=S // CAP)
            with eng.Fori(0, rounds) as rnd, eng.Fori(0, TURNS) as t:
                yield rnd, t, rnd * TURNS + t

        with nc.Block() as block:

            @block.sync
            def _(sp):
                rounds = sp.value_load(M["rounds"][0:1, 0:1], min_val=1, max_val=S // CAP)
                with sp.Fori(0, rounds) as rnd:
                    first = rnd * TURNS
                    with sp.Fori(0, TURNS - 1) as t:
                        for i in range(UNROLL):
                            j, m = use(i, first + t)
                            sp.wait_ge(y_r[j], m + 2)
                            load_expert(sp, A, M, j, t * UNROLL + i + NB)
                    for i in range(UNROLL):
                        j, m = use(i, first + TURNS - 1)
                        sp.wait_ge(y_r[j], m + 2)
                        if i < NB:
                            load_expert(sp, A, M, j, NE - NB + i)
                    sp.sem_inc(seen_sp)
                    with sp.If(rnd + 1 < rounds):
                        for j in range(NB):
                            load_expert(sp, A, M, j, j)

            @block.gpsimd
            def _(pool):
                for j in range(NB):
                    pool.iota(idx[NB + j][:, :], [[0, 2]], base=2 * S + LIST + j * CAP, channel_multiplier=1).then_inc(spare, 1)
                    pool.memset(y[j][:, :], 0.0).then_inc(spare, 1)

                def write_rows(i, j, m):
                    pool.wait_ge(y_lo[j], m + 1)
                    pool.wait_ge(y_hi[j], m + 1)
                    pool.sem_inc(seen)
                    pool.indirect_dma_start(out=y_dram, out_offset=bass.IndirectOffsetOnAxis(ap=idx[i][:, 1:2], axis=0),
                                            in_=y[j][:, :], in_offset=None).then_inc(y_out[j], 16)

                pool.wait_ge(spare, 2 * NB)
                for rnd, t, n in turns(pool):
                    for i in range(UNROLL):
                        j, m = use(i, n)
                        pool.wait_ge(idx_in[i], n * 16 + 16)
                        pool.sem_inc(seen)
                        pool.indirect_dma_start(out=xg[j][:, :], out_offset=None, in_=xn_dram,
                                                in_offset=bass.IndirectOffsetOnAxis(ap=idx[i][:, 0:1], axis=0)).then_inc(x_in[j], 16)
                        write_rows((i + NB) % UNROLL, j, m)
                total = pool.value_load(M["rounds"][0:1, 0:1], min_val=1, max_val=S // CAP) * (NE // NB)
                for j in range(NB):
                    write_rows(NB + j, j, total)
                for j in range(NB):
                    pool.wait_ge(y_out[j], total * 16 + 16)
                    pool.wait_ge(idx_in[j], total // (UNROLL // NB) * 16 + 16)
                pool.sem_inc(seen)

            @block.tensor
            def _(pe):
                for j in range(NB):
                    pe.sem_inc(y_r[j])

                def turn_tokens(i, n):
                    j, m = use(i, n)
                    pe.wait_ge(x_in[j], m * 16 + 16)
                    pe.sem_inc(seen_pe)
                    for k in range(KC):
                        x = pe.transpose(t_bank[i % 2][:, k * CAP:(k + 1) * CAP], xg[j][:, k * P:(k + 1) * P], const["ident"][0:CAP, 0:CAP])
                    x.then_inc(turned[j], 1)

                def gate_and_up(i, n):
                    j, m = use(i, n)
                    pe.wait_ge(w_in[j], m * 48 + 48)
                    pe.wait_ge(t_st[j], m + 1)
                    for k in range(KC):
                        for a, w in enumerate((wg[j], wu[j])):
                            x = pe.matmul(g_bank[i % 2][a * CAP:(a + 1) * CAP, 0:DE], xT[i % 2][:, k, :], w[:, k, :],
                                          start=(k == 0), stop=(k == KC - 1))
                    x.then_inc(gu[j], 1)

                def turn_hidden(i, n):
                    j, m = use(i, n)
                    pe.wait_ge(mul_r[j], m + 1)
                    pe.sem_inc(seen_pe)
                    for f in range(FC):
                        x = pe.transpose(h_bank[i % 2][:, f * CAP:(f + 1) * CAP], hid_t[i % 2][CAP:P, f * P:(f + 1) * P], const["ident"][CAP:P, CAP:P])
                    x.then_inc(h_turned[j], 1)

                def down(i, n):
                    j, m = use(i, n)
                    pe.wait_ge(hid_r[j], m + 1)
                    j2, m2 = use(i - 2, n)
                    pe.wait_ge(y_lo[j2], m2 + 2)
                    pe.wait_ge(y_hi[j2], m2 + 2)
                    for f in range(FC):
                        for half in range(2):
                            x = pe.matmul(y_bank[i % 2][half * CAP:(half + 1) * CAP, :], hid[i % 2][:, f, :], wd[j][:, f, half * 512:(half + 1) * 512],
                                          start=(f == 0), stop=(f == FC - 1))
                    x.then_inc(y_r[j], 1)

                for rnd, t, n in turns(pe):
                    turn_tokens(0, n)
                    for i in range(UNROLL):
                        if i + 1 < UNROLL:
                            turn_tokens(i + 1, n)
                        gate_and_up(i, n)
                        if i:
                            down(i - 1, n)
                        turn_hidden(i, n)
                    down(UNROLL - 1, n)

            @block.scalar
            def _(act):
                for j in range(NB):
                    act.dma_start(idx[j][:, :], lists[:, j:j + 1, :].rearrange("c a b -> c (a b)")).then_inc(idx_in[j], 16)
                    act.sem_inc(y_hi[j])

                def store_tokens(i, n):
                    j, m = use(i, n)
                    act.wait_ge(turned[j], m + 1)
                    act.activation(xT[i % 2][:, :, :].rearrange("p k c -> p (k c)"), t_bank[i % 2][:, :], ACT.Copy).then_inc(t_st[j], 1)

                def store_high(i, n):
                    j, m = use(i, n)
                    act.wait_ge(y_r[j], m + 2)
                    act.wait_ge(y_out[j], m * 16 + 16)
                    act.activation(y[j][:, 512:D], y_bank[i % 2][CAP:P, :], ACT.Copy).then_inc(y_hi[j], 1)
                    ahead = (i + NB) % UNROLL
                    act.dma_start(idx[ahead][:, :], lists[:, bass.ds(n * UNROLL + i + NB, 1), :].rearrange("c a b -> c (a b)")).then_inc(idx_in[ahead], 16)

                for rnd, t, n in turns(act):
                    store_tokens(0, n)
                    for i in range(UNROLL):
                        if i + 1 < UNROLL:
                            store_tokens(i + 1, n)
                        j, m = use(i, n)
                        act.wait_ge(gu[j], m + 1)
                        act.activation(act_g[i % 2][CAP:P, :], g_bank[i % 2][0:CAP, 0:DE], ACT.Silu).then_inc(silu[j], 1)
                        if i:
                            store_high(i - 1, n)
                    store_high(UNROLL - 1, n)

            @block.vector
            def _(dve):
                for j in range(NB):
                    dve.sem_inc(y_lo[j])

                def store_low(i, n):
                    j, m = use(i, n)
                    dve.wait_ge(y_r[j], m + 2)
                    dve.wait_ge(y_out[j], m * 16 + 16)
                    dve.tensor_copy(y[j][:, 0:512], y_bank[i % 2][0:CAP, :]).then_inc(y_lo[j], 1)

                for rnd, t, n in turns(dve):
                    for i in range(UNROLL):
                        j, m = use(i, n)
                        dve.wait_ge(silu[j], m + 1)
                        dve.tensor_tensor(hid_t[i % 2][CAP:P, :], g_bank[i % 2][CAP:P, 0:DE],
                                          act_g[i % 2][CAP:P, :], ALU.mult).then_inc(mul_r[j], 1)
                        if i:
                            store_low(i - 1, n)
                        dve.wait_ge(h_turned[j], m + 1)
                        dve.tensor_copy(hid[i % 2][:, :, :].rearrange("p f c -> p (f c)"), h_bank[i % 2][:, 0:FC * CAP]).then_inc(hid_r[j], 1)
                    store_low(UNROLL - 1, n)


def combine(nc, const, h, y_dram, M):
    with Scope(nc) as s:
        yg = s.sb("expert_rows", [P, TT, 2, D])
        rows = y_dram[0:2 * S, :].rearrange("(c p k) d -> p c k d", p=P, k=2)
        sq = s.sb("fin_sq", [P, D])
        ss = s.sb("fin_ss", [P, TT])
        rs = s.sb("fin_rstd", [P, TT])
        got = s.sems("rows_gathered", 4)
        added = s.sem("rows_added")
        squared, rstd, scaled = s.sem("fin_squares"), s.sem("fin_rstd_ready"), s.sem("fin_scaled")
        with nc.Block() as block:

            @block.sync
            def _(sp):
                for c in range(TT):
                    sp.dma_start(yg[:, c, :, :], rows[:, c, :, :]).then_inc(got[c], 16)

            @block.vector
            def _(dve):
                for i in range(2 * TT):
                    c, j = i // 2, i % 2
                    dve.wait_ge(got[c], 16)
                    if j:
                        dve.wait_ge(added, i)
                    dve.scalar_tensor_tensor(out=h[:, c, :], in0=yg[:, c, j, :], scalar=M["weights"][:, j, c:c + 1], in1=h[:, c, :],
                                             op0=ALU.mult, op1=ALU.add).then_inc(added, 1)
                dve.wait_ge(squared, TT)
                dve.tensor_scalar(ss[:, :], ss[:, :], 1.0 / D, EPS, ALU.mult, ALU.add).then_inc(rstd, 1)
                dve.wait_ge(rstd, 2)
                dve.reciprocal(rs[:, :], ss[:, :]).then_inc(rstd, 1)
                dve.wait_ge(rstd, 3)
                for c in range(TT):
                    dve.scalar_tensor_tensor(out=h[:, c, :], in0=h[:, c, :], scalar=rs[:, c:c + 1], in1=const["fin_g"][:, :],
                                             op0=ALU.mult, op1=ALU.mult).then_inc(scaled, 1)

            @block.scalar
            def _(act):
                for c in range(TT):
                    act.wait_ge(added, 2 * c + 2)
                    if c:
                        act.wait_ge(squared, c)
                    act.activation(sq[:, :], h[:, c, :], ACT.Square, accum_out=ss[:, c:c + 1]).then_inc(squared, 1)
                act.wait_ge(rstd, 1)
                act.activation(ss[:, :], ss[:, :], ACT.Sqrt).then_inc(rstd, 1)


A_REL = 2 * 2 * P - 1
CLS = 4
BUCKETS = 32
SKEW = 16
COL = {"qa": 0, "ka": 512, "va": 640, "qb": 768, "kb": 2304, "vb": 3840, "ga": 5376, "gb": 5888, "mg": 6400}


def by_class(x):
    return x.rearrange("p (t c) -> p c t", c=CLS)


def bias_rows(nc, A, const, T):
    with Scope(nc) as s:
        hot = s.sb("bucket_hot", [BUCKETS, 3, 512])
        rel = s.sb("rel_bias", [BUCKETS, 32])
        win = s.sb("window", [NH, 4, 512])
        tab = s.sb("bias_rows", [NH, 4, 512])
        bank = [s.ps(f"bias_ps{i}") for i in range(4)]
        loaded, ready, added, stored = (s.sem("bias_" + n) for n in ("loaded", "ready", "added", "stored"))
        dram = T["bias_dram"]
        with nc.Block() as block:

            @block.sync
            def _(sp):
                sp.dma_start(hot[:, :, :], A["const_bucket_hot"].rearrange("g b x -> b g x")).then_inc(loaded, 16)
                sp.dma_start(rel[:, :], A["rel_bias_2"]).then_inc(loaded, 16)
                sp.dma_start(win[:, :, :], A["const_window"].rearrange("g h x -> h g x")).then_inc(loaded, 16)
                sp.dma_start(T["sink"][:, :], A["sink_a_2"].broadcast_to([P, NH])).then_inc(loaded, 16)
                sp.wait_ge(added, 4)
                for g in range(4):
                    sp.dma_start(dram[g], tab[:, g:g + 1, :].broadcast_to([NH, SKEW, 512])).then_inc(stored, 16)
                sp.wait_ge(stored, 64)

            @block.tensor
            def _(pe):
                pe.wait_ge(loaded, 64)
                for g in range(4):
                    pe.matmul(bank[g][0:NH, :], rel[:, g * NH:(g + 1) * NH], hot[:, max(g - 1, 0), :], start=True, stop=True).then_inc(ready, 1)

            @block.vector
            def _(dve):
                for g in range(4):
                    dve.wait_ge(ready, g + 1)
                    dve.tensor_tensor(tab[:, g, :], bank[g][0:NH, :], win[:, g, :], ALU.add).then_inc(added, 1)


def head_gain_columns(nc, const, T):
    with Scope(nc) as s:
        done = s.sem("head_gains_ready")
        with nc.Block() as block:

            @block.vector
            def _(dve):
                for i, name in enumerate(("q_norm_a_2", "k_norm_a_2", "q_norm_b_2", "k_norm_b_2")):
                    dve.tensor_scalar(T["head_gains"][:, i:i + 1], par_col(const, PARAM_AT[name]), HD ** -0.5 if i % 2 == 0 else 1.0,
                                      None, ALU.mult).then_inc(done, 1)
                dve.wait_ge(done, 4)


def project_second(nc, A, const, hT, T):
    UNIT, NBANK = 256, 6
    w = A["w_in_2"].rearrange("l (k p) n -> p (l k) n", p=P)
    gains = T["head_gains"]
    jobs = []
    for u in range(21):
        col = u * UNIT
        if col < COL["ka"]:
            jobs += [(u, "qk", x, T["qa"][:, col // P + x, :], 0, False) for x in range(2)]
        elif col == COL["ka"]:
            jobs += [(u, "ka", 0, T["ka"], 1, False)]
            jobs += [(u, "va", 0, T["va"][:, :, :], None, False)]
        elif col < COL["vb"]:
            name = "qb" if col < COL["kb"] else "kb"
            for x in range(2):
                f = (col - COL[name]) // P + x
                jobs.append((u, "qk", x, T[name][:, f, :], 2 if name == "qb" else 3, f >= FT))
        else:
            g, half = divmod((col - COL["vb"]) // UNIT, 2)
            for pair in range(2):
                dst = T["v0"][:, :, half * UNIT:(half + 1) * UNIT] if g == 0 else \
                    T["v12"][:, :, (2 * (g - 1) + half) * UNIT:(2 * (g - 1) + half + 1) * UNIT]
                jobs.append((u, "vb", pair, dst[:, 2 * pair:2 * pair + 2, :], None, g > 0))
    last_job = {}
    for n, job in enumerate(jobs):
        last_job[job[0]] = n
    normed = [n for n, job in enumerate(jobs) if job[1] in ("qk", "ka")]
    plain = [n for n, job in enumerate(jobs) if job[1] not in ("qk", "ka")]
    with Scope(nc) as s:
        wts = SplitWeights(s, "w_in_2", w, [u * UNIT for u in range(21)], UNIT, lambda u: (ready, last_job[u] + 1))
        sq = s.sb("qk_sq", [P, 2, S])
        rs = s.sb("qk_rstd", [P, 2, S])
        bank = [s.ps(f"proj_ps{i}") for i in range(NBANK)]
        sums = [s.ps(f"qk_sum_ps{i}") for i in range(2)]
        ready = s.sem("projected")
        v_st = s.sem("v2_stored")
        squared, summed, logged, rstd, gained, qk_st = (s.sem("head_norm_" + n) for n in ("squared", "summed", "logged", "rstd", "gained", "stored"))
        with nc.Block() as block:

            @block.sync
            def _(sp):
                for u in range(21):
                    wts.load(sp, u)

            @block.tensor
            def _(pe):
                def head_sums(i):
                    pe.wait_ge(squared, i + 1)
                    if i >= 2:
                        pe.wait_ge(logged, i - 1)
                    pe.matmul(sums[i % 2][:, :], const["heads"][:, :], sq[:, i % 2, :], start=True, stop=True).then_inc(summed, 1)

                for n, (u, kind, x, dst, gain, perm) in enumerate(jobs):
                    wts.wait(pe, u)
                    if n >= NBANK:
                        o = n - NBANK
                        if o in normed:
                            pe.wait_ge(qk_st, normed.index(o) + 1)
                        else:
                            pe.wait_ge(v_st, plain.index(o) + 1)
                    b = bank[n % NBANK]

                    def tokens(k):
                        return [p[:, k, :] for p in hT]

                    if kind in ("qk", "ka"):
                        m = split_product(pe, b[:, :], lambda k: wts.parts(u, k, slice(x * P, (x + 1) * P)), tokens, KC)
                    else:
                        cols, nc_ = (slice(P, 2 * P), TT) if kind == "va" else (slice(0, UNIT), 2)
                        width = cols.stop - cols.start
                        for i in range(nc_):
                            c = i if kind == "va" else 2 * x + i

                            def some(k):
                                return [by_class(p[:, k, :])[:, c, :] if perm else p[:, k, c * P:(c + 1) * P] for p in hT]

                            m = split_product(pe, b[:, i * width:(i + 1) * width], some, lambda k: wts.parts(u, k, cols), KC)
                    m.then_inc(ready, 1)
                    if n >= 1 and n - 1 in normed:
                        head_sums(normed.index(n - 1))

            @block.scalar
            def _(act):
                act.preload_act_table_set("natural_log_exp_and_others")
                wts.split_high(act, 0)
                for n, (u, kind, x, dst, gain, perm) in enumerate(jobs):
                    if n == 0 or last_job.get(u - 1) == n - 1:
                        wts.split_high(act, u + 1)
                    if n in normed:
                        i = normed.index(n)
                        act.wait_ge(ready, n + 1)
                        if i >= 2:
                            act.wait_ge(summed, i - 1)
                        act.activation(sq[:, i % 2, :], bank[n % NBANK][:, :], ACT.Square).then_inc(squared, 1)
                        act.wait_ge(summed, i + 1)
                        if i >= 2:
                            act.wait_ge(qk_st, i - 1)
                        act.activation(rs[:, i % 2, :], sums[i % 2][:, :], ACT.Ln, scale=1.0 / HD, bias=const["eps"][:, :]).then_inc(logged, 1)
                        act.wait_ge(logged, i + 1)
                        act.activation(rs[:, i % 2, :], rs[:, i % 2, :], ACT.Exp, scale=-0.5).then_inc(rstd, 1)
                    else:
                        act.wait_ge(ready, n + 1)
                        width = P if kind == "va" else UNIT
                        act.activation(dst, bank[n % NBANK][:, :].rearrange("p (c w) -> p c w", w=width), ACT.Copy).then_inc(v_st, 1)

            @block.vector
            def _(dve):
                wts.split_low(dve, 0)
                for n, (u, kind, x, dst, gain, perm) in enumerate(jobs):
                    if n == 0 or last_job.get(u - 1) == n - 1:
                        wts.split_low(dve, u + 1)
                    if n not in normed:
                        continue
                    i = normed.index(n)
                    dve.wait_ge(rstd, i + 1)
                    r = rs[:, i % 2, :]
                    dve.tensor_scalar(r, r, gains[:, gain:gain + 1], None, ALU.mult).then_inc(gained, 1)
                    dve.wait_ge(gained, i + 1)
                    src = bank[n % NBANK][:, :]
                    if kind == "ka":
                        for head in range(2):
                            at = slice(head * HD, (head + 1) * HD)
                            for half in range(2):
                                o = dve.tensor_tensor(dst[half * HD:(half + 1) * HD, head, :], src[at, :], r[at, :], ALU.mult)
                    elif perm:
                        o = dve.tensor_tensor(dst.rearrange("p (c t) -> p c t", c=CLS), by_class(src), by_class(r), ALU.mult)
                    else:
                        o = dve.tensor_tensor(dst, src, r, ALU.mult)
                    o.then_inc(qk_st, 1)


def windowed_attention(nc, const, T):
    HU = 4
    units = [(g, i, q) for g in range(3) for i in range(TT) for q in range(2)]
    NU = len(units)
    W = 3 * P
    with Scope(nc) as s:
        sc = s.sb("scores", [P, 2, HU, W])
        pt = s.sb("probs_t", [P, 3, W])
        mx = s.sb("row_max", [P, NU, HU])
        nm = s.sb("row_max_neg", [P, NU, HU])
        dn = s.sb("denominators", [P, NU, HU])
        ex = s.sb("sink_exp", [P, 2 * TT, HU])
        inv = s.sb("inverses", [P, 2, HU])
        s_bank = [s.ps(f"attn_score_ps{i}") for i in range(3)]
        t_bank = [s.ps(f"attn_turn_ps{i}") for i in range(2)]
        o_bank = [s.ps(f"attn_out_ps{i}") for i in range(2)]
        sc_ready, biased, p_ready, turned, pt_st, o_st = (
            s.sem("attn_" + n) for n in ("scores", "biased", "probs", "turned", "turned_stored", "stored"))
        used = s.sem("probs_t_used")
        negated, small, sunk = s.sem("row_max_negated"), s.sem("attn_small_step"), s.sem("sink_exp_ready")
        tiled = s.sems("bias_tile_loaded", 4)
        n_small = [0]
        small_at = {}

        def keys(g, i):
            if g == 2:
                return 0, [0, 1]
            b = [j for j in (i - 1, i, i + 1) if 0 <= j < TT]
            return (b[0] - i + 1) * P, b

        with nc.Block() as block:

            @block.sync
            def _(sp):
                dram = T["bias_dram"]
                for g, tile, w in ((0, T["band"][0], W), (1, T["band"][1], W), (2, T["classes"][:, :, 0:P], P),
                                   (3, T["classes"][:, :, P:2 * P], P)):
                    for p in range(0, P, SKEW):
                        src = bass.AP(dram.tensor, dram.offset + g * NH * SKEW * 512 + P - 1 - p, [[511, SKEW], [SKEW * 512, NH], [1, w]])
                        sp.dma_start(tile[p:p + SKEW, :, :], src).then_inc(tiled[g], 16)

            @block.vector
            def _(dve):
                def step(ins):
                    n_small[0] += 1
                    ins.then_inc(small, 1)
                    dve.wait_ge(small, n_small[0])

                def bias(u, h):
                    g, i, q = units[u]
                    c0, bl = keys(g, i)
                    w = len(bl) * P
                    n = HU * u + h
                    if i == 0 and q == 0 and h == 0:
                        for k in ((0,), (1,), (2, 3))[g]:
                            dve.wait_ge(tiled[k], 16 * P // SKEW)
                    dve.wait_ge(sc_ready, n + 1)
                    tile = T["classes"][:, HU * q + h, 0:w] if g == 2 else T["band"][g][:, HU * q + h, c0:c0 + w]
                    dve.tensor_tensor(sc[:, u % 2, h, 0:w], s_bank[n % 3][:, 0:w], tile, ALU.add).then_inc(biased, 1)

                def row_max(u):
                    g, i, q = units[u]
                    w = len(keys(g, i)[1]) * P
                    dve.wait_ge(biased, HU * (u + 1))
                    m = mx[:, u, :]
                    step(dve.tensor_reduce(m, sc[:, u % 2, :, 0:w], AX_X, ALU.max))
                    if g == 0:
                        step(dve.tensor_tensor(m, m, T["sink"][:, HU * q:HU * (q + 1)], ALU.max))
                    dve.tensor_scalar(nm[:, u, :], m, -1.0, None, ALU.mult).then_inc(negated, 1)
                    if g == 0:
                        step(dve.tensor_tensor(ex[:, u, :], T["sink"][:, HU * q:HU * (q + 1)], m, ALU.subtract))
                        small_at[u] = n_small[0]

                def finish(u):
                    g, i, q = units[u]
                    dve.wait_ge(used, HU * (u + 1))
                    o = o_bank[u % 2][:, 0:HU * HD].rearrange("p (h d) -> p h d", h=HU)
                    if g == 0:
                        dve.wait_ge(sunk, u + 1)
                        dve.wait_ge(p_ready, HU * (u + 1))
                        step(dve.tensor_tensor(dn[:, u, :], dn[:, u, :], ex[:, u, :], ALU.add))
                        step(dve.reciprocal(inv[:, u % 2, :], dn[:, u, :]))
                        dve.tensor_tensor(T["ya"][:, i, HU * HD * q:HU * HD * (q + 1)].rearrange("p (h d) -> p h d", h=HU), o,
                                          inv[:, u % 2, :].unsqueeze(2).to_broadcast([P, HU, HD]), ALU.mult).then_inc(o_st, 1)
                    else:
                        dst = T["y0"] if g == 1 else T["y12"]
                        dve.wait_ge(p_ready, HU * (u + 1))
                        step(dve.tensor_copy(dst[:, i, HW + HU * q:HW + HU * (q + 1)], mx[:, u, :]))
                        step(dve.tensor_copy(dst[:, i, HW + NH + HU * q:HW + NH + HU * (q + 1)], dn[:, u, :]))
                        dve.tensor_copy(dst[:, i, HU * HD * q:HU * HD * (q + 1)], o_bank[u % 2][:, 0:HU * HD]).then_inc(o_st, 1)

                for h in range(HU):
                    bias(0, h)
                row_max(0)
                for u in range(NU):
                    w = len(keys(*units[u][0:2])[1]) * P
                    if u + 1 < NU and u >= 1:
                        dve.wait_ge(turned, HU * u)
                    for h in range(HU):
                        if u + 1 < NU:
                            bias(u + 1, h)
                        n = HU * u + h
                        dve.wait_ge(turned, n + 1)
                        if n >= 3:
                            dve.wait_ge(used, n - 2)
                        dve.tensor_copy(pt[:, n % 3, 0:w], t_bank[n % 2][:, 0:w]).then_inc(pt_st, 1)
                    if u + 1 < NU:
                        row_max(u + 1)
                    if u >= 1:
                        finish(u - 1)
                finish(NU - 1)

            @block.tensor
            def _(pe):
                def scores(u, h):
                    g, i, q = units[u]
                    n = HU * u + h
                    head = HU * q + h
                    f, b = head // 2, HD * (head % 2)
                    if n >= 3:
                        pe.wait_ge(biased, n - 2)
                    bank = s_bank[n % 3]
                    rows = slice(i * P, (i + 1) * P)
                    if g == 2:
                        for k in range(2):
                            m = pe.matmul(bank[:, k * P:(k + 1) * P], T["qb"][b:b + HD, (k + 1) * FT + f, rows],
                                          T["kb"][b:b + HD, (k + 1) * FT + f, rows], start=True, stop=True)
                    else:
                        bl = keys(g, i)[1]
                        kk = T["ka"][b:b + HD, head // 4, bl[0] * P:(bl[-1] + 1) * P] if g == 0 else \
                            T["kb"][b:b + HD, f, bl[0] * P:(bl[-1] + 1) * P]
                        qq = (T["qa"] if g == 0 else T["qb"])[b:b + HD, f, rows]
                        m = pe.matmul(bank[:, 0:len(bl) * P], qq, kk, start=True, stop=True)
                    m.then_inc(sc_ready, 1)

                def turn(u, h):
                    n = HU * u + h
                    nb = len(keys(*units[u][0:2])[1])
                    pe.wait_ge(p_ready, n + 1)
                    if n >= 2:
                        pe.wait_ge(pt_st, n - 1)
                    for j in range(nb):
                        m = pe.transpose(t_bank[n % 2][:, j * P:(j + 1) * P], sc[:, u % 2, h, j * P:(j + 1) * P], const["ident"][:, :])
                    m.then_inc(turned, 1)

                def values(u, h):
                    g, i, q = units[u]
                    n = HU * u + h
                    head = HU * q + h
                    pe.wait_ge(pt_st, n + 1)
                    if h == 0 and u >= 2:
                        pe.wait_ge(o_st, u - 1)
                    bl = keys(g, i)[1]
                    for j, b in enumerate(bl):
                        if g == 0:
                            v = T["va"][:, b, (head // 4) * HD:(head // 4 + 1) * HD]
                        elif g == 1:
                            v = T["v0"][:, b, head * HD:(head + 1) * HD]
                        else:
                            v = T["v12"][:, i, b * HW + head * HD:b * HW + (head + 1) * HD]
                        m = pe.matmul(o_bank[u % 2][:, h * HD:(h + 1) * HD], pt[:, n % 3, j * P:(j + 1) * P], v,
                                      start=(j == 0), stop=(j == len(bl) - 1))
                    m.then_inc(used, 1)

                for h in range(HU):
                    scores(0, h)
                for u in range(NU):
                    for h in range(HU):
                        if u + 1 < NU:
                            scores(u + 1, h)
                        turn(u, h)
                        if h:
                            values(u, h - 1)
                        elif u:
                            values(u - 1, HU - 1)
                values(NU - 1, HU - 1)

            @block.scalar
            def _(act):
                act.preload_act_table_set("natural_log_exp_and_others")
                for u in range(NU):
                    g, i, q = units[u]
                    w = len(keys(g, i)[1]) * P
                    act.wait_ge(negated, u + 1)
                    for h in range(HU):
                        act.activation(sc[:, u % 2, h, 0:w], sc[:, u % 2, h, 0:w], ACT.Exp, bias=nm[:, u, h:h + 1],
                                       accum_out=dn[:, u, h:h + 1]).then_inc(p_ready, 1)
                    if g == 0:
                        act.wait_ge(small, small_at[u])
                        act.activation(ex[:, u, :], ex[:, u, :], ACT.Exp).then_inc(sunk, 1)


def merge_groups(nc, const, T):
    W = HW + 2 * NH
    with Scope(nc) as s:
        m = s.sb("merged_max", [P, TT, NH])
        e = [s.sb(f"part_exp{i}", [P, TT, NH]) for i in range(2)]
        d = [s.sb(f"part_den{i}", [P, TT, NH]) for i in range(2)]
        out_st, back, st, ac = s.sem("classes_stored"), s.sem("classes_back"), s.sem("merge_step"), s.sem("merge_exp")
        dram = T["part_dram"]
        y = [T["y0"], T["y12"]]
        with nc.Block() as block:

            @block.sync
            def _(sp):
                for c in range(CLS):
                    sp.dma_start(dram.rearrange("(t c) w -> c t w", c=CLS)[c], y[1][:, c, :]).then_inc(out_st, 16)
                sp.wait_ge(out_st, 16 * CLS)
                sp.dma_start(y[1][:, :, :], dram.rearrange("(c p) w -> p c w", p=P)).then_inc(back, 16)

            @block.scalar
            def _(act):
                for j in range(2):
                    act.wait_ge(st, 3 + j)
                    act.activation(e[j][:, :, :], e[j][:, :, :], ACT.Exp).then_inc(ac, 1)

            @block.vector
            def _(dve):
                n = [0]

                def step(ins):
                    n[0] += 1
                    ins.then_inc(st, 1)
                    dve.wait_ge(st, n[0])

                mx = [x[:, :, HW:HW + NH] for x in y]
                den = [x[:, :, HW + NH:W] for x in y]
                dve.wait_ge(back, 16)
                step(dve.tensor_tensor(m[:, :, :], mx[0], mx[1], ALU.max))
                step(dve.tensor_copy(d[0][:, :, :], den[0]))
                for j in range(2):
                    step(dve.tensor_tensor(e[j][:, :, :], mx[j], m[:, :, :], ALU.subtract))
                for j in range(2):
                    dve.wait_ge(ac, j + 1)
                    step(dve.tensor_tensor(d[j][:, :, :], e[j][:, :, :], den[j], ALU.mult))
                step(dve.tensor_tensor(d[0][:, :, :], d[0][:, :, :], d[1][:, :, :], ALU.add))
                step(dve.reciprocal(d[0][:, :, :], d[0][:, :, :]))
                for j in range(2):
                    step(dve.tensor_tensor(e[j][:, :, :], e[j][:, :, :], d[0][:, :, :], ALU.mult))
                for c in range(TT):
                    for j in range(2):
                        o = y[j][:, c, 0:HW].rearrange("p (h d) -> p h d", h=NH)
                        step(dve.tensor_tensor(o, o, e[j][:, c, :].unsqueeze(2).to_broadcast([P, NH, HD]), ALU.mult))
                    step(dve.tensor_tensor(y[0][:, c, 0:HW], y[0][:, c, 0:HW], y[1][:, c, 0:HW], ALU.add))


def gate_and_merge(nc, A, const, hT, T, merged):
    UNIT, NBANK = 256, 6
    w = A["w_in_2"].rearrange("l (k p) n -> p (l k) n", p=P)
    wa = A["w_branch_a_2"].rearrange("l (k p) n -> p (l k) n", p=P)
    wb = A["w_branch_b_2"].rearrange("l (k p) n -> p (l k) n", p=P)
    first = COL["ga"] // UNIT
    mg = COL["mg"] // UNIT
    units = list(range(first, mg))
    for j in range(4):
        units += [mg + j, mg + 4 + j]
    NGU = mg - first
    with Scope(nc) as s:
        def used(n):
            j, b = divmod(n - NGU, 2)
            return ready, 2 * (n + 1) if n < NGU else 2 * NGU + 8 * j + 5 + b

        wts = SplitWeights(s, "gate_w", w, [u * UNIT for u in units], UNIT, used)
        bw = [s.sb(f"branch_w{i}", [P, FT, D]) for i in range(2)]
        yT = s.sb("branches_t", [P, 2 * FT, S])
        sg = s.sb("gate_sigmoid", [P, 3, S])
        mix = s.sb("mix_part", [P, 2, S])
        bank = [s.ps(f"gate_ps{i}") for i in range(NBANK)]
        t_bank = [s.ps(f"turn_ps{i}") for i in range(2)]
        b_in = s.sem("branch_w_loaded")
        turned, t_st, ready, sig_r, gated, part, st = (
            s.sem("gm_" + n) for n in ("turned", "turned_stored", "ready", "sigmoid", "gated", "part", "stored"))
        y = [T["ya"], T["y0"]]
        with nc.Block() as block:

            @block.sync
            def _(sp):
                for n in range(len(units)):
                    wts.load(sp, n)
                    if n < 2:
                        sp.dma_start(bw[n][:, :, :], (wa, wb)[n]).then_inc(b_in, 16)

            @block.tensor
            def _(pe):
                for f in range(2 * FT):
                    if f >= 2:
                        pe.wait_ge(t_st, f - 1)
                    for c in range(TT):
                        m = pe.transpose(t_bank[f % 2][:, c * P:(c + 1) * P], y[f // FT][:, c, (f % FT) * P:(f % FT + 1) * P], const["ident"][:, :])
                    m.then_inc(turned, 1)
                n = 0

                def tile(unit, half):
                    split_product(pe, bank[n % NBANK][:, :], lambda k: wts.parts(unit, k, slice(half * P, (half + 1) * P)),
                                  lambda k: [p[:, k, :] for p in hT], KC).then_inc(ready, 1)

                for i in range(NGU):
                    wts.wait(pe, i)
                    for half in range(2):
                        if n >= NBANK:
                            pe.wait_ge(gated, n - NBANK + 1)
                        tile(i, half)
                        n += 1
                pe.wait_ge(b_in, 32)
                for j in range(4):
                    for half in range(2):
                        for b in range(2):
                            i = NGU + 2 * j + b
                            if half == 0:
                                wts.wait(pe, i)
                            o = n - NBANK
                            if o < 2 * NGU:
                                pe.wait_ge(gated, o + 1)
                            else:
                                k, r = divmod(o - 2 * NGU, 4)
                                pe.wait_ge(sig_r, 2 * NGU + 2 * k + r + 1) if r < 2 else pe.wait_ge(part, 3 * k + r - 1)
                            tile(i, half)
                            n += 1
                        if j == 0 and half == 0:
                            pe.wait_ge(gated, 2 * NGU)
                        for b in range(2):
                            o = n - NBANK
                            if o < 2 * NGU:
                                pe.wait_ge(gated, o + 1)
                            else:
                                k, r = divmod(o - 2 * NGU, 4)
                                pe.wait_ge(sig_r, 2 * NGU + 2 * k + r + 1) if r < 2 else pe.wait_ge(part, 3 * k + r - 1)
                            t = 2 * j + half
                            for k in range(FT):
                                m = pe.matmul(bank[n % NBANK][:, :], bw[b][:, k, t * P:(t + 1) * P], yT[:, b * FT + k, :],
                                              start=(k == 0), stop=(k == FT - 1))
                            m.then_inc(ready, 1)
                            n += 1

            @block.scalar
            def _(act):
                wts.split_high(act, 0)
                for f in range(2 * NGU):
                    if f % 2 == 0:
                        wts.split_high(act, f // 2 + 1)
                    act.wait_ge(ready, f + 1)
                    if f >= 3:
                        act.wait_ge(gated, f - 2)
                    act.activation(sg[:, f % 3, :], bank[f % NBANK][:, :], ACT.Sigmoid).then_inc(sig_r, 1)
                wts.split_high(act, NGU + 1)
                for t in range(KC):
                    for b in range(2):
                        i = 2 * NGU + 2 * t + b
                        n = 2 * NGU + 4 * t + b
                        act.wait_ge(ready, n + 1)
                        o = i - 3
                        if o < 2 * NGU:
                            act.wait_ge(gated, o + 1)
                        else:
                            k, r = divmod(o - 2 * NGU, 2)
                            act.wait_ge(part, 3 * k + r + 1)
                        act.activation(sg[:, i % 3, :], bank[n % NBANK][:, :], ACT.Sigmoid,
                                       bias=par_col(const, PARAM_AT["b_merge_2"] + b * KC + t)).then_inc(sig_r, 1)
                        if t % 2:
                            wts.split_high(act, NGU + t + 1 + b)

            @block.vector
            def _(dve):
                for f in range(2 * FT):
                    if f == FT:
                        wts.split_low(dve, 0)
                    dve.wait_ge(turned, f + 1)
                    dve.tensor_copy(yT[:, f, :], t_bank[f % 2][:, :]).then_inc(t_st, 1)
                for f in range(2 * FT):
                    if f % 2 == 0:
                        wts.split_low(dve, f // 2 + 1)
                    dve.wait_ge(sig_r, f + 1)
                    dve.wait_ge(t_st, 2 * FT)
                    dve.tensor_tensor(sg[:, f % 3, :], bank[f % NBANK][:, :], sg[:, f % 3, :], ALU.mult).then_inc(st, 1)
                    dve.wait_ge(st, f + 1)
                    dve.tensor_tensor(yT[:, f, :], yT[:, f, :], sg[:, f % 3, :], ALU.mult).then_inc(gated, 1)
                wts.split_low(dve, NGU + 1)
                for t in range(KC):
                    if t % 2:
                        for b in range(2):
                            wts.split_low(dve, NGU + t + 1 + b)
                    for b in range(2):
                        n = 2 * NGU + 4 * t + 2 + b
                        i = 2 * NGU + 2 * t + b
                        dve.wait_ge(ready, n + 1)
                        dve.wait_ge(sig_r, i + 1)
                        if b == 0 and t:
                            dve.wait_ge(part, 3 * t)
                        dve.tensor_tensor(mix[:, b, :], bank[n % NBANK][:, :], sg[:, i % 3, :], ALU.mult).then_inc(part, 1)
                    dve.wait_ge(part, 3 * t + 2)
                    dve.tensor_tensor(merged[:, t, :], mix[:, 0, :], mix[:, 1, :], ALU.add).then_inc(part, 1)


def second_block(nc, A, const, out):
    with Scope(nc) as b2:
        recycle(nc)
        hT = [b2.sb("block_in_high", [P, KC, S], F32R), b2.sb("block_in_low", [P, KC, S], F32R)]
        T = {"ya": b2.sb("y_a", [P, TT, HW]), "y0": b2.sb("y_b0", [P, TT, HW + 2 * NH]),
             "head_gains": b2.sb("head_gains", [P, 4]), "sink": b2.sb("sink", [P, NH]),
             "bias_dram": nc.dram_tensor("bias_rows_dram", (4, NH, SKEW, 512), F32, kind="Internal").ap(),
             "part_dram": nc.dram_tensor("class_part_dram", (S, HW + 2 * NH), F32, kind="Internal").ap()}
        norm_to_features(nc, const["h"], PARAM_AT["norm_gain_2"], hT[0], const, "n2", low=hT[1])
        head_gain_columns(nc, const, T)
        with Scope(nc) as s:
            qk_a = s.sb("qk_a", [P, (FT + 2) * S])
            T["qa"] = qk_a[:, 0:FT * S].rearrange("p (f t) -> p f t", f=FT)
            T["ka"] = qk_a[:, FT * S:(FT + 2) * S].rearrange("p (f t) -> p f t", f=2)
            T["y12"] = qk_a[:, 0:TT * (HW + 2 * NH)].rearrange("p (c w) -> p c w", c=TT)
            T["qb"], T["kb"] = s.sb("qb", [P, 3 * FT, S]), s.sb("kb", [P, 3 * FT, S])
            T["va"], T["v0"], T["v12"] = s.sb("va", [P, TT, P]), s.sb("vb0", [P, TT, HW]), s.sb("vb12", [P, TT, 2 * HW])
            bias_rows(nc, A, const, T)
            project_second(nc, A, const, hT, T)
            recycle(nc)
            T["band"] = [s.sb(f"band_bias{g_}", [P, NH, 3 * P]) for g_ in range(2)]
            T["classes"] = s.sb("class_bias", [P, NH, 2 * P])
            windowed_attention(nc, const, T)
            merge_groups(nc, const, T)
        merged = b2.sb("merged", [P, KC, S])
        gate_and_merge(nc, A, const, hT, T, merged)
        out_projection(nc, const, A["w_out_2"], merged, KC, const["h"], "wo2", out.rearrange("b t d -> (b t) d"))


def program(nc, A, out):
    Scope.ended = []
    with Scope(nc) as g:
        const = {"h": g.sb("h", [P, TT, D]), "ident": g.sb("ident", [P, P]), "par": g.sb("params", [P, N_PARAMS]),
                 "heads": g.sb("heads", [P, P]),
                 "eps": g.sb("eps", [P, 1]), "gn_eps": g.sb("gn_eps", [P, 1]), "log_shift": g.sb("log_shift", [P, 1]), "x_loaded": g.sem("x_loaded"), "row_params": g.sem("row_params_loaded")}
        once = g.stack.enter_context(Scope(nc))
        const.update({"causal": once.sb("causal", [P, 4, P]), "neg_causal": once.sb("neg_causal", [P, P]),
                      "minus_ones": once.sb("minus_ones", [P, P]), "suffix": once.sb("suffix", [P, P]),
                      "level": once.sb("level", [P, 7, P]),
                      "one_minus_mu": once.sb("one_minus_mu", [P, RT]), "one_minus_ka": once.sb("one_minus_ka", [P, FT]),
                      "ffn_g": once.sb("ffn_gain", [P, D]), "fin_g": once.sb("final_gain", [P, D])})
        setup_constants(nc, A, const)
        with Scope(nc) as b1:
            mixT = b1.sb("mixer_out", [P, KC, S])
            um = b1.sb("um", [P, RT, S])
            with Scope(nc) as sc:
                qk = sc.sb("qk", [P, 2 * FT, S])
                v = sc.sb("v", [P, TT, HW])
                with Scope(nc) as s:
                    xnT = s.sb("xnT", [P, KC, S])
                    norm_to_features(nc, const["h"], PARAM_AT["norm_mix_g"], xnT, const, "n1", const["x_loaded"])
                    project_first(nc, A, xnT, um, qk, v, const)
                stick_breaking(nc, const, qk, v, mixT)
            with Scope(nc) as rw:
                R = {"gate": rw.sb("gate", [P, FT, S]), "bonus": rw.sb("bonus", [P, FT, S]),
                     "kr": rw.sb("kk_r", [P, FT * NC, 2, CH]), "bh": rw.sb("b_hat", [P, FT, S]),
                     "kh": rw.sb("k_hat", [P, FT, S]), "mid": rw.sb("mid_decay", [P, FT * NC]),
                     "ends": rw.sb("chunk_sums", [P, FT * NC])}
                rwkv_features(nc, A, const, um, R)
                R["q"] = rw.sb("q_hat", [P, FT, S])
                R["o"] = rw.sb("rwkv_out", [P, FT, S])
                R["mn"] = rw.sb("m_n", [P, FT * NC, 2, HD])
                rwkv_chunks(nc, const, um, R)
                rwkv_output(nc, const, R, mixT)
            out_projection(nc, const, A["w_out"], mixT, KC, const["h"], "wo")
        with Scope(nc) as moe:
            M = {"slots": moe.sb("slots", [P, 2, TT], I32), "weights": moe.sb("route_weights", [P, 2, TT]),
                 "rounds": moe.sb("rounds", [P, 1], I32),
                 "gate": [moe.sb(f"w_gate{j}", [P, KC, DE]) for j in range(NB)],
                 "up": [moe.sb(f"w_up{j}", [P, KC, DE]) for j in range(NB)],
                 "down": [moe.sb(f"w_down{j}", [P, FC, D]) for j in range(NB)],
                 "weights_in": moe.sems("expert_loaded", NB)}
            xn_dram = nc.dram_tensor("ffn_in_dram", (S, D), F32, kind="Internal").ap()
            list_dram = nc.dram_tensor("expert_lists", (LIST, 2), I32, kind="Internal").ap()
            y_dram = nc.dram_tensor("expert_rows_dram", (2 * S + LIST + NB * CAP, D), F32, kind="Internal").ap()
            route(nc, A, const, const["h"], xn_dram, list_dram, M)
            recycle(nc)
            experts(nc, A, const, xn_dram, list_dram, y_dram, M)
            combine(nc, const, const["h"], y_dram, M)
        once.stack.close()
        second_block(nc, A, const, out)


def shape_constants():
    def bucket(rel):
        half, exact = BUCKETS // 2, BUCKETS // 4
        n = np.abs(rel)
        large = exact + (np.log(np.maximum(n, exact).astype(np.float32) / np.float32(exact)) / np.float32(np.log(1024 / exact))
                         * np.float32(half - exact)).astype(np.int32)
        return (rel > 0) * half + np.where(n < exact, n, np.minimum(large, half - 1))

    x = np.arange(512)
    band = np.minimum(x, A_REL - 1) - (2 * P - 1)
    apart = np.minimum(x, 2 * P - 2) - (P - 1)
    rels = [band, 4 * apart, 4 * apart]
    hot = np.stack([(bucket(r)[None, :] == np.arange(BUCKETS)[:, None]) for r in rels]).astype(np.float32)
    ok = [np.abs(band) <= 128, np.abs(band) <= 64, np.abs(apart) <= 64, apart % 4 == 0]
    window = np.stack([np.broadcast_to(np.where(o, 0.0, NEG), (NH, 512)) for o in ok]).astype(np.float32)
    return {"const_bucket_hot": np.ascontiguousarray(hot), "const_window": np.ascontiguousarray(window)}


def kernel(**inputs):
    import concourse.bacc as bacc
    from concourse.bass_utils import run_bass_kernel_spmd

    nc = bacc.Bacc("TRN2", target_bir_lowering=False, num_devices=1)
    arrays, A = {}, {}
    for name, a in {**inputs, **shape_constants()}.items():
        a = np.ascontiguousarray(a)
        arrays[name + "_dram"] = a
        A[name] = nc.dram_tensor(name + "_dram", a.shape, mybir.dt.from_np(a.dtype), kind="ExternalInput").ap()
    out = nc.dram_tensor("out_dram", (1, S, D), F32, kind="ExternalOutput").ap()
    program(nc, A, out)
    r = run_bass_kernel_spmd(nc, [arrays], core_ids=[0])
    return r.results[0]["out_dram"]
```

```python
from contextlib import ExitStack

import numpy as np

import concourse.bass as bass
from concourse import mybir

F32 = mybir.dt.float32
F32R = mybir.dt.float32r
I32 = mybir.dt.int32
ALU = mybir.AluOpType
ACT = mybir.ActivationFunctionType
AX_X = mybir.AxisListType.X

P = 128
S = 512
TT = S // P
D = 1024
KC = D // P
NH = 8
HD = 64
HW = NH * HD
FT = HW // P
SB_IN = 3 * HW
RW_IN = 3 * HW + 64 + 64 + 128
RT = RW_IN // P
EPS = 1e-6
GN_EPS = 64e-5
DECAY = float(np.exp(-0.5))
NEG = -1e30
LOG_BITS = 30
CH = P
NC = S // CH

NG, EPG = 4, 8
NE = NG * EPG
DE = 256
CAP = 64
NB = 4
UNROLL = 8
LIST = NE * S + NB * CAP
FC = DE // P

PARAM_ROWS = [("norm_mix_g", 8), ("shift_mu", RT), ("sb_out_g", 4), ("rw_w0", 4), ("rw_a0", 4), ("rw_k_k", 4),
              ("rw_k_a", 4), ("rw_r_k", 4), ("rw_ln_w", 4), ("rw_ln_b", 4), ("norm_gain_2", 8), ("b_merge_2", 16),
              ("q_norm_a_2", 1), ("k_norm_a_2", 1), ("q_norm_b_2", 1), ("k_norm_b_2", 1)]
PARAM_AT = {}
_row = 0
for _name, _n in PARAM_ROWS:
    PARAM_AT[_name] = _row
    _row += _n
N_PARAMS = _row


class Scope:

    ended = []

    def __init__(self, nc):
        self.nc = nc
        self.stack = ExitStack()
        self.own = []

    def __enter__(self):
        return self

    def __exit__(self, *e):
        Scope.ended += self.own
        self.own = []
        return self.stack.__exit__(*e)

    def sb(self, name, shape, dt=F32):
        return self.stack.enter_context(self.nc.sbuf_tensor(name, shape, dt))

    def ps(self, name, n=512):
        return self.stack.enter_context(self.nc.psum_tensor(name, [P, n], F32))

    def sem(self, name):
        self.own.append(self.nc.alloc_semaphore(name))
        return self.own[-1]

    def sems(self, name, n):
        return [self.sem(f"{name}{i}") for i in range(n)]


def recycle(nc):
    nc.clear_and_free_semaphores(Scope.ended)
    Scope.ended = []
    nc.all_engine_barrier()


def make_masks(pool, made, const):
    n = [0]

    def step(ins):
        n[0] += 1
        ins.then_inc(made, 1)
        pool.wait_ge(made, n[0])

    cm = const["causal"]
    step(pool.memset(cm[:, :, :], 1.0))
    for k in range(4):
        step(pool.affine_select(out=cm[:, k, :], in_=cm[:, k, :], fill=0.0, base=0, pattern=[[1, P]],
                                compare_op=(ALU.is_gt, ALU.is_ge)[k % 2], channel_multiplier=-1))
    step(pool.memset(const["neg_causal"][:, :], 0.0))
    step(pool.affine_select(out=const["neg_causal"][:, :], in_=const["neg_causal"][:, :], fill=NEG, base=0,
                            pattern=[[1, P]], compare_op=ALU.is_gt, channel_multiplier=-1))
    step(pool.memset(const["minus_ones"][:, :], -1.0))
    step(pool.memset(const["suffix"][:, :], -1.0))
    step(pool.affine_select(out=const["suffix"][:, :], in_=const["suffix"][:, :], fill=0.0, base=0,
                            pattern=[[-1, P]], compare_op=ALU.is_ge, channel_multiplier=1))
    for l in range(7):
        m = 1 << l
        lv = const["level"][:, l, :]
        step(pool.memset(lv, 0.0))
        v = lv.rearrange("p (b h x) -> p b h x", h=2, x=m)[:, :, 0, :]
        step(pool.memset(v, 1.0))
        nb = P // (2 * m)
        step(pool.affine_select(out=v, in_=v, fill=0.0, base=-m, pattern=[[-2 * m, nb], [0, m]],
                                compare_op=ALU.is_ge, channel_multiplier=1))
        step(pool.affine_select(out=v, in_=v, fill=0.0, base=2 * m, pattern=[[2 * m, nb], [0, m]],
                                compare_op=ALU.is_gt, channel_multiplier=-1))


def setup_constants(nc, A, const):
    with Scope(nc) as s:
        rows = s.sb("param_rows", [P, P])
        pst = s.ps("param_ps")
        loaded = s.sem("params_loaded")
        padded = s.sem("param_rows_padded")
        turned = s.sem("params_turned")
        copied = s.sem("params_copied")
        made = s.sem("masks_made")
        ident, par = const["ident"], const["par"]
        n_loads = len(PARAM_ROWS)
        with nc.Block() as block:

            @block.sync
            def _(sp):
                sp.wait_ge(padded, 1)
                for name, n in PARAM_ROWS:
                    r = PARAM_AT[name]
                    if "_norm_" in name:
                        sp.dma_start(rows[r:r + 1, :].rearrange("a (k n) -> a k n", k=2),
                                     A[name].rearrange("(l a) n -> l a n", a=1).broadcast_to([1, 2, HD])).then_inc(loaded, 16)
                    else:
                        src = A[name]
                        if len(src.shape) == 3:
                            src = src.rearrange("l a b -> l (a b)")
                        sp.dma_start(rows[r:r + n, :], src.rearrange("l (n p) -> (l n) p", p=P)).then_inc(loaded, 16)
                sp.dma_start(const["ffn_g"][:, :], A["norm_ffn_g"][0:1, :].broadcast_to([P, D])).then_inc(const["row_params"], 16)
                sp.dma_start(const["fin_g"][:, :], A["final_norm_g"].rearrange("(a d) -> a d", a=1).broadcast_to([P, D])).then_inc(const["row_params"], 16)

            @block.gpsimd
            def _(pool):
                n = [0]

                def step(ins):
                    n[0] += 1
                    ins.then_inc(made, 1)
                    pool.wait_ge(made, n[0])

                step(pool.memset(const["eps"][:, :], EPS))
                step(pool.memset(const["gn_eps"][:, :], GN_EPS))
                step(pool.memset(const["log_shift"][:, :], float(0.5 * LOG_BITS * np.log(2.0))))
                step(pool.memset(ident[:, :], 0.0))
                step(pool.affine_select(out=ident[:, :], in_=ident[:, :], compare_op=ALU.not_equal, fill=1.0, base=0,
                                        pattern=[[-1, P]], channel_multiplier=1))
                step(pool.memset(const["heads"][:, :], 0.0))
                step(pool.memset(const["heads"][0:HD, 0:HD], 1.0))
                step(pool.memset(const["heads"][HD:P, HD:P], 1.0))
                step(pool.tensor_copy(const["heads_exact"][:, :], const["heads"][:, :]))

            @block.scalar
            def _(act):
                act.dma_start(const["h"][:, :, :], A["x"].rearrange("b (c p) d -> p (b c) d", p=P)).then_inc(const["x_loaded"], 16)

            @block.tensor
            def _(pe):
                pe.wait_ge(made, 5)
                pe.wait_ge(loaded, 16 * n_loads)
                pe.transpose(pst[:, 0:P], rows[:, :], ident[:, :]).then_inc(turned, 1)

            @block.vector
            def _(dve):
                dve.memset(rows[:, :], 0.0).then_inc(padded, 1)
                dve.wait_ge(turned, 1)
                dve.tensor_copy(par[:, :], pst[:, 0:N_PARAMS]).then_inc(copied, 1)
                mu = PARAM_AT["shift_mu"]
                dve.wait_ge(copied, 1)
                dve.tensor_scalar(const["one_minus_mu"][:, :], par[:, mu:mu + RT], -1.0, 1.0, ALU.mult, ALU.add).then_inc(copied, 1)
                ka = PARAM_AT["rw_k_a"]
                dve.tensor_scalar(const["one_minus_ka"][:, :], par[:, ka:ka + FT], -1.0, 1.0, ALU.mult, ALU.add).then_inc(copied, 1)
                dve.wait_ge(copied, 3)


def norm_to_features(nc, src, gain, dst, const, tag, wts, x_loaded=None, scratch=None):
    high, low = dst
    with Scope(nc) as s:
        xs = scratch if scratch is not None else s.sb(tag + "_scaled", [P, TT, D])
        ss = s.sb(tag + "_ss", [P, TT])
        rs = s.sb(tag + "_rstd", [P, TT])
        banks = [s.ps(f"{tag}_ps{i}") for i in range(4)]
        squared = s.sem(tag + "_squares_summed")
        rstd = s.sem(tag + "_rstd_ready")
        scaled = s.sem(tag + "_tokens_scaled")
        turned = s.sem(tag + "_chunk_turned")
        high_st = s.sem(tag + "_high_part_stored")
        low_st = s.sem(tag + "_low_part_stored")
        ident, par = const["ident"], const["par"]
        with nc.Block() as block:

            @block.sync
            def _(sp):
                for n in range(2):
                    wts.load(sp, n)

            @block.scalar
            def _(act):
                if x_loaded is not None:
                    act.wait_ge(x_loaded, 16)
                for c in range(TT):
                    if c:
                        act.wait_ge(squared, c)
                    act.activation(high[:, 0:2, :], src[:, c, :].rearrange("p (k t) -> p k t", k=2), ACT.Square, accum_out=ss[:, c:c + 1]).then_inc(squared, 1)
                act.wait_ge(rstd, 1)
                act.activation(ss[:, :], ss[:, :], ACT.Sqrt).then_inc(rstd, 1)
                wts.split_high(act, 0)
                for k in range(KC):
                    act.wait_ge(turned, k + 1)
                    act.activation(high[:, k, :], banks[k % 4][:, :], ACT.Copy,
                                   scale=par[:, gain + k:gain + k + 1]).then_inc(high_st, 1)

            @block.vector
            def _(dve):
                dve.wait_ge(squared, TT)
                dve.tensor_scalar(ss[:, :], ss[:, :], 1.0 / D, EPS, ALU.mult, ALU.add).then_inc(rstd, 1)
                dve.wait_ge(rstd, 2)
                dve.reciprocal(rs[:, :], ss[:, :]).then_inc(rstd, 1)
                dve.wait_ge(rstd, 3)
                for c in range(TT):
                    dve.tensor_scalar(xs[:, c, :], src[:, c, :], rs[:, c:c + 1], None, ALU.mult).then_inc(scaled, 1)
                wts.split_low(dve, 0)
                for k in range(KC):
                    dve.wait_ge(high_st, k + 1)
                    dve.scalar_tensor_tensor(out=low[:, k, :], in0=banks[k % 4][:, :], scalar=par[:, gain + k:gain + k + 1],
                                             in1=high[:, k, :], op0=ALU.mult, op1=ALU.subtract).then_inc(low_st, 1)

            @block.tensor
            def _(pe):
                for k in range(KC):
                    if k >= 4:
                        pe.wait_ge(low_st, k - 3)
                    for c in range(TT):
                        pe.wait_ge(scaled, c + 1)
                        t = pe.transpose(banks[k % 4][:, c * P:(c + 1) * P], xs[:, c, k * P:(k + 1) * P], ident[:, :])
                    t.then_inc(turned, 1)


UNIT = 256


def first_weights(s, A):
    w = A["w_in"].rearrange("l (k p) n -> p (l k) n", p=P)
    cols = [SB_IN + UNIT * i for i in range(RW_IN // UNIT)] + [UNIT * i for i in range(SB_IN // UNIT)]
    return SplitWeights(s, "w_in", w, cols, UNIT).place_parts(s)


def project_first(nc, A, xnT, um, qk, v, const, wts):
    NBANK = 6
    NU = len(wts.cols)
    FU = (RT + 2 * FT) * P // UNIT
    with Scope(nc) as s:
        shifted = s.sb("shifted", [P, 2, S])
        banks = [s.ps(f"u_ps{i}") for i in range(NBANK)]
        vbank = banks[0:4]
        ready = s.sem("u_tile_ready")
        sh_zero = s.sem("shift_zeroed")
        sh = s.sem("u_shifted")
        mixed = s.sem("u_mixed")
        qk_st = s.sem("qk_stored")
        v_ready = s.sem("v_ready")
        masks_made = s.sem("first_masks_made")
        wts.used = lambda n: (ready, 2 * (n + 1))
        v_st = s.sem("v_stored")
        with nc.Block() as block:

            @block.sync
            def _(sp):
                for i in range(2, NU):
                    wts.load(sp, i)

            @block.tensor
            def _(pe):
                n = 0
                for i in range(NU):
                    wts.wait(pe, i)
                    if i < FU:
                        for half in range(2):
                            if n >= NBANK:
                                done = n - NBANK + 1
                                pe.wait_ge(mixed, min(done, RT))
                                if done > RT:
                                    pe.wait_ge(qk_st, done - RT)
                            split_product(pe, banks[n % NBANK][:, :], lambda k: wts.parts(i, k, slice(half * P, (half + 1) * P)),
                                          lambda k: [x[:, k, :] for x in xnT], KC).then_inc(ready, 1)
                            n += 1
                    else:
                        part = i - FU
                        if part == 0:
                            pe.wait_ge(qk_st, 2 * FT)
                        for c in range(TT):
                            m = split_product(pe, vbank[c][:, part * UNIT:(part + 1) * UNIT],
                                              lambda k: [x[:, k, c * P:(c + 1) * P] for x in xnT],
                                              lambda k: wts.parts(i, k, slice(0, UNIT)), KC)
                            if c == TT - 1 and part == 1:
                                m.then_inc(v_ready, 1)

            @block.gpsimd
            def _(pool):
                make_masks(pool, masks_made, const)

            @block.scalar
            def _(act):
                mu = PARAM_AT["shift_mu"]
                act.wait_ge(sh_zero, 1)
                wts.split_high(act, 1)
                for j in range(RT):
                    if j % 2 == 0 and j:
                        wts.split_high(act, j // 2 + 1)
                    act.wait_ge(ready, j + 1)
                    if j >= 2:
                        act.wait_ge(mixed, j - 1)
                    act.activation(shifted[:, j % 2, 1:S], banks[j % NBANK][:, 0:S - 1], ACT.Copy,
                                   scale=par_col(const, mu + j)).then_inc(sh, 1)
                for j in range(2 * FT):
                    n = RT + j
                    if n % 2 == 0:
                        wts.split_high(act, n // 2 + 1)
                    act.wait_ge(ready, n + 1)
                    act.activation(qk[:, j, :], banks[n % NBANK][:, :], ACT.Copy,
                                   scale=HD ** -0.5 if j < FT else 1.0).then_inc(qk_st, 1)
                for j in range(FU + 1, NU):
                    wts.split_high(act, j)

            @block.vector
            def _(dve):
                dve.memset(shifted[:, :, 0:1], 0.0).then_inc(sh_zero, 1)
                wts.split_low(dve, 1)
                for j in range(RT):
                    if j % 2 == 0 and j:
                        wts.split_low(dve, j // 2 + 1)
                    dve.wait_ge(sh, j + 1)
                    dve.scalar_tensor_tensor(out=um[:, j, :], in0=banks[j % NBANK][:, :],
                                             scalar=const["one_minus_mu"][:, j:j + 1], in1=shifted[:, j % 2, :],
                                             op0=ALU.mult, op1=ALU.add).then_inc(mixed, 1)
                for j in range(RT // 2 + 1, NU):
                    wts.split_low(dve, j)
                dve.wait_ge(v_ready, 1)
                for c in range(TT):
                    dve.tensor_copy(v[:, c, :], vbank[c][:, :]).then_inc(v_st, 1)


def split_product(pe, out, a, b, n):
    for k in range(n):
        for i, j in ((0, 0), (0, 1), (1, 0)):
            m = pe.matmul(out, a(k)[i], b(k)[j], start=(k == 0 and i + j == 0), stop=(k == n - 1 and i == 1))
    return m


class SplitWeights:

    def __init__(self, s, tag, w, cols, unit, used=None, raw=None):
        self.w, self.cols, self.unit, self.used = w, cols, unit, used
        if raw is None:
            raw = s.sb(tag + "_raw", [P, 2, KC, unit])
        self.raw = [raw[:, i] for i in range(2)] if not isinstance(raw, list) else raw
        self.tag, self.part = tag, None
        self.loaded = s.sems(tag + "_loaded", 2)
        self.high, self.low = s.sem(tag + "_high_ready"), s.sem(tag + "_low_ready")

    def place_parts(self, s):
        self.part = [s.sb(f"{self.tag}_{n}", [P, 2, KC, self.unit], F32R) for n in ("high", "low")]
        return self

    def load(self, sp, n):
        if n >= 2:
            sp.wait_ge(self.low, n - 1)
        sp.dma_start(self.raw[n % 2], self.w[:, :, self.cols[n]:self.cols[n] + self.unit]).then_inc(self.loaded[n % 2], 16)

    def split_high(self, act, n):
        if n >= len(self.cols):
            return
        if n >= 2:
            act.wait_ge(*self.used(n - 2))
        act.wait_ge(self.loaded[n % 2], 16 * (n // 2 + 1))
        act.activation(self.part[0][:, n % 2, :, :], self.raw[n % 2], ACT.Copy).then_inc(self.high, 1)

    def split_low(self, dve, n):
        if n >= len(self.cols):
            return
        if n >= 2:
            dve.wait_ge(*self.used(n - 2))
        dve.wait_ge(self.high, n + 1)
        dve.tensor_tensor(self.part[1][:, n % 2, :, :], self.raw[n % 2], self.part[0][:, n % 2, :, :],
                          ALU.subtract).then_inc(self.low, 1)

    def wait(self, pe, n):
        pe.wait_ge(self.low, n + 1)

    def parts(self, n, k, cols):
        return [p[:, n % 2, k, cols] for p in self.part]


def par_col(const, i):
    return const["par"][:, i:i + 1]


def normalize_heads(nc, const, tiles, tag):
    with Scope(nc) as s:
        sq = s.sb(tag + "_sq", [P, 2, S])
        rs = s.sb(tag + "_rstd", [P, 2, S])
        banks = [s.ps(f"{tag}_ps{i}") for i in range(2)]
        squared = s.sem("head_squares")
        summed = s.sem("head_sums")
        logged = s.sem("head_logs")
        rstd = s.sem("head_rstd")
        scaled = s.sem("head_scaled")
        n = len(tiles)
        with nc.Block() as block:

            @block.scalar
            def _(act):
                act.preload_act_table_set("natural_log_exp_and_others")
                for j in range(n + 1):
                    if j < n:
                        if j >= 2:
                            act.wait_ge(summed, j - 1)
                        act.activation(sq[:, j % 2, :], tiles[j][0], ACT.Square).then_inc(squared, 1)
                    if j >= 1:
                        i = j - 1
                        act.wait_ge(summed, i + 1)
                        if i >= 2:
                            act.wait_ge(scaled, i - 1)
                        act.activation(rs[:, i % 2, :], banks[i % 2][:, :], ACT.Ln, scale=1.0 / HD,
                                       bias=const["eps"][:, :]).then_inc(logged, 1)
                        act.wait_ge(logged, i + 1)
                        act.activation(rs[:, i % 2, :], rs[:, i % 2, :], ACT.Exp, scale=-0.5).then_inc(rstd, 1)

            @block.tensor
            def _(pe):
                for j in range(n):
                    pe.wait_ge(squared, j + 1)
                    if j >= 2:
                        pe.wait_ge(logged, j - 1)
                    pe.matmul(banks[j % 2][:, :], const["heads"][:, :], sq[:, j % 2, :], start=True, stop=True).then_inc(summed, 1)

            @block.vector
            def _(dve):
                for j in range(n):
                    src, gain, dst = tiles[j]
                    dve.wait_ge(rstd, j + 1)
                    dve.scalar_tensor_tensor(out=dst, in0=src, scalar=gain, in1=rs[:, j % 2, :],
                                             op0=ALU.mult, op1=ALU.mult).then_inc(scaled, 1)


def stick_breaking(nc, const, qk, v, mixT):
    OFF = [0, 512, 1024, 896]
    N = 1280
    with Scope(nc) as outer, Scope(nc) as s:
        raw = outer.sb("stick_out", [P, FT, S])
        zt = [s.stack.enter_context(nc.psum_tensor(f"z_ps{i}", [P, 3 * 512], F32)) for i in range(2)]
        avt = [s.ps(f"av_ps{i}") for i in range(2)]
        ln = s.sb("ln_rest", [P, 2, N])
        spl = s.sb("softplus", [P, 2, N])
        wt = s.sb("stick_weights", [P, 2, N])
        z_ready = s.sem("z_ready")
        abs_ready = s.sem("abs_ready")
        e_ready = s.sem("exp_ready")
        l_ready = s.sem("log_ready")
        sp_ready = s.sem("softplus_ready")
        masked = s.sem("softplus_masked")
        suf_ready = s.sem("suffix_ready")
        neg_ready = s.sem("diagonal_masked")
        w_ready = s.sem("stick_weights_ready")
        av_ready = s.sem("stick_av_ready")
        raw_ready = s.sem("stick_out_ready")

        def diagonals(t):
            return [t[:, 0:2 * S].rearrange("p (a n) -> p a n", a=2)[:, :, 0:P],
                    t[:, OFF[3]:OFF[3] + 2 * P].rearrange("p (a n) -> p a n", a=2)]

        def twice(mask):
            return mask.unsqueeze(1).to_broadcast([P, 2, P])

        def blk(t, i, t0=None):
            t0 = i if t0 is None else t0
            return t[:, OFF[i] + (t0 - i) * P:OFF[i] + (TT - i) * P]

        with nc.Block() as block:

            @block.tensor
            def _(pe):
                def scores(h):
                    f, b = h // 2, HD * (h % 2)
                    if h >= 2:
                        pe.wait_ge(w_ready, h - 1)
                    for i in (0, 1, 3, 2):
                        m = pe.matmul(blk(zt[h % 2], i), qk[b:b + HD, FT + f, i * P:(i + 1) * P], qk[b:b + HD, f, i * P:S],
                                      start=(i != 3), stop=True, skip_group_check=True)
                    m.then_inc(z_ready, 1)

                def suffix(h):
                    pe.wait_ge(masked, 2 * (h + 1))
                    for i in range(TT):
                        for j in range(i, TT):
                            m = pe.matmul(blk(zt[h % 2], i, j), const["suffix" if j == i else "minus_ones"][:, :],
                                          blk(spl[:, h % 2, :], j), start=False, stop=True, skip_group_check=True)
                    m.then_inc(suf_ready, 1)

                def values(h):
                    b = HD * (h % 2)
                    pe.wait_ge(w_ready, h + 1)
                    if h >= 4:
                        pe.wait_ge(raw_ready, h // 2 - 1)
                    for i in range(TT):
                        m = pe.matmul(avt[h // 2 % 2][b:b + HD, i * P:S], v[:, i, h * HD:(h + 1) * HD],
                                      blk(wt[:, h % 2, :], i), start=(i == 0), stop=(i == TT - 1))
                    m.then_inc(av_ready, 1)

                scores(0)
                scores(1)
                for h in range(NH):
                    suffix(h)
                    if h >= 1:
                        values(h - 1)
                    if h + 2 < NH:
                        scores(h + 2)
                values(NH - 1)

            @block.vector
            def _(dve):
                def softplus(h):
                    dve.wait_ge(l_ready, h + 1)
                    if h >= 2:
                        dve.wait_ge(suf_ready, h - 1)
                    dve.scalar_tensor_tensor(out=spl[:, h % 2, :], in0=zt[h % 2][:, 0:N], scalar=0.0, in1=ln[:, h % 2, :],
                                             op0=ALU.max, op1=ALU.add).then_inc(sp_ready, 1)

                def mask(h):
                    dve.wait_ge(suf_ready, h + 1)
                    for d in diagonals(zt[h % 2]):
                        dve.tensor_tensor(d, d, twice(const["neg_causal"][:, :]), ALU.add).then_inc(neg_ready, 1)

                softplus(0)
                for h in range(NH):
                    if h + 1 < NH:
                        softplus(h + 1)
                    mask(h)

            @block.gpsimd
            def _(pool):
                for h in range(NH):
                    pool.wait_ge(sp_ready, h + 1)
                    for d in diagonals(spl[:, h % 2, :]):
                        pool.tensor_tensor(d, d, twice(const["causal"][:, 0, :]), ALU.mult).then_inc(masked, 1)

            @block.scalar
            def _(act):
                def log_rest(h):
                    x = ln[:, h % 2, :]
                    act.wait_ge(z_ready, h + 1)
                    if h >= 2:
                        act.wait_ge(sp_ready, h - 1)
                    act.activation(x, zt[h % 2][:, 0:N], ACT.Abs).then_inc(abs_ready, 1)
                    act.wait_ge(abs_ready, h + 1)
                    act.activation(x, x, ACT.Exp, scale=-1.0).then_inc(e_ready, 1)
                    act.wait_ge(e_ready, h + 1)
                    act.activation(x, x, ACT.Ln, bias=1.0).then_inc(l_ready, 1)

                def weights(h):
                    act.wait_ge(neg_ready, 2 * (h + 1))
                    if h >= 2:
                        act.wait_ge(av_ready, h - 1)
                    act.activation(wt[:, h % 2, :], zt[h % 2][:, 0:N], ACT.Exp).then_inc(w_ready, 1)

                act.preload_act_table_set("natural_log_exp_and_others")
                log_rest(0)
                for h in range(NH):
                    if h + 1 < NH:
                        log_rest(h + 1)
                    weights(h)
                    if h % 2 == 0 and h >= 2:
                        f = h // 2 - 1
                        act.wait_ge(av_ready, h)
                        act.activation(raw[:, f, :], avt[f % 2][:, :], ACT.Copy).then_inc(raw_ready, 1)
                act.wait_ge(av_ready, NH)
                act.activation(raw[:, FT - 1, :], avt[(FT - 1) % 2][:, :], ACT.Copy).then_inc(raw_ready, 1)

        s.stack.close()
        g = PARAM_AT["sb_out_g"]
        normalize_heads(nc, const, [(raw[:, f, :], par_col(const, g + f), mixT[:, f, :]) for f in range(FT)],
                        "sbn")


def rwkv_features(nc, A, const, um, R):
    r, k, vv = um[:, 0:FT, :], um[:, FT:2 * FT, :], um[:, 2 * FT:3 * FT, :]
    with Scope(nc) as s:
        wa2 = s.sb("lora_w2_a2", [P, HW])
        g2 = s.sb("lora_g2", [P, HW])
        lora = s.sb("lora_in", [P, 2, S])
        sig = s.sb("decay_sigmoid", [P, FT, S])
        rate = s.sb("rate", [P, FT, S])
        kkn = s.sb("kkn", [P, FT, S])
        cum = s.sb("decay_sums", [P, FT, S])
        e1 = s.sb("e1", [P, FT, S])
        e2 = s.sb("e2", [P, FT, S])
        ones0 = s.sb("chunk_starts", [P, S])
        banks = [s.ps(f"lora_ps{i}") for i in range(8)]
        loaded = s.sem("lora_loaded")
        lora_in = s.sem("lora_in_ready")
        prod = s.sem("lora_product")
        act_st = s.sem("lora_act_stored")
        gate_st = s.sem("gate_stored")
        sq_r = s.sem("kk_squared")
        ss_r = s.sem("kk_summed")
        mx = s.sem("kk_sum_bounded")
        rs_l = s.sem("kk_log")
        rs_r = s.sem("kk_rstd")
        dv = s.sem("rwkv_vector_step")
        ex = s.sem("decay_exp_ready")
        bz = s.sem("bonus_summed")
        start = s.sem("chunk_starts_ready")
        names = {}
        kk_col = PARAM_AT["rw_k_k"]
        with nc.Block() as block:

            @block.sync
            def _(sp):
                sp.dma_start(wa2[0:64, :], A["rw_w2"][0]).then_inc(loaded, 16)
                sp.dma_start(wa2[64:128, :], A["rw_a2"][0]).then_inc(loaded, 16)
                sp.dma_start(g2[:, :], A["rw_g2"][0]).then_inc(loaded, 16)

            @block.vector
            def _(dve):
                n = [0]

                def step(name, ins):
                    n[0] += 1
                    names[name] = n[0]
                    ins.then_inc(dv, 1)
                    return n[0]

                for f in range(FT):
                    dve.wait_ge(ss_r, f + 1)
                    dve.tensor_scalar(e2[:, f, :], banks[f][:, :], 1e-24, None, ALU.max).then_inc(mx, 1)
                dve.wait_ge(start, 2)
                for f in range(FT):
                    dve.wait_ge(act_st, f + 1)
                    a = step("cum", dve.tensor_tensor_scan(cum[:, f, :], ones0[:, :], sig[:, f, :], 0.0, ALU.mult, ALU.add))
                dve.wait_ge(dv, a)
                cum3 = cum[:, :, :].rearrange("p f (c t) -> p (f c) t", t=CH)
                sig3 = sig[:, :, :].rearrange("p f (c t) -> p (f c) t", t=CH)
                a = step("ends", dve.tensor_copy(R["ends"][:, :], cum3[:, :, CH - 1]))
                dve.wait_ge(dv, a)
                ends = R["ends"][:, :].unsqueeze(2).to_broadcast([P, FT * NC, CH])
                a = step("csc", dve.scalar_tensor_tensor(out=cum3, in0=ends, scalar=-0.5, in1=cum3, op0=ALU.mult, op1=ALU.add))
                dve.wait_ge(dv, a)
                step("csx", dve.tensor_tensor(sig3, cum3, sig3, ALU.subtract))
                dve.wait_ge(rs_r, 1)
                for f in range(FT):
                    a = step("kkn", dve.scalar_tensor_tensor(out=kkn[:, f, :], in0=k[:, f, :], scalar=par_col(const, kk_col + f),
                                                             in1=e2[:, f, :], op0=ALU.mult, op1=ALU.mult))
                dve.wait_ge(act_st, 2 * FT)
                for f in range(FT):
                    b = step("fac", dve.tensor_scalar(e1[:, f, :], rate[:, f, :], par_col(const, PARAM_AT["rw_k_a"] + f),
                                                      const["one_minus_ka"][:, f:f + 1], ALU.mult, ALU.add))
                dve.wait_ge(dv, b)
                a = step("k2", dve.tensor_tensor(k, k, e1[:, :, :], ALU.mult))
                dve.wait_ge(dv, a)
                for f in range(FT):
                    step("rk", dve.scalar_tensor_tensor(out=R["bonus"][:, f, :], in0=r[:, f, :], scalar=par_col(const, PARAM_AT["rw_r_k"] + f),
                                                        in1=k[:, f, :], op0=ALU.mult, op1=ALU.mult))
                a = step("b", dve.tensor_tensor(rate[:, :, :], kkn[:, :, :], rate[:, :, :], ALU.mult))
                dve.wait_ge(dv, a)
                names["kkn"] = a
                c4 = lambda x: x.rearrange("p f (c t) -> p (f c) t", t=CH)
                KR = R["kr"]
                dve.wait_ge(ex, 1)
                step("krk", dve.tensor_tensor(KR[:, :, 0, :], c4(kkn[:, :, :]), sig3, ALU.mult))
                dve.wait_ge(ex, 3)
                step("krr", dve.tensor_tensor(KR[:, :, 1, :], c4(r), c4(e1[:, :, :]), ALU.mult))
                step("bh", dve.tensor_tensor(R["bh"][:, :, :], rate[:, :, :], e2[:, :, :], ALU.mult))
                for f in range(FT):
                    dve.wait_ge(bz, f + 1)
                    step("bonus", dve.tensor_tensor(R["bonus"][:, f, :], banks[f][:, :], vv[:, f, :], ALU.mult))

            @block.gpsimd
            def _(pool):
                pool.memset(ones0[:, :], 1.0).then_inc(start, 1)
                pool.wait_ge(start, 1)
                pool.memset(ones0[:, 0:S:CH], 0.0).then_inc(start, 1)
                pool.wait_ge(dv, names["rk"])
                pool.wait_ge(ex, 3)
                pool.tensor_tensor(R["kh"][:, :, :], k, e2[:, :, :], ALU.mult).then_inc(start, 1)

            @block.tensor
            def _(pe):
                pe.wait_ge(sq_r, FT)
                for f in range(FT):
                    pe.matmul(banks[f][:, :], const["heads"][:, :], e1[:, f, :], start=True, stop=True).then_inc(ss_r, 1)
                pe.wait_ge(loaded, 48)
                pe.wait_ge(lora_in, 3)
                for f in range(FT):
                    cols = slice(f * P, (f + 1) * P)
                    pe.matmul(banks[4 + f][:, :], wa2[0:64, cols], lora[0:64, 0, :], start=True, stop=True).then_inc(prod, 1)
                for f in range(FT):
                    cols = slice(f * P, (f + 1) * P)
                    pe.wait_ge(mx, f + 1)
                    pe.matmul(banks[f][:, :], wa2[64:128, cols], lora[64:128, 0, :], start=True, stop=True).then_inc(prod, 1)
                for f in range(FT):
                    cols = slice(f * P, (f + 1) * P)
                    pe.wait_ge(act_st, f + 1)
                    pe.matmul(banks[4 + f][:, :], g2[:, cols], lora[:, 1, :], start=True, stop=True).then_inc(prod, 1)
                pe.wait_ge(dv, names["rk"])
                for f in range(FT):
                    pe.wait_ge(act_st, 4 + f + 1)
                    pe.matmul(banks[f][:, :], const["heads"][:, :], R["bonus"][:, f, :], start=True, stop=True).then_inc(bz, 1)

            @block.scalar
            def _(act):
                for f in range(FT):
                    act.activation(e1[:, f, :], k[:, f, :], ACT.Square, scale=par_col(const, kk_col + f)).then_inc(sq_r, 1)
                act.activation(lora[0:64, 0, :], um[0:64, 3 * FT, :], ACT.Tanh).then_inc(lora_in, 1)
                act.activation(lora[64:128, 0, :], um[64:128, 3 * FT, :], ACT.Copy).then_inc(lora_in, 1)
                act.activation(lora[:, 1, :], um[:, 3 * FT + 1, :], ACT.Sigmoid).then_inc(lora_in, 1)
                for f in range(FT):
                    act.wait_ge(prod, f + 1)
                    act.activation(sig[:, f, :], banks[4 + f][:, :], ACT.Sigmoid,
                                   bias=par_col(const, PARAM_AT["rw_w0"] + f)).then_inc(act_st, 1)
                for f in range(FT):
                    act.wait_ge(prod, 4 + f + 1)
                    act.activation(rate[:, f, :], banks[f][:, :], ACT.Sigmoid,
                                   bias=par_col(const, PARAM_AT["rw_a0"] + f)).then_inc(act_st, 1)
                act.preload_act_table_set("natural_log_exp_and_others")
                act.wait_ge(mx, FT)
                act.activation(e2[:, :, :], e2[:, :, :], ACT.Ln, scale=float(2.0 ** LOG_BITS)).then_inc(rs_l, 1)
                act.wait_ge(rs_l, 1)
                act.activation(e2[:, :, :], e2[:, :, :], ACT.Exp, scale=-0.5, bias=const["log_shift"][:, :]).then_inc(rs_r, 1)
                for f in range(FT):
                    act.wait_ge(prod, 8 + f + 1)
                    act.activation(R["gate"][:, f, :], banks[4 + f][:, :], ACT.Copy).then_inc(gate_st, 1)
                act.wait_ge(dv, names["csx"])
                act.activation(sig[:, :, :], sig[:, :, :], ACT.Exp, scale=-DECAY).then_inc(ex, 1)
                act.wait_ge(dv, names["kkn"])
                act.activation(e1[:, :, :], cum[:, :, :], ACT.Exp, scale=-DECAY).then_inc(ex, 1)
                act.activation(e2[:, :, :], cum[:, :, :], ACT.Exp, scale=DECAY).then_inc(ex, 1)
                act.activation(R["mid"][:, :], R["ends"][:, :], ACT.Exp, scale=-0.5 * DECAY).then_inc(ex, 1)


def rwkv_chunks(nc, const, um, R, scratch):
    LEVELS = 7
    G = 2 * NC
    vT = um[:, 2 * FT:3 * FT, :]
    with Scope(nc) as s:
        tok = s.sb("token_side", [P, 2, NC, 5, P])
        KK, BV, V, B, K = range(5)
        sc = s.sb("chunk_scores", [P, G, 4, CH])
        x, xt, u, gh = (scratch[:, i * G * CH:(i + 1) * G * CH].rearrange("p (g t) -> p g t", g=G) for i in range(4))
        gh = gh.rearrange("p g (k n) -> p g k n", k=2)
        s_bank = [s.ps(f"score_ps{i}") for i in range(2)]
        l_bank = [[s.ps(f"level_ps{q}{i}") for i in range(2)] for q in range(2)]
        f_bank = [s.ps(f"final_ps{i}") for i in range(2)]
        sc_bank = s_bank + l_bank[0]
        kk_st = s.sem("kk_tokens_stored")
        tok_ready, tok_st = s.sem("tokens_turned"), s.sem("tokens_stored")
        sc_ready, sc_st = s.sem("scores_ready"), s.sem("scores_stored")
        bv_ready, bv_st = s.sem("bv_ready"), s.sem("bv_stored")
        u_ready, u_st = s.sems("u_ready", 2), s.sems("u_stored", 2)
        xu_ready, ux_ready = s.sems("xu_ready", 2), s.sems("ux_ready", 2)
        x_st, xt_st = s.sems("x_stored", 2), s.sems("xt_stored", 2)
        gh_ready, gh_st = s.sem("gh_ready"), s.sem("gh_stored")
        qo_ready, mn_ready = s.sem("q_o_ready"), s.sem("m_n_ready")
        q_st, o_st, mn_st = s.sem("q_stored"), s.sem("o_stored"), s.sem("m_n_stored")
        ident = const["ident"][:, :]
        with nc.Block() as block:

            @block.tensor
            def _(pe):
                for f in range(FT):
                    t = tok[:, f % 2]
                    for c in range(NC):
                        i = NC * f + c
                        bank = f_bank[c % 2]
                        if c >= 2:
                            pe.wait_ge(tok_st, i - 1)
                        elif f:
                            pe.wait_ge(gh_st, 2 * f)
                            pe.wait_ge(q_st, 2 * f)
                            pe.wait_ge(o_st, 2 * f)
                        cs = slice(c * CH, (c + 1) * CH)
                        for j, src in enumerate((R["kr"][:, i, 0, :], vT[:, f, cs], R["bh"][:, f, cs], R["kh"][:, f, cs])):
                            m = pe.transpose(bank[:, j * P:(j + 1) * P], src, ident)
                        m.then_inc(tok_ready, 1)
                    if f:
                        pe.wait_ge(bv_st, f)
                        pe.wait_ge(mn_st, 2 * f)
                    for c in range(NC):
                        if c >= 2:
                            pe.wait_ge(sc_st, G * f + 2 * c - 2)
                        cs = slice(c * CH, (c + 1) * CH)
                        for j, src in enumerate((R["bh"], R["kh"])):
                            for odd in range(2):
                                b = HD * odd
                                m = pe.matmul(sc_bank[(2 * c + odd) % 4][:, j * 2 * CH:(j + 1) * 2 * CH], src[b:b + HD, f, cs],
                                              R["kr"][b:b + HD, NC * f + c, :, :], start=True, stop=True)
                                if j:
                                    m.then_inc(sc_ready, 1)
                    pe.wait_ge(sc_st, G * (f + 1))
                    pe.wait_ge(kk_st, NC * (f + 1))
                    pe.wait_ge(tok_st, NC * (f + 1))
                    for g in range(G):
                        m = pe.matmul(s_bank[0][:, g * HD:(g + 1) * HD], sc[:, g, 2, :], t[:, g // 2, V, (g % 2) * HD:(g % 2 + 1) * HD],
                                      start=True, stop=True)
                    m.then_inc(bv_ready, 1)
                    for l in range(LEVELS):
                        for q in range(2):
                            if l:
                                pe.wait_ge(x_st[q], 6 * f + l)
                            for g in range(4 * q, 4 * q + 4):
                                cols = slice((g % 4) * CH, (g % 4 + 1) * CH)
                                m = pe.matmul(l_bank[q][0][:, cols], sc[:, g, 0, :], x[:, g, :] if l else ident, start=True, stop=True)
                            m.then_inc(u_ready[q], 1)
                        for q in range(2):
                            pe.wait_ge(u_st[q], LEVELS * f + l + 1)
                            if l:
                                pe.wait_ge(xt_st[q], LEVELS * f + l)
                            if 0 < l < LEVELS - 1:
                                for g in range(4 * q, 4 * q + 4):
                                    cols = slice((g % 4) * CH, (g % 4 + 1) * CH)
                                    m = pe.matmul(l_bank[q][0][:, cols], xt[:, g, :], u[:, g, :], start=True, stop=True)
                                m.then_inc(xu_ready[q], 1)
                            for g in range(4 * q, 4 * q + 4):
                                cols = slice((g % 4) * CH, (g % 4 + 1) * CH)
                                m = pe.matmul(l_bank[q][1][:, cols], u[:, g, :], xt[:, g, :] if l else ident, start=True, stop=True)
                            m.then_inc(ux_ready[q], 1)
                    for q in range(2):
                        pe.wait_ge(xt_st[q], LEVELS * (f + 1))
                        pe.wait_ge(bv_st, f + 1)
                        if q:
                            pe.wait_ge(gh_st, 2 * f + q)
                        for g in range(4 * q, 4 * q + 4):
                            b = HD * (g % 2)
                            m = pe.matmul(f_bank[0][:, (g % 4) * P:(g % 4 + 1) * P], xt[:, g, :], t[:, g // 2, KK:BV + 1, b:b + HD],
                                          start=True, stop=True)
                        m.then_inc(gh_ready, 1)
                        pe.wait_ge(gh_st, 2 * f + q + 1)
                        if q:
                            pe.wait_ge(q_st, 2 * f + q)
                            pe.wait_ge(o_st, 2 * f + q)
                            pe.wait_ge(mn_st, 2 * f + q)
                        for g in range(4 * q, 4 * q + 4):
                            c, b = g // 2, HD * (g % 2)
                            qo = f_bank[1][b:b + HD, (c % 2) * 2 * CH:(c % 2 + 1) * 2 * CH]
                            pe.matmul(qo[:, 0:CH], gh[:, g, 0, :], sc[:, g, 1, :], start=True, stop=True)
                            pe.matmul(qo[:, CH:2 * CH], gh[:, g, 1, :], sc[:, g, 1, :], start=True, stop=False)
                            m = pe.matmul(qo[:, CH:2 * CH], t[:, c, V, b:b + HD], sc[:, g, 3, :], start=False, stop=True)
                        m.then_inc(qo_ready, 1)
                        for g in range(4 * q, 4 * q + 4):
                            c, b = g // 2, HD * (g % 2)
                            mn = s_bank[1][b:b + HD, (c % 2) * 2 * HD:(c % 2 + 1) * 2 * HD]
                            pe.matmul(mn[:, 0:HD], gh[:, g, 0, :], t[:, c, B, b:b + HD], start=True, stop=True)
                            pe.matmul(mn[:, HD:2 * HD], t[:, c, B, b:b + HD], gh[:, g, 1, :], start=True, stop=False)
                            m = pe.matmul(mn[:, HD:2 * HD], t[:, c, K, b:b + HD], t[:, c, V, b:b + HD], start=False, stop=True)
                        m.then_inc(mn_ready, 1)

            @block.scalar
            def _(act):
                for f in range(FT):
                    for c in range(NC):
                        i = NC * f + c
                        act.wait_ge(tok_ready, i + 1)
                        bank = f_bank[c % 2][:, :].rearrange("p (j n) -> p j n", j=4)
                        act.activation(tok[:, f % 2, c, KK, :], bank[:, 0, :], ACT.Copy).then_inc(kk_st, 1)
                        act.activation(tok[:, f % 2, c, V:K + 1, :], bank[:, 1:4, :], ACT.Copy).then_inc(tok_st, 1)
                    act.wait_ge(bv_ready, f + 1)
                    act.activation(tok[:, f % 2, :, BV, :], s_bank[0][:, :].rearrange("p (c n) -> p c n", c=NC), ACT.Copy).then_inc(bv_st, 1)
                    for q in range(2):
                        act.wait_ge(gh_ready, 2 * f + q + 1)
                        act.activation(gh[:, 4 * q:4 * q + 4, :, :].rearrange("p g k n -> p (g k n)"), f_bank[0][:, :], ACT.Copy,
                                       scale=-1.0).then_inc(gh_st, 1)
                        act.wait_ge(q_st, 2 * f + q + 1)
                        qo = f_bank[1][:, :].rearrange("p (c k t) -> p c k t", c=2, k=2)
                        act.activation(R["o"][:, f, 2 * q * CH:2 * (q + 1) * CH].rearrange("p (c t) -> p c t", c=2), qo[:, :, 1, :],
                                       ACT.Copy).then_inc(o_st, 1)
                        act.wait_ge(mn_ready, 2 * f + q + 1)
                        i = NC * f + 2 * q
                        act.activation(R["mn"][:, i:i + 2, :, :].rearrange("p c k n -> p (c k n)"), s_bank[1][:, 0:4 * HD], ACT.Copy).then_inc(mn_st, 1)

            @block.vector
            def _(dve):
                for f in range(FT):
                    if f:
                        dve.wait_ge(mn_ready, 2 * f)
                        dve.wait_ge(qo_ready, 2 * f)
                    for g in range(G):
                        dve.wait_ge(sc_ready, G * f + g + 1)
                        dve.tensor_tensor(sc[:, g, :, :].rearrange("p k t -> p (k t)"), sc_bank[g % 4][:, :],
                                          const["causal"][:, :, :].rearrange("p k t -> p (k t)"), ALU.mult).then_inc(sc_st, 1)
                    ids = const["ident"][:, :].unsqueeze(1).to_broadcast([P, 4, CH])
                    for l in range(LEVELS):
                        lv = const["level"][:, l, :].unsqueeze(1).to_broadcast([P, 4, CH])
                        for q in range(2):
                            gs = slice(4 * q, 4 * q + 4)
                            bank = [l_bank[q][j][:, :].rearrange("p (g t) -> p g t", g=4) for j in range(2)]
                            dve.wait_ge(u_ready[q], LEVELS * f + l + 1)
                            if l:
                                dve.wait_ge(ux_ready[q], LEVELS * f + l)
                            dve.tensor_tensor(u[:, gs, :], bank[0], lv, ALU.mult).then_inc(u_st[q], 1)
                        for q in range(2):
                            gs = slice(4 * q, 4 * q + 4)
                            bank = [l_bank[q][j][:, :].rearrange("p (g t) -> p g t", g=4) for j in range(2)]
                            if l == 0:
                                dve.wait_ge(u_st[q], LEVELS * f + 1)
                                dve.tensor_tensor(x[:, gs, :], ids, u[:, gs, :], ALU.subtract).then_inc(x_st[q], 1)
                            elif l < LEVELS - 1:
                                dve.wait_ge(xu_ready[q], 5 * f + l)
                                dve.tensor_tensor(x[:, gs, :], x[:, gs, :], bank[0], ALU.subtract).then_inc(x_st[q], 1)
                            dve.wait_ge(ux_ready[q], LEVELS * f + l + 1)
                            dve.tensor_tensor(xt[:, gs, :], xt[:, gs, :] if l else ids, bank[1], ALU.subtract).then_inc(xt_st[q], 1)
                    for q in range(2):
                        dve.wait_ge(qo_ready, 2 * f + q + 1)
                        qo = f_bank[1][:, :].rearrange("p (c k t) -> p c k t", c=2, k=2)
                        i = NC * f + 2 * q
                        dve.tensor_tensor(R["q"][:, f, 2 * q * CH:2 * (q + 1) * CH].rearrange("p (c t) -> p c t", c=2), qo[:, :, 0, :],
                                          R["kr"][:, i:i + 2, 1, :], ALU.add).then_inc(q_st, 1)


def rwkv_output(nc, const, R, mixT, next_w):
    with Scope(nc) as s:
        st = s.sb("chunk_state", [P, NC, FT, HD])
        z = s.sb("state_sum", [P, FT, HD])
        mm = s.sb("mid_products", [P, FT, NC])
        xc = s.sb("centred", [P, 2, S])
        sq = s.sb("centred_sq", [P, 2, S])
        rs = s.sb("group_rstd", [P, 2, S])
        z_bank = s.ps("state_ps")
        o_bank = [s.ps(f"out_ps{i}") for i in range(2)]
        m_bank = [s.ps(f"mean_ps{i}") for i in range(2)]
        v_bank = [s.ps(f"var_ps{i}") for i in range(2)]
        step_ready = s.sem("state_product_ready")
        zs = s.sem("state_step")
        o_ready, o_st = s.sem("out_ready"), s.sem("out_stored")
        mean, cent, sqd, var, lg, rstd, fin = (s.sem("group_" + n) for n in ("mean", "centred", "squared", "var", "log", "rstd", "done"))
        mid = R["mid"][:, :].rearrange("p (f c) -> p f c", c=NC)
        mn = R["mn"][:, :, :, :].rearrange("p (f c) k n -> p f c k n", c=NC)
        with nc.Block() as block:

            @block.sync
            def _(sp):
                for n in range(2):
                    next_w.load(sp, n)

            @block.tensor
            def _(pe):
                for c in range(1, NC - 1):
                    pe.wait_ge(zs, 1 + 3 * (c - 1) + 1)
                    for f in range(FT):
                        for b in (0, HD):
                            m = pe.matmul(z_bank[b:b + HD, f * HD:(f + 1) * HD], R["mn"][b:b + HD, f * NC + c, 0, :],
                                          st[b:b + HD, c, f, :], start=True, stop=True)
                    m.then_inc(step_ready, 1)
                pe.wait_ge(zs, 1 + 3 * (NC - 2) + 1)
                for j in range(FT + 2):
                    if j < FT:
                        if j >= 2:
                            pe.wait_ge(o_st, j - 1)
                        for c in range(1, NC):
                            for b in (0, HD):
                                m = pe.matmul(o_bank[j % 2][b:b + HD, c * CH:(c + 1) * CH], st[b:b + HD, c, j, :],
                                              R["q"][b:b + HD, j, c * CH:(c + 1) * CH], start=True, stop=True)
                        m.then_inc(o_ready, 1)
                    if 0 <= j - 1 < FT:
                        i = j - 1
                        pe.wait_ge(o_st, i + 1)
                        if i >= 2:
                            pe.wait_ge(cent, i - 1)
                        pe.matmul(m_bank[i % 2][:, :], const["heads"][:, :], R["o"][:, i, :], start=True, stop=True).then_inc(mean, 1)
                    if 0 <= j - 2 < FT:
                        i = j - 2
                        pe.wait_ge(sqd, i + 1)
                        if i >= 2:
                            pe.wait_ge(lg, i - 1)
                        pe.matmul(v_bank[i % 2][:, :], const["heads"][:, :], sq[:, i % 2, :], start=True, stop=True).then_inc(var, 1)

            @block.vector
            def _(dve):
                def bc(f3):
                    return f3.unsqueeze(2).to_broadcast([P, FT, HD])

                dve.tensor_tensor(mm[:, :, 0:NC - 1], mid[:, :, 0:NC - 1], mid[:, :, 1:NC], ALU.mult).then_inc(zs, 1)
                dve.wait_ge(zs, 1)
                dve.tensor_tensor(st[:, 1, :, :], mn[:, :, 0, 1, :], bc(mm[:, :, 0]), ALU.mult).then_inc(zs, 1)
                n = 2
                for c in range(1, NC - 1):
                    dve.wait_ge(zs, n)
                    dve.wait_ge(step_ready, c)
                    dve.tensor_tensor(z[:, :, :], z_bank[:, 0:FT * HD].rearrange("p (f n) -> p f n", f=FT), st[:, c, :, :], ALU.add).then_inc(zs, 1)
                    dve.wait_ge(zs, n + 1)
                    dve.tensor_tensor(z[:, :, :], z[:, :, :], mn[:, :, c, 1, :], ALU.add).then_inc(zs, 1)
                    dve.wait_ge(zs, n + 2)
                    dve.tensor_tensor(st[:, c + 1, :, :], z[:, :, :], bc(mm[:, :, c]), ALU.mult).then_inc(zs, 1)
                    n += 3
                w, bcol = PARAM_AT["rw_ln_w"], PARAM_AT["rw_ln_b"]
                for j in range(FT + 2):
                    if j < FT:
                        dve.wait_ge(o_ready, j + 1)
                        o = R["o"][:, j, CH:S]
                        dve.tensor_tensor(o, o_bank[j % 2][:, CH:S], o, ALU.add).then_inc(o_st, 1)
                    if 0 <= j - 1 < FT:
                        i = j - 1
                        dve.wait_ge(mean, i + 1)
                        if i >= 2:
                            dve.wait_ge(fin, 3 * (i - 1))
                            dve.wait_ge(sqd, i - 1)
                        dve.scalar_tensor_tensor(out=xc[:, i % 2, :], in0=m_bank[i % 2][:, :], scalar=-1.0 / HD,
                                                 in1=R["o"][:, i, :], op0=ALU.mult, op1=ALU.add).then_inc(cent, 1)
                    if 0 <= j - 2 < FT:
                        i = j - 2
                        dve.wait_ge(rstd, i + 1)
                        dve.wait_ge(cent, i + 1)
                        y = xc[:, i % 2, :]
                        dve.scalar_tensor_tensor(out=y, in0=y, scalar=par_col(const, w + i), in1=rs[:, i % 2, :],
                                                 op0=ALU.mult, op1=ALU.mult).then_inc(fin, 1)
                        dve.wait_ge(fin, 3 * i + 1)
                        dve.scalar_tensor_tensor(out=y, in0=y, scalar=par_col(const, bcol + i), in1=R["bonus"][:, i, :],
                                                 op0=ALU.add, op1=ALU.add).then_inc(fin, 1)
                        dve.wait_ge(fin, 3 * i + 2)
                        dve.tensor_tensor(mixT[:, FT + i, :], y, R["gate"][:, i, :], ALU.mult).then_inc(fin, 1)

            @block.scalar
            def _(act):
                act.preload_act_table_set("natural_log_exp_and_others")
                for i in range(FT):
                    act.wait_ge(cent, i + 1)
                    if i >= 2:
                        act.wait_ge(var, i - 1)
                    act.activation(sq[:, i % 2, :], xc[:, i % 2, :], ACT.Square).then_inc(sqd, 1)
                    act.wait_ge(var, i + 1)
                    if i >= 2:
                        act.wait_ge(fin, 3 * (i - 2) + 1)
                    act.activation(rs[:, i % 2, :], v_bank[i % 2][:, :], ACT.Ln, scale=1.0 / HD, bias=const["gn_eps"][:, :]).then_inc(lg, 1)
                    act.wait_ge(lg, i + 1)
                    act.activation(rs[:, i % 2, :], rs[:, i % 2, :], ACT.Exp, scale=-0.5).then_inc(rstd, 1)


def out_projection(nc, const, wts, xT, h, tag, out=None):
    NU = len(wts.cols)
    with Scope(nc) as s:
        wts.place_parts(s)
        x = [s.sb(tag + "_x_high", [P, KC, S], F32R), s.sb(tag + "_x_low", [P, KC, S], F32R)]
        banks = [s.ps(f"{tag}_ps{i}") for i in range(8)]
        x_high, x_low, ready, added, stored = (s.sem(f"{tag}_{n}") for n in ("x_high", "x_low", "ready", "added", "stored"))
        wts.used = lambda n: (ready, TT * (n + 1))
        with nc.Block() as block:

            @block.sync
            def _(sp):
                for u in range(2, NU):
                    wts.load(sp, u)
                if out is not None:
                    for u in range(NU):
                        cols = slice(u * UNIT, (u + 1) * UNIT)
                        sp.wait_ge(added, TT * (u + 1))
                        sp.dma_start(out.rearrange("(c p) d -> p c d", p=P)[:, :, cols], h[:, :, cols]).then_inc(stored, 16)
                    sp.wait_ge(stored, 16 * NU)

            @block.tensor
            def _(pe):
                for u in range(NU):
                    wts.wait(pe, u)
                    if u >= 2:
                        pe.wait_ge(added, TT * (u - 1))
                    for k in range(KC):
                        if u == 0:
                            pe.wait_ge(x_low, k + 1)
                        for c in range(TT):
                            for a, b in ((0, 0), (0, 1), (1, 0)):
                                m = pe.matmul(banks[TT * (u % 2) + c][:, 0:UNIT], x[a][:, k, c * P:(c + 1) * P],
                                              wts.parts(u, k, slice(0, UNIT))[b], start=(k == 0 and a + b == 0),
                                              stop=(k == KC - 1 and a == 1))
                            if k == KC - 1:
                                m.then_inc(ready, 1)

            @block.scalar
            def _(act):
                wts.split_high(act, 0)
                for k in range(KC):
                    act.activation(x[0][:, k, :], xT[:, k, :], ACT.Copy).then_inc(x_high, 1)
                for u in range(1, NU):
                    wts.split_high(act, u)

            @block.gpsimd
            def _(pool):
                for k in range(KC):
                    pool.wait_ge(x_high, k + 1)
                    pool.tensor_tensor(x[1][:, k, :], xT[:, k, :], x[0][:, k, :], ALU.subtract).then_inc(x_low, 1)

            @block.vector
            def _(dve):
                wts.split_low(dve, 0)
                for u in range(NU):
                    wts.split_low(dve, u + 1)
                    for c in range(TT):
                        dve.wait_ge(ready, TT * u + c + 1)
                        dst = h[:, c, u * UNIT:(u + 1) * UNIT]
                        dve.tensor_tensor(dst, banks[TT * (u % 2) + c][:, 0:UNIT], dst, ALU.add).then_inc(added, 1)


def route(nc, A, const, h, xn_dram, list_dram, M):
    NL = NG + NE
    MADE = 10
    with Scope(nc) as s:
        sq = s.sb("ffn_sq", [P, D])
        ss = s.sb("ffn_ss", [P, TT])
        rs = s.sb("ffn_rstd", [P, TT])
        xg = s.sb("ffn_in", [P, TT, D])
        xT = s.sb("ffn_in_t", [P, KC, S])
        wr = s.sb("router_w", [P, KC, NL])
        br = s.sb("router_b", [P, NL])
        lg = s.sb("router_logits", [P, TT, NL])
        desc = s.sb("descending", [P, EPG])
        base = s.sb("list_base", [P, NE])
        steps = s.sb("round_limits", [P, S // CAP])
        ids = s.sb("token_ids", [P, 2, TT, 2], I32)
        empty = s.sb("empty_list", [P, LIST // P, 2], I32)
        t4 = s.sb("t4", [P, TT, NG])
        grp = s.sb("group_hot", [P, TT, NG])
        ex4 = s.sb("group_exp", [P, TT, NG])
        gm = s.sb("group_max", [P, TT])
        a1 = s.sb("a1", [P, TT])
        gval = s.sb("group_prob", [P, TT])
        pick = s.sb("picked", [P, TT, NG, EPG])
        sel = s.sb("selected", [P, TT, EPG])
        t8 = s.sb("t8", [P, TT, EPG])
        hot = [s.sb(f"expert_hot{i}", [P, TT, EPG]) for i in range(2)]
        top = [s.sb(f"expert_top{i}", [P, TT]) for i in range(2)]
        p2 = s.sb("second_exp", [P, TT])
        full = [s.sb(f"expert_full{i}", [P, TT, NG, EPG]) for i in range(2)]
        both = s.sb("expert_both", [P, TT, NE])
        nboth = s.sb("expert_both_neg", [P, TT, NE])
        places = s.sb("places", [P, 2, TT])
        reached = s.sb("rounds_reached", [P, 2 * TT, S // CAP])
        t32 = s.sb("t32", [P, TT, NE])
        slotf = s.sb("slots_float", [P, 2, TT])
        tot = s.sb("totals", [P, NE])
        most = s.sb("most", [P, 1])
        rf = s.sb("rounds_float", [P, 1])
        t_bank = [s.ps(f"ffn_ps{i}") for i in range(4)]
        l_bank = s.ps("logit_ps")
        r_bank = s.ps("rank_ps")
        squared, rstd, scaled = s.sem("ffn_squares"), s.sem("ffn_rstd_ready"), s.sem("ffn_scaled")
        turned, even_st, odd_st = s.sem("ffn_turned"), s.sem("ffn_even_stored"), s.sem("ffn_odd_stored")
        loaded, xn_st, zeroed, made = s.sem("router_loaded"), s.sem("ffn_in_stored"), s.sem("list_zeroed"), s.sem("router_constants")
        logits, ranks, dv, ac = s.sem("logits_ready"), s.sem("ranks_ready"), s.sem("route_step"), s.sem("route_exp")
        put = s.sem("ids_scattered")
        slots_ready = s.sem("slots_ready")
        with nc.Block() as block:

            @block.vector
            def _(dve):
                n = [0]

                def step(ins, name=None):
                    n[0] += 1
                    if name:
                        M[name] = n[0]
                    ins.then_inc(dv, 1)
                    dve.wait_ge(dv, n[0])

                def wide(x, k):
                    return x.unsqueeze(2).to_broadcast([P, TT, k])

                def row(x, k):
                    return x[:, 0:k].unsqueeze(1).to_broadcast([P, TT, k])

                def first_of_max(vals, best, tmp, hot_out, k):
                    step(dve.tensor_reduce(best, vals, AX_X, ALU.max))
                    step(dve.tensor_tensor(tmp, vals, wide(best, k), ALU.is_ge))
                    step(dve.tensor_tensor(tmp, tmp, row(desc, k), ALU.mult))
                    step(dve.tensor_reduce(a1[:, :], tmp, AX_X, ALU.max))
                    step(dve.tensor_tensor(hot_out, tmp, wide(a1[:, :], k), ALU.is_equal))

                dve.wait_ge(squared, TT)
                dve.tensor_scalar(ss[:, :], ss[:, :], 1.0 / D, EPS, ALU.mult, ALU.add).then_inc(rstd, 1)
                dve.wait_ge(rstd, 2)
                dve.reciprocal(rs[:, :], ss[:, :]).then_inc(rstd, 1)
                dve.wait_ge(rstd, 3)
                dve.wait_ge(const["row_params"], 32)
                for c in range(TT):
                    dve.scalar_tensor_tensor(out=xg[:, c, :], in0=h[:, c, :], scalar=rs[:, c:c + 1], in1=const["ffn_g"][:, :],
                                             op0=ALU.mult, op1=ALU.mult).then_inc(scaled, 1)
                for k in range(1, KC, 2):
                    dve.wait_ge(turned, k + 1)
                    dve.tensor_copy(xT[:, k, :], t_bank[k % 4][:, :]).then_inc(odd_st, 1)
                dve.wait_ge(logits, 1)
                dve.wait_ge(made, MADE)
                step(dve.tensor_tensor(lg[:, :, :], l_bank[:, 0:TT * NL].rearrange("p (c n) -> p c n", c=TT),
                                       br[:, :].unsqueeze(1).to_broadcast([P, TT, NL]), ALU.add))
                first_of_max(lg[:, :, 0:NG], gm[:, :], t4[:, :, :], grp[:, :, :], NG)
                step(dve.tensor_tensor(t4[:, :, :], lg[:, :, 0:NG], wide(gm[:, :], NG), ALU.subtract), "group_less")
                dve.wait_ge(ac, 1)
                step(dve.tensor_reduce(gval[:, :], ex4[:, :, :], AX_X, ALU.add))
                step(dve.reciprocal(gval[:, :], gval[:, :]))
                step(dve.tensor_tensor(pick[:, :, :, :], lg[:, :, NG:NL].rearrange("p c (g e) -> p c g e", g=NG),
                                       grp[:, :, :].unsqueeze(3).to_broadcast([P, TT, NG, EPG]), ALU.mult))
                step(dve.tensor_reduce(sel[:, :, :], pick[:, :, :, :].rearrange("p c g e -> p c e g"), AX_X, ALU.add))
                first_of_max(sel[:, :, :], top[0][:, :], t8[:, :, :], hot[0][:, :, :], EPG)
                step(dve.tensor_scalar(t8[:, :, :], hot[0][:, :, :], NEG, None, ALU.mult))
                step(dve.tensor_tensor(sel[:, :, :], sel[:, :, :], t8[:, :, :], ALU.add))
                first_of_max(sel[:, :, :], top[1][:, :], t8[:, :, :], hot[1][:, :, :], EPG)
                step(dve.tensor_tensor(p2[:, :], top[1][:, :], top[0][:, :], ALU.subtract), "top_less")
                for j in range(2):
                    step(dve.tensor_tensor(full[j][:, :, :, :], grp[:, :, :].unsqueeze(3).to_broadcast([P, TT, NG, EPG]),
                                           hot[j][:, :, :].unsqueeze(2).to_broadcast([P, TT, NG, EPG]), ALU.mult))
                flat = [full[j][:, :, :, :].rearrange("p c g e -> p c (g e)") for j in range(2)]
                step(dve.tensor_tensor(both[:, :, :], flat[0], flat[1], ALU.add))
                step(dve.tensor_scalar(nboth[:, :, :], both[:, :, :], -1.0, None, ALU.mult), "both")
                dve.wait_ge(ac, 2)
                step(dve.tensor_scalar(a1[:, :], p2[:, :], 1.0, None, ALU.add))
                step(dve.reciprocal(a1[:, :], a1[:, :]))
                step(dve.tensor_tensor(M["weights"][:, 0, :], gval[:, :], a1[:, :], ALU.mult))
                step(dve.tensor_tensor(M["weights"][:, 1, :], M["weights"][:, 0, :], p2[:, :], ALU.mult))
                dve.wait_ge(ranks, 1)
                rank = r_bank[:, 0:TT * NE].rearrange("p (c e) -> p c e", c=TT)
                for j in range(2):
                    step(dve.tensor_tensor(t32[:, :, :], rank, flat[j], ALU.mult))
                    step(dve.tensor_reduce(places[:, j, :], t32[:, :, :], AX_X, ALU.add))
                    step(dve.tensor_tensor(t32[:, :, :], base[:, :].unsqueeze(1).to_broadcast([P, TT, NE]), flat[j], ALU.mult))
                    step(dve.tensor_reduce(slotf[:, j, :], t32[:, :, :], AX_X, ALU.add))
                step(dve.tensor_tensor(slotf[:, :, :], slotf[:, :, :], places[:, :, :], ALU.add))
                pl = places[:, :, :].rearrange("p j c -> p (j c)")
                step(dve.tensor_tensor(reached[:, :, :], pl.unsqueeze(2).to_broadcast([P, 2 * TT, S // CAP]),
                                       steps[:, :].unsqueeze(1).to_broadcast([P, 2 * TT, S // CAP]), ALU.is_ge))
                step(dve.tensor_reduce(pl, reached[:, :, :], AX_X, ALU.add))
                step(dve.scalar_tensor_tensor(out=slotf[:, :, :].rearrange("p j c -> p (j c)"), in0=pl, scalar=float((NE - 1) * CAP),
                                              in1=slotf[:, :, :].rearrange("p j c -> p (j c)"), op0=ALU.mult, op1=ALU.add))
                step(dve.tensor_copy(tot[:, :], r_bank[:, TT * NE:(TT + 1) * NE]))
                step(dve.tensor_reduce(most[:, :], tot[:, :], AX_X, ALU.max))
                step(dve.tensor_scalar(steps[:, :], steps[:, :], most[:, 0:1], None, ALU.is_lt))
                step(dve.tensor_reduce(rf[:, :], steps[:, :], AX_X, ALU.add))
                step(dve.tensor_copy(M["rounds"][:, 0:1], rf[:, :]))
                dve.tensor_copy(M["slots"][:, :, :], slotf[:, :, :]).then_inc(slots_ready, 1)

            @block.sync
            def _(sp):
                sp.dma_start(wr[:, :, 0:NG], A["router_grp_w"].rearrange("l (k p) n -> p (l k) n", p=P)).then_inc(loaded, 16)
                sp.dma_start(wr[:, :, NG:NL], A["router_exp_w"].rearrange("l (k p) n -> p (l k) n", p=P)).then_inc(loaded, 16)
                sp.dma_start(br[:, 0:NG], A["router_grp_b"].broadcast_to([P, NG])).then_inc(loaded, 16)
                sp.dma_start(br[:, NG:NL], A["router_exp_b"].broadcast_to([P, NE])).then_inc(loaded, 16)
                for j in range(NB):
                    load_expert(sp, A, M, j, j)
                sp.wait_ge(made, MADE)
                sp.dma_start(list_dram.rearrange("(p n) a -> p (n a)", p=P),
                             empty[:, :, :].rearrange("p n a -> p (n a)")).then_inc(zeroed, 16)
                for c in range(TT):
                    sp.wait_ge(scaled, c + 1)
                    sp.dma_start(xn_dram[c * P:(c + 1) * P, :], xg[:, c, :]).then_inc(xn_st, 16)
                sp.wait_ge(xn_st, 16 * TT)

            @block.gpsimd
            def _(pool):
                pool.iota(desc[:, :], [[-1, EPG]], base=EPG, channel_multiplier=0, allow_small_or_imprecise_dtypes=True).then_inc(made, 1)
                pool.iota(base[:, :], [[CAP, NE]], base=-(NE - 1) * CAP, channel_multiplier=0, allow_small_or_imprecise_dtypes=True).then_inc(made, 1)
                pool.iota(steps[:, :], [[CAP, S // CAP]], base=0, channel_multiplier=0, allow_small_or_imprecise_dtypes=True).then_inc(made, 1)
                for j in range(2):
                    pool.iota(ids[:, j, :, 0], [[P, TT]], base=0, channel_multiplier=1).then_inc(made, 1)
                    pool.iota(ids[:, j, :, 1], [[2 * P, TT]], base=j, channel_multiplier=2).then_inc(made, 1)
                pool.memset(empty[:, :, 0], 0).then_inc(made, 1)
                pool.iota(empty[:, :, 1], [[1, LIST // P]], base=2 * S, channel_multiplier=LIST // P).then_inc(made, 1)
                pool.memset(M["rounds"][:, :], 0).then_inc(made, 1)
                pool.wait_ge(zeroed, 16)
                pool.wait_ge(made, MADE)
                pool.wait_ge(slots_ready, 1)
                for j in range(2):
                    for c in range(TT):
                        pool.indirect_dma_start(out=list_dram, out_offset=bass.IndirectOffsetOnAxis(ap=M["slots"][:, j, c:c + 1], axis=0),
                                                in_=ids[:, j, c, :], in_offset=None).then_inc(put, 16)
                pool.wait_ge(put, 16 * 2 * TT)

            @block.scalar
            def _(act):
                for c in range(TT):
                    if c:
                        act.wait_ge(squared, c)
                    act.activation(sq[:, :], h[:, c, :], ACT.Square, accum_out=ss[:, c:c + 1]).then_inc(squared, 1)
                act.wait_ge(rstd, 1)
                act.activation(ss[:, :], ss[:, :], ACT.Sqrt).then_inc(rstd, 1)
                act.preload_act_table(ACT.Exp)
                for k in range(0, KC, 2):
                    act.wait_ge(turned, k + 1)
                    act.activation(xT[:, k, :], t_bank[k % 4][:, :], ACT.Copy).then_inc(even_st, 1)
                act.wait_ge(dv, M["group_less"])
                act.activation(ex4[:, :, :], t4[:, :, :], ACT.Exp).then_inc(ac, 1)
                act.wait_ge(dv, M["top_less"])
                act.activation(p2[:, :], p2[:, :], ACT.Exp).then_inc(ac, 1)

            @block.tensor
            def _(pe):
                for k in range(KC):
                    if k >= 4:
                        pe.wait_ge((even_st, odd_st)[k % 2], (k - 4) // 2 + 1)
                    for c in range(TT):
                        pe.wait_ge(scaled, c + 1)
                        t = pe.transpose(t_bank[k % 4][:, c * P:(c + 1) * P], xg[:, c, k * P:(k + 1) * P], const["ident"][:, :])
                    t.then_inc(turned, 1)
                pe.wait_ge(loaded, 64)
                pe.wait_ge(even_st, KC // 2)
                pe.wait_ge(odd_st, KC // 2)
                for c in range(TT):
                    for k in range(KC):
                        m = pe.matmul(l_bank[:, c * NL:(c + 1) * NL], xT[:, k, c * P:(c + 1) * P], wr[:, k, :],
                                      start=(k == 0), stop=(k == KC - 1))
                m.then_inc(logits, 1)
                pe.wait_ge(dv, M["both"])
                for c in range(TT + 1):
                    for b in range(min(c, TT - 1) + 1 if c < TT else TT):
                        same = b == c
                        m = pe.matmul(r_bank[:, c * NE:(c + 1) * NE], (const["causal"][:, 0, :] if same else const["minus_ones"][:, :]),
                                      (both if same else nboth)[:, b, :], start=(b == 0), stop=(b == min(c, TT - 1)))
                m.then_inc(ranks, 1)



def load_expert(sp, A, M, j, e):
    for name, slot in (("exp_w_gate", M["gate"][j]), ("exp_w_up", M["up"][j]), ("exp_w_down", M["down"][j])):
        w = A[name].rearrange("l e (k p) n -> p (l e) k n", p=P)
        sp.dma_start(slot[:, :, :], w[:, bass.ds(e, 1), :, :].rearrange("p a k n -> p (a k) n")).then_inc(M["weights_in"][j], 16)


def experts(nc, A, const, xn_dram, list_dram, y_dram, M):
    with Scope(nc) as s:
        wg, wu, wd, w_in = M["gate"], M["up"], M["down"], M["weights_in"]
        idx = [s.sb(f"list_places{i}", [CAP, 2], I32) for i in range(UNROLL)]
        xg = [s.sb(f"gathered{j}", [CAP, D]) for j in range(NB)]
        xT = [s.sb(f"gathered_t{j}", [P, KC, CAP]) for j in range(2)]
        act_g = [s.sb(f"silu{j}", [P, DE]) for j in range(2)]
        hid_t = [s.sb(f"hidden_t{j}", [P, DE]) for j in range(2)]
        hid = [s.sb(f"hidden{j}", [P, FC, CAP]) for j in range(2)]
        y = [s.sb(f"expert_out{j}", [CAP, D]) for j in range(NB)]
        t_bank = [s.ps(f"gathered_ps{j}") for j in range(2)]
        g_bank = [s.ps(f"hidden_ps{j}") for j in range(2)]
        h_bank = [s.ps(f"hidden_turned_ps{j}") for j in range(2)]
        y_bank = [s.ps(f"expert_ps{j}") for j in range(2)]
        idx_in = s.sems("index_loaded", UNROLL)
        x_in = s.sems("tokens_gathered", NB)
        turned = s.sems("gathered_turned", NB)
        t_st = s.sems("gathered_stored", NB)
        gu = s.sems("gate_up_ready", NB)
        silu = s.sems("silu_ready", NB)
        mul_r = s.sems("hidden_multiplied", NB)
        h_turned = s.sems("hidden_turned", NB)
        hid_r = s.sems("hidden_ready", NB)
        y_r = s.sems("expert_ready", NB)
        y_lo, y_hi = s.sems("expert_low_stored", NB), s.sems("expert_high_stored", NB)
        y_out = s.sems("expert_written", NB)
        spare, seen, seen_sp, seen_pe = s.sem("spare_rows_ready"), s.sem("waits_seen"), s.sem("slots_seen"), s.sem("gathers_seen")
        TURNS = NE // UNROLL
        lists = list_dram.rearrange("(l c) a -> c l a", c=CAP)

        def use(i, n):
            return i % NB, n * (UNROLL // NB) + i // NB

        def turns(eng):
            rounds = eng.value_load(M["rounds"][0:1, 0:1], min_val=1, max_val=S // CAP)
            with eng.Fori(0, rounds) as rnd, eng.Fori(0, TURNS) as t:
                yield rnd, t, rnd * TURNS + t

        with nc.Block() as block:

            @block.sync
            def _(sp):
                rounds = sp.value_load(M["rounds"][0:1, 0:1], min_val=1, max_val=S // CAP)
                with sp.Fori(0, rounds) as rnd:
                    first = rnd * TURNS
                    with sp.Fori(0, TURNS - 1) as t:
                        for i in range(UNROLL):
                            j, m = use(i, first + t)
                            sp.wait_ge(y_r[j], m + 2)
                            load_expert(sp, A, M, j, t * UNROLL + i + NB)
                    for i in range(UNROLL):
                        j, m = use(i, first + TURNS - 1)
                        sp.wait_ge(y_r[j], m + 2)
                        if i < NB:
                            load_expert(sp, A, M, j, NE - NB + i)
                    sp.sem_inc(seen_sp)
                    with sp.If(rnd + 1 < rounds):
                        for j in range(NB):
                            load_expert(sp, A, M, j, j)

            @block.gpsimd
            def _(pool):
                for j in range(NB):
                    pool.iota(idx[NB + j][:, :], [[0, 2]], base=2 * S + LIST + j * CAP, channel_multiplier=1).then_inc(spare, 1)
                    pool.memset(y[j][:, :], 0.0).then_inc(spare, 1)

                def write_rows(i, j, m):
                    pool.wait_ge(y_lo[j], m + 1)
                    pool.wait_ge(y_hi[j], m + 1)
                    pool.sem_inc(seen)
                    pool.indirect_dma_start(out=y_dram, out_offset=bass.IndirectOffsetOnAxis(ap=idx[i][:, 1:2], axis=0),
                                            in_=y[j][:, :], in_offset=None).then_inc(y_out[j], 16)

                pool.wait_ge(spare, 2 * NB)
                for rnd, t, n in turns(pool):
                    for i in range(UNROLL):
                        j, m = use(i, n)
                        pool.wait_ge(idx_in[i], n * 16 + 16)
                        pool.sem_inc(seen)
                        pool.indirect_dma_start(out=xg[j][:, :], out_offset=None, in_=xn_dram,
                                                in_offset=bass.IndirectOffsetOnAxis(ap=idx[i][:, 0:1], axis=0)).then_inc(x_in[j], 16)
                        write_rows((i + NB) % UNROLL, j, m)
                total = pool.value_load(M["rounds"][0:1, 0:1], min_val=1, max_val=S // CAP) * (NE // NB)
                for j in range(NB):
                    write_rows(NB + j, j, total)
                for j in range(NB):
                    pool.wait_ge(y_out[j], total * 16 + 16)
                    pool.wait_ge(idx_in[j], total // (UNROLL // NB) * 16 + 16)
                pool.sem_inc(seen)

            @block.tensor
            def _(pe):
                for j in range(NB):
                    pe.sem_inc(y_r[j])

                def turn_tokens(i, n):
                    j, m = use(i, n)
                    pe.wait_ge(x_in[j], m * 16 + 16)
                    pe.sem_inc(seen_pe)
                    for k in range(KC):
                        x = pe.transpose(t_bank[i % 2][:, k * CAP:(k + 1) * CAP], xg[j][:, k * P:(k + 1) * P], const["ident"][0:CAP, 0:CAP])
                    x.then_inc(turned[j], 1)

                def gate_and_up(i, n):
                    j, m = use(i, n)
                    pe.wait_ge(w_in[j], m * 48 + 48)
                    pe.wait_ge(t_st[j], m + 1)
                    for k in range(KC):
                        for a, w in enumerate((wg[j], wu[j])):
                            x = pe.matmul(g_bank[i % 2][a * CAP:(a + 1) * CAP, 0:DE], xT[i % 2][:, k, :], w[:, k, :],
                                          start=(k == 0), stop=(k == KC - 1))
                    x.then_inc(gu[j], 1)

                def turn_hidden(i, n):
                    j, m = use(i, n)
                    pe.wait_ge(mul_r[j], m + 1)
                    pe.sem_inc(seen_pe)
                    for f in range(FC):
                        x = pe.transpose(h_bank[i % 2][:, f * CAP:(f + 1) * CAP], hid_t[i % 2][CAP:P, f * P:(f + 1) * P], const["ident"][CAP:P, CAP:P])
                    x.then_inc(h_turned[j], 1)

                def down(i, n):
                    j, m = use(i, n)
                    pe.wait_ge(hid_r[j], m + 1)
                    j2, m2 = use(i - 2, n)
                    pe.wait_ge(y_lo[j2], m2 + 2)
                    pe.wait_ge(y_hi[j2], m2 + 2)
                    for f in range(FC):
                        for half in range(2):
                            x = pe.matmul(y_bank[i % 2][half * CAP:(half + 1) * CAP, :], hid[i % 2][:, f, :], wd[j][:, f, half * 512:(half + 1) * 512],
                                          start=(f == 0), stop=(f == FC - 1))
                    x.then_inc(y_r[j], 1)

                for rnd, t, n in turns(pe):
                    turn_tokens(0, n)
                    for i in range(UNROLL):
                        if i + 1 < UNROLL:
                            turn_tokens(i + 1, n)
                        gate_and_up(i, n)
                        if i:
                            down(i - 1, n)
                        turn_hidden(i, n)
                    down(UNROLL - 1, n)

            @block.scalar
            def _(act):
                for j in range(NB):
                    act.dma_start(idx[j][:, :], lists[:, j:j + 1, :].rearrange("c a b -> c (a b)")).then_inc(idx_in[j], 16)
                    act.sem_inc(y_hi[j])

                def store_tokens(i, n):
                    j, m = use(i, n)
                    act.wait_ge(turned[j], m + 1)
                    act.activation(xT[i % 2][:, :, :].rearrange("p k c -> p (k c)"), t_bank[i % 2][:, :], ACT.Copy).then_inc(t_st[j], 1)

                def store_high(i, n):
                    j, m = use(i, n)
                    act.wait_ge(y_r[j], m + 2)
                    act.wait_ge(y_out[j], m * 16 + 16)
                    act.activation(y[j][:, 512:D], y_bank[i % 2][CAP:P, :], ACT.Copy).then_inc(y_hi[j], 1)
                    ahead = (i + NB) % UNROLL
                    act.dma_start(idx[ahead][:, :], lists[:, bass.ds(n * UNROLL + i + NB, 1), :].rearrange("c a b -> c (a b)")).then_inc(idx_in[ahead], 16)

                for rnd, t, n in turns(act):
                    store_tokens(0, n)
                    for i in range(UNROLL):
                        if i + 1 < UNROLL:
                            store_tokens(i + 1, n)
                        j, m = use(i, n)
                        act.wait_ge(gu[j], m + 1)
                        act.activation(act_g[i % 2][CAP:P, :], g_bank[i % 2][0:CAP, 0:DE], ACT.Silu).then_inc(silu[j], 1)
                        if i:
                            store_high(i - 1, n)
                    store_high(UNROLL - 1, n)

            @block.vector
            def _(dve):
                for j in range(NB):
                    dve.sem_inc(y_lo[j])

                def store_low(i, n):
                    j, m = use(i, n)
                    dve.wait_ge(y_r[j], m + 2)
                    dve.wait_ge(y_out[j], m * 16 + 16)
                    dve.tensor_copy(y[j][:, 0:512], y_bank[i % 2][0:CAP, :]).then_inc(y_lo[j], 1)

                for rnd, t, n in turns(dve):
                    for i in range(UNROLL):
                        j, m = use(i, n)
                        dve.wait_ge(silu[j], m + 1)
                        dve.tensor_tensor(hid_t[i % 2][CAP:P, :], g_bank[i % 2][CAP:P, 0:DE],
                                          act_g[i % 2][CAP:P, :], ALU.mult).then_inc(mul_r[j], 1)
                        if i:
                            store_low(i - 1, n)
                        dve.wait_ge(h_turned[j], m + 1)
                        dve.tensor_copy(hid[i % 2][:, :, :].rearrange("p f c -> p (f c)"), h_bank[i % 2][:, 0:FC * CAP]).then_inc(hid_r[j], 1)
                    store_low(UNROLL - 1, n)


A_REL = 2 * 2 * P - 1
CLS = 4
BUCKETS = 32
SKEW = 16
COL = {"qa": 0, "ka": 512, "va": 640, "qb": 768, "kb": 2304, "vb": 3840, "ga": 5376, "gb": 5888, "mg": 6400}


class BiasRows:

    def __init__(self, s, A, const):
        self.A, self.const = A, const
        self.hot = s.sb("bucket_hot", [BUCKETS, 3, 512])
        self.rel = s.sb("rel_bias", [BUCKETS, 4 * NH])
        self.win = s.sb("window", [NH, 4, 512])
        self.tab = s.sb("bias_rows", [NH, 4, 512])
        self.bank = [s.ps(f"bias_ps{i}") for i in range(4)]
        self.loaded, self.ready, self.added, self.stored, self.gains = (
            s.sem("bias_" + n) for n in ("loaded", "ready", "added", "stored", "head_gains"))

    def load(self, act):
        A, loaded = self.A, self.loaded
        act.dma_start(self.hot[:, :, :], A["const_bucket_hot"].rearrange("g b x -> b g x")).then_inc(loaded, 16)
        act.dma_start(self.rel[:, :], A["rel_bias_2"]).then_inc(loaded, 16)
        act.dma_start(self.win[:, :, :], A["const_window"].rearrange("g h x -> h g x")).then_inc(loaded, 16)
        act.dma_start(self.const["sink"][:, :], A["sink_a_2"].broadcast_to([P, NH])).then_inc(loaded, 16)

    def pick(self, pe):
        pe.wait_ge(self.loaded, 64)
        for g in range(4):
            pe.matmul(self.bank[g][0:NH, :], self.rel[:, g * NH:(g + 1) * NH], self.hot[:, max(g - 1, 0), :],
                      start=True, stop=True).then_inc(self.ready, 1)

    def add_windows(self, dve):
        for i, name in enumerate(("q_norm_a_2", "k_norm_a_2", "q_norm_b_2", "k_norm_b_2")):
            dve.tensor_scalar(self.const["head_gains"][:, i:i + 1], par_col(self.const, PARAM_AT[name]),
                              HD ** -0.5 if i % 2 == 0 else 1.0, None, ALU.mult).then_inc(self.gains, 1)
        for g in range(4):
            dve.wait_ge(self.ready, g + 1)
            dve.tensor_tensor(self.tab[:, g, :], self.bank[g][0:NH, :], self.win[:, g, :], ALU.add).then_inc(self.added, 1)
        dve.wait_ge(self.gains, 4)

    def store(self, act):
        act.wait_ge(self.added, 4)
        for g in range(4):
            act.dma_start(self.const["bias_dram"][g], self.tab[:, g:g + 1, :].broadcast_to([NH, SKEW, 512])).then_inc(self.stored, 16)
        act.wait_ge(self.stored, 64)


def combine(nc, A, const, h, y_dram, M):
    with Scope(nc) as s:
        bias = BiasRows(s, A, const)
        yg = s.sb("expert_rows", [P, TT, 2, D])
        rows = y_dram[0:2 * S, :].rearrange("(c p k) d -> p c k d", p=P, k=2)
        sq = s.sb("fin_sq", [P, D])
        ss = s.sb("fin_ss", [P, TT])
        rs = s.sb("fin_rstd", [P, TT])
        got = s.sems("rows_gathered", 4)
        added = s.sem("rows_added")
        squared, rstd, scaled = s.sem("fin_squares"), s.sem("fin_rstd_ready"), s.sem("fin_scaled")
        with nc.Block() as block:

            @block.sync
            def _(sp):
                for c in range(TT):
                    sp.dma_start(yg[:, c, :, :], rows[:, c, :, :]).then_inc(got[c], 16)

            @block.tensor
            def _(pe):
                bias.pick(pe)

            @block.vector
            def _(dve):
                for i in range(2 * TT):
                    c, j = i // 2, i % 2
                    dve.wait_ge(got[c], 16)
                    if j:
                        dve.wait_ge(added, i)
                    dve.scalar_tensor_tensor(out=h[:, c, :], in0=yg[:, c, j, :], scalar=M["weights"][:, j, c:c + 1], in1=h[:, c, :],
                                             op0=ALU.mult, op1=ALU.add).then_inc(added, 1)
                bias.add_windows(dve)
                dve.wait_ge(squared, TT)
                dve.tensor_scalar(ss[:, :], ss[:, :], 1.0 / D, EPS, ALU.mult, ALU.add).then_inc(rstd, 1)
                dve.wait_ge(rstd, 2)
                dve.reciprocal(rs[:, :], ss[:, :]).then_inc(rstd, 1)
                dve.wait_ge(rstd, 3)
                for c in range(TT):
                    dve.scalar_tensor_tensor(out=h[:, c, :], in0=h[:, c, :], scalar=rs[:, c:c + 1], in1=const["fin_g"][:, :],
                                             op0=ALU.mult, op1=ALU.mult).then_inc(scaled, 1)

            @block.scalar
            def _(act):
                bias.load(act)
                for c in range(TT):
                    act.wait_ge(added, 2 * c + 2)
                    if c:
                        act.wait_ge(squared, c)
                    act.activation(sq[:, :], h[:, c, :], ACT.Square, accum_out=ss[:, c:c + 1]).then_inc(squared, 1)
                act.wait_ge(rstd, 1)
                act.activation(ss[:, :], ss[:, :], ACT.Sqrt).then_inc(rstd, 1)
                bias.store(act)


def by_class(x):
    return x.rearrange("p (t c) -> p c t", c=CLS)


def second_weights(s, A):
    w = A["w_in_2"].rearrange("l (k p) n -> p (l k) n", p=P)
    return SplitWeights(s, "w_in_2", w, list(range(0, COL["ga"], UNIT)), UNIT).place_parts(s)


def project_second(nc, A, const, hT, T, wts):
    NBANK = 6
    gains = const["head_gains"]
    jobs = []
    for u in range(len(wts.cols)):
        col = u * UNIT
        if col < COL["ka"]:
            jobs += [(u, "qk", x, T["qa"][:, col // P + x, :], 0, False) for x in range(2)]
        elif col == COL["ka"]:
            jobs += [(u, "ka", 0, T["ka"], 1, False)]
            jobs += [(u, "va", 0, T["va"][:, :, :], None, False)]
        elif col < COL["vb"]:
            name = "qb" if col < COL["kb"] else "kb"
            for x in range(2):
                f = (col - COL[name]) // P + x
                jobs.append((u, "qk", x, T[name][:, f, :], 2 if name == "qb" else 3, f >= FT))
        else:
            g, half = divmod((col - COL["vb"]) // UNIT, 2)
            for pair in range(2):
                dst = T["v0"][:, :, half * UNIT:(half + 1) * UNIT] if g == 0 else \
                    T["v12"][:, :, (2 * (g - 1) + half) * UNIT:(2 * (g - 1) + half + 1) * UNIT]
                jobs.append((u, "vb", pair, dst[:, 2 * pair:2 * pair + 2, :], None, g > 0))
    last_job = {}
    for n, job in enumerate(jobs):
        last_job[job[0]] = n
    normed = [n for n, job in enumerate(jobs) if job[1] in ("qk", "ka")]
    plain = [n for n, job in enumerate(jobs) if job[1] not in ("qk", "ka")]
    with Scope(nc) as s:
        sq, rs = (T["scratch"][:, i * 2 * S:(i + 1) * 2 * S].rearrange("p (b t) -> p b t", b=2) for i in range(2))
        sq_part = [s.sb(f"qk_sq_{n}", [P, b, S], F32R) for n, b in (("high", 2), ("low", 1))]
        bank = [s.ps(f"proj_ps{i}") for i in range(NBANK)]
        sums = [s.ps(f"qk_sum_ps{i}") for i in range(2)]
        ready = s.sem("projected")
        sq_high, sq_low = s.sem("sq_high_ready"), s.sem("sq_low_ready")
        wts.used = lambda u: (ready, last_job[u] + 1)
        v_st = s.sem("v2_stored")
        squared, summed, logged, rstd, gained, qk_st = (s.sem("head_norm_" + n) for n in ("squared", "summed", "logged", "rstd", "gained", "stored"))
        with nc.Block() as block:

            @block.sync
            def _(sp):
                for u in range(2, len(wts.cols)):
                    wts.load(sp, u)

            @block.tensor
            def _(pe):
                def head_sums(i):
                    pe.wait_ge(sq_low, i + 1)
                    if i >= 2:
                        pe.wait_ge(logged, i - 1)
                    for j in range(2):
                        m = pe.matmul(sums[i % 2][:, :], const["heads_exact"][:, :], sq_part[j][:, i % (2 - j), :], start=(j == 0), stop=(j == 1))
                    m.then_inc(summed, 1)

                for n, (u, kind, x, dst, gain, perm) in enumerate(jobs):
                    wts.wait(pe, u)
                    if n >= NBANK:
                        o = n - NBANK
                        if o in normed:
                            pe.wait_ge(qk_st, normed.index(o) + 1)
                        else:
                            pe.wait_ge(v_st, plain.index(o) + 1)
                    b = bank[n % NBANK]

                    def tokens(k):
                        return [p[:, k, :] for p in hT]

                    if kind in ("qk", "ka"):
                        m = split_product(pe, b[:, :], lambda k: wts.parts(u, k, slice(x * P, (x + 1) * P)), tokens, KC)
                    else:
                        cols, nc_ = (slice(P, 2 * P), TT) if kind == "va" else (slice(0, UNIT), 2)
                        width = cols.stop - cols.start
                        for i in range(nc_):
                            c = i if kind == "va" else 2 * x + i

                            def some(k):
                                return [by_class(p[:, k, :])[:, c, :] if perm else p[:, k, c * P:(c + 1) * P] for p in hT]

                            m = split_product(pe, b[:, i * width:(i + 1) * width], some, lambda k: wts.parts(u, k, cols), KC)
                    m.then_inc(ready, 1)
                    if n >= 1 and n - 1 in normed:
                        head_sums(normed.index(n - 1))

            @block.scalar
            def _(act):
                act.preload_act_table_set("natural_log_exp_and_others")
                def factors(i):
                    act.wait_ge(summed, i + 1)
                    if i >= 2:
                        act.wait_ge(qk_st, i - 1)
                    act.activation(rs[:, i % 2, :], sums[i % 2][:, :], ACT.Ln, scale=1.0 / HD, bias=const["eps"][:, :]).then_inc(logged, 1)
                    act.wait_ge(logged, i + 1)
                    act.activation(rs[:, i % 2, :], rs[:, i % 2, :], ACT.Exp, scale=-0.5).then_inc(rstd, 1)

                for n, (u, kind, x, dst, gain, perm) in enumerate(jobs):
                    act.wait_ge(ready, n + 1)
                    if n in normed:
                        i = normed.index(n)
                        if i >= 2:
                            act.wait_ge(summed, i - 1)
                        act.activation(sq[:, i % 2, :], bank[n % NBANK][:, :], ACT.Square).then_inc(squared, 1)
                        act.wait_ge(squared, i + 1)
                        act.activation(sq_part[0][:, i % 2, :], sq[:, i % 2, :], ACT.Copy).then_inc(sq_high, 1)
                    else:
                        width = P if kind == "va" else UNIT
                        act.activation(dst, bank[n % NBANK][:, :].rearrange("p (c w) -> p c w", w=width), ACT.Copy).then_inc(v_st, 1)
                    if n == 0 or last_job.get(u - 1) == n - 1:
                        wts.split_high(act, u + 1)
                    if n - 1 in normed:
                        factors(normed.index(n - 1))

            @block.gpsimd
            def _(pool):
                for i in range(len(normed)):
                    pool.wait_ge(sq_high, i + 1)
                    if i:
                        pool.wait_ge(summed, i)
                    pool.tensor_tensor(sq_part[1][:, 0, :], sq[:, i % 2, :], sq_part[0][:, i % 2, :], ALU.subtract).then_inc(sq_low, 1)

            @block.vector
            def _(dve):
                for m, (u, *_) in enumerate(jobs):
                    if m == 0 or last_job.get(u - 1) == m - 1:
                        wts.split_low(dve, u + 1)
                    n = m - 1
                    if n not in normed:
                        continue
                    u, kind, x, dst, gain, perm = jobs[n]
                    i = normed.index(n)
                    dve.wait_ge(rstd, i + 1)
                    r = rs[:, i % 2, :]
                    dve.tensor_scalar(r, r, gains[:, gain:gain + 1], None, ALU.mult).then_inc(gained, 1)
                    dve.wait_ge(gained, i + 1)
                    src = bank[n % NBANK][:, :]
                    if kind == "ka":
                        for head in range(2):
                            at = slice(head * HD, (head + 1) * HD)
                            for half in range(2):
                                o = dve.tensor_tensor(dst[half * HD:(half + 1) * HD, head, :], src[at, :], r[at, :], ALU.mult)
                    elif perm:
                        o = dve.tensor_tensor(dst.rearrange("p (c t) -> p c t", c=CLS), by_class(src), by_class(r), ALU.mult)
                    else:
                        o = dve.tensor_tensor(dst, src, r, ALU.mult)
                    o.then_inc(qk_st, 1)


def windowed_attention(nc, const, T, next_w):
    HU = 4
    units = [(g, i, q) for g in range(3) for i in range(TT) for q in range(2)]
    NU = len(units)
    W = 3 * P
    with Scope(nc) as s:
        sc = s.sb("scores", [P, 2, HU, W])
        pt = s.sb("probs_t", [P, 3, W])
        mx = s.sb("row_max", [P, NU, HU])
        nm = s.sb("row_max_neg", [P, NU, HU])
        dn = s.sb("denominators", [P, NU, HU])
        ex = s.sb("sink_exp", [P, 2 * TT, HU])
        inv = s.sb("inverses", [P, 2, HU])
        s_bank = [s.ps(f"attn_score_ps{i}") for i in range(4)]
        t_bank = [s.ps(f"attn_turn_ps{i}") for i in range(2)]
        o_bank = [s.ps(f"attn_out_ps{i}") for i in range(2)]
        sc_ready, biased, p_ready, turned, pt_st, o_st = (
            s.sem("attn_" + n) for n in ("scores", "biased", "probs", "turned", "turned_stored", "stored"))
        used = s.sem("probs_t_used")
        negated, small, sunk = s.sem("row_max_negated"), s.sem("attn_small_step"), s.sem("sink_exp_ready")
        tiled = s.sems("bias_tile_loaded", 4)
        class_out = s.sem("classes_stored")
        n_small = [0]
        small_at = {}

        def keys(g, i):
            if g == 2:
                return 0, [0, 1]
            b = [j for j in (i - 1, i, i + 1) if 0 <= j < TT]
            return (b[0] - i + 1) * P, b

        with nc.Block() as block:

            @block.sync
            def _(sp):
                dram = const["bias_dram"]
                for g, tile, w in ((0, T["band"][0], W), (1, T["band"][1], W), (2, T["classes"][:, :, 0:P], P),
                                   (3, T["classes"][:, :, P:2 * P], P)):
                    for p in range(0, P, SKEW):
                        src = bass.AP(dram.tensor, dram.offset + g * NH * SKEW * 512 + P - 1 - p, [[511, SKEW], [SKEW * 512, NH], [1, w]])
                        sp.dma_start(tile[p:p + SKEW, :, :], src).then_inc(tiled[g], 16)
                sp.wait_ge(used, HU * units.index((2, 0, 0)))
                next_w.load(sp, 0)
                for c in range(CLS):
                    sp.wait_ge(o_st, units.index((2, c, 1)) + 1)
                    sp.dma_start(T["part_dram"].rearrange("(t c) w -> c t w", c=CLS)[c], T["y12"][:, c, :]).then_inc(class_out, 16)
                sp.wait_ge(class_out, 16 * CLS)

            @block.vector
            def _(dve):
                def step(ins):
                    n_small[0] += 1
                    ins.then_inc(small, 1)
                    dve.wait_ge(small, n_small[0])

                def bias(u, h):
                    g, i, q = units[u]
                    c0, bl = keys(g, i)
                    w = len(bl) * P
                    n = HU * u + h
                    if i == 0 and q == 0 and h == 0:
                        for k in ((0,), (1,), (2, 3))[g]:
                            dve.wait_ge(tiled[k], 16 * P // SKEW)
                    dve.wait_ge(sc_ready, n + 1)
                    tile = T["classes"][:, HU * q + h, 0:w] if g == 2 else T["band"][g][:, HU * q + h, c0:c0 + w]
                    dve.tensor_tensor(sc[:, u % 2, h, 0:w], s_bank[n % 4][:, 0:w], tile, ALU.add).then_inc(biased, 1)

                def row_max(u):
                    g, i, q = units[u]
                    w = len(keys(g, i)[1]) * P
                    dve.wait_ge(biased, HU * (u + 1))
                    m = mx[:, u, :]
                    step(dve.tensor_reduce(m, sc[:, u % 2, :, 0:w], AX_X, ALU.max))
                    if g == 0:
                        step(dve.tensor_tensor(m, m, const["sink"][:, HU * q:HU * (q + 1)], ALU.max))
                    dve.tensor_scalar(nm[:, u, :], m, -1.0, None, ALU.mult).then_inc(negated, 1)
                    if g == 0:
                        step(dve.tensor_tensor(ex[:, u, :], const["sink"][:, HU * q:HU * (q + 1)], m, ALU.subtract))
                        small_at[u] = n_small[0]

                def finish(u):
                    g, i, q = units[u]
                    dve.wait_ge(used, HU * (u + 1))
                    o = o_bank[u % 2][:, 0:HU * HD].rearrange("p (h d) -> p h d", h=HU)
                    if g == 0:
                        dve.wait_ge(sunk, u + 1)
                        dve.wait_ge(p_ready, HU * (u + 1))
                        step(dve.tensor_tensor(dn[:, u, :], dn[:, u, :], ex[:, u, :], ALU.add))
                        step(dve.reciprocal(inv[:, u % 2, :], dn[:, u, :]))
                        dve.tensor_tensor(T["ya"][:, i, HU * HD * q:HU * HD * (q + 1)].rearrange("p (h d) -> p h d", h=HU), o,
                                          inv[:, u % 2, :].unsqueeze(2).to_broadcast([P, HU, HD]), ALU.mult).then_inc(o_st, 1)
                    else:
                        dst = T["y0"] if g == 1 else T["y12"]
                        dve.wait_ge(p_ready, HU * (u + 1))
                        step(dve.tensor_copy(dst[:, i, HW + HU * q:HW + HU * (q + 1)], mx[:, u, :]))
                        step(dve.tensor_copy(dst[:, i, HW + NH + HU * q:HW + NH + HU * (q + 1)], dn[:, u, :]))
                        dve.tensor_copy(dst[:, i, HU * HD * q:HU * HD * (q + 1)], o_bank[u % 2][:, 0:HU * HD]).then_inc(o_st, 1)

                for n in range(HU):
                    bias(0, n)
                row_max(0)
                bias(1, 0)
                for u in range(NU):
                    w = len(keys(*units[u][0:2])[1]) * P
                    for h in range(HU):
                        n = HU * u + h
                        if n + HU + 1 < HU * NU:
                            bias(*divmod(n + HU + 1, HU))
                        if h == HU - 2 and u + 1 < NU:
                            row_max(u + 1)
                        dve.wait_ge(turned, n + 1)
                        if n >= 3:
                            dve.wait_ge(used, n - 2)
                        dve.tensor_copy(pt[:, n % 3, 0:w], t_bank[n % 2][:, 0:w]).then_inc(pt_st, 1)
                    if u >= 1:
                        finish(u - 1)
                finish(NU - 1)

            @block.tensor
            def _(pe):
                def scores(n):
                    u, h = divmod(n, HU)
                    g, i, q = units[u]
                    f, kv = (HU * q + h) // 2, (HU * q + h) // 4
                    rows = slice(i * P, (i + 1) * P)
                    bl = keys(g, i)[1]
                    ks = slice(bl[0] * P, (bl[-1] + 1) * P)
                    if n >= 4:
                        pe.wait_ge(biased, n - 2)
                    for k in range(2 if g == 2 else 1):
                        for odd in range(2):
                            at = slice(odd * HD, (odd + 1) * HD)
                            bank = s_bank[(n + odd) % 4]
                            if g == 2:
                                m = pe.matmul(bank[:, k * P:(k + 1) * P], T["qb"][at, (k + 1) * FT + f, rows],
                                              T["kb"][at, (k + 1) * FT + f, rows], start=True, stop=True)
                            elif g == 1:
                                m = pe.matmul(bank[:, 0:len(bl) * P], T["qb"][at, f, rows], T["kb"][at, f, ks], start=True, stop=True)
                            else:
                                m = pe.matmul(bank[:, 0:len(bl) * P], T["qa"][at, f, rows], T["ka"][at, kv, ks], start=True, stop=True)
                            if k == (1 if g == 2 else 0):
                                m.then_inc(sc_ready, 1)

                def turn(u, h):
                    n = HU * u + h
                    nb = len(keys(*units[u][0:2])[1])
                    pe.wait_ge(p_ready, n + 1)
                    if n >= 2:
                        pe.wait_ge(pt_st, n - 1)
                    for j in range(nb):
                        m = pe.transpose(t_bank[n % 2][:, j * P:(j + 1) * P], sc[:, u % 2, h, j * P:(j + 1) * P], const["ident"][:, :])
                    m.then_inc(turned, 1)

                def values(u, h):
                    g, i, q = units[u]
                    n = HU * u + h
                    head = HU * q + h
                    pe.wait_ge(pt_st, n + 1)
                    if h == 0 and u >= 2:
                        pe.wait_ge(o_st, u - 1)
                    bl = keys(g, i)[1]
                    for j, b in enumerate(bl):
                        if g == 0:
                            v = T["va"][:, b, (head // 4) * HD:(head // 4 + 1) * HD]
                        elif g == 1:
                            v = T["v0"][:, b, head * HD:(head + 1) * HD]
                        else:
                            v = T["v12"][:, i, b * HW + head * HD:b * HW + (head + 1) * HD]
                        m = pe.matmul(o_bank[u % 2][:, h * HD:(h + 1) * HD], pt[:, n % 3, j * P:(j + 1) * P], v,
                                      start=(j == 0), stop=(j == len(bl) - 1))
                    m.then_inc(used, 1)

                for n in range(0, HU + 2, 2):
                    scores(n)
                for u in range(NU):
                    for h in range(HU):
                        n = HU * (u + 1) + h + 2
                        if h % 2 == 0 and n < HU * NU:
                            scores(n)
                        turn(u, h)
                        if h:
                            values(u, h - 1)
                        elif u:
                            values(u - 1, HU - 1)
                values(NU - 1, HU - 1)

            @block.scalar
            def _(act):
                act.preload_act_table_set("natural_log_exp_and_others")
                for u in range(NU):
                    g, i, q = units[u]
                    w = len(keys(g, i)[1]) * P
                    act.wait_ge(negated, u + 1)
                    for h in range(HU):
                        act.activation(sc[:, u % 2, h, 0:w], sc[:, u % 2, h, 0:w], ACT.Exp, bias=nm[:, u, h:h + 1],
                                       accum_out=dn[:, u, h:h + 1]).then_inc(p_ready, 1)
                    if g == 0:
                        act.wait_ge(small, small_at[u])
                        act.activation(ex[:, u, :], ex[:, u, :], ACT.Exp).then_inc(sunk, 1)


class GroupMerge:

    STEPS = 10 + 3 * TT

    def __init__(self, s, T):
        self.m = s.sb("merged_max", [P, TT, NH])
        self.e = [s.sb(f"part_exp{i}", [P, TT, NH]) for i in range(2)]
        self.d = [s.sb(f"part_den{i}", [P, TT, NH]) for i in range(2)]
        self.loaded, self.st, self.exped = s.sem("classes_back"), s.sem("merge_step"), s.sem("merge_exp")
        self.dram = T["part_dram"]
        self.y = [T["y0"], T["y12"]]

    def load(self, sp):
        sp.dma_start(self.y[1][:, :, :], self.dram.rearrange("(c p) w -> p c w", p=P)).then_inc(self.loaded, 16)

    def exps(self, act):
        for j in range(2):
            act.wait_ge(self.st, 3 + j)
            act.activation(self.e[j][:, :, :], self.e[j][:, :, :], ACT.Exp).then_inc(self.exped, 1)

    def weigh(self, dve):
        n = [0]

        def step(ins):
            n[0] += 1
            ins.then_inc(self.st, 1)
            dve.wait_ge(self.st, n[0])

        m, e, d, y = self.m, self.e, self.d, self.y
        mx = [x[:, :, HW:HW + NH] for x in y]
        den = [x[:, :, HW + NH:HW + 2 * NH] for x in y]
        dve.wait_ge(self.loaded, 16)
        step(dve.tensor_tensor(m[:, :, :], mx[0], mx[1], ALU.max))
        step(dve.tensor_copy(d[0][:, :, :], den[0]))
        for j in range(2):
            step(dve.tensor_tensor(e[j][:, :, :], mx[j], m[:, :, :], ALU.subtract))
        for j in range(2):
            dve.wait_ge(self.exped, j + 1)
            step(dve.tensor_tensor(d[j][:, :, :], e[j][:, :, :], den[j], ALU.mult))
        step(dve.tensor_tensor(d[0][:, :, :], d[0][:, :, :], d[1][:, :, :], ALU.add))
        step(dve.reciprocal(d[0][:, :, :], d[0][:, :, :]))
        for j in range(2):
            step(dve.tensor_tensor(e[j][:, :, :], e[j][:, :, :], d[0][:, :, :], ALU.mult))
        for c in range(TT):
            for j in range(2):
                o = y[j][:, c, 0:HW].rearrange("p (h d) -> p h d", h=NH)
                step(dve.tensor_tensor(o, o, e[j][:, c, :].unsqueeze(2).to_broadcast([P, NH, HD]), ALU.mult))
            step(dve.tensor_tensor(y[0][:, c, 0:HW], y[0][:, c, 0:HW], y[1][:, c, 0:HW], ALU.add))
        assert n[0] == self.STEPS


GATE_UNITS = (COL["mg"] - COL["ga"]) // UNIT


def gate_weights(s, A, raw):
    first = COL["ga"] // UNIT
    mg = COL["mg"] // UNIT
    units = list(range(first, mg))
    for j in range(4):
        units += [mg + j, mg + 4 + j]
    return SplitWeights(s, "gate_w", A["w_in_2"].rearrange("l (k p) n -> p (l k) n", p=P), [u * UNIT for u in units], UNIT, raw=raw)


def gate_and_merge(nc, A, const, hT, T, merged, wts, next_w):
    NBANK = 6
    wa = A["w_branch_a_2"].rearrange("l (k p) n -> p (l k) n", p=P)
    wb = A["w_branch_b_2"].rearrange("l (k p) n -> p (l k) n", p=P)
    NGU = GATE_UNITS
    with Scope(nc) as s:
        def used(n):
            j, b = divmod(n - NGU, 2)
            return ready, 2 * (n + 1) if n < NGU else 2 * NGU + 8 * j + 5 + b

        wts.used = used
        wts.raw.append(s.sb("gate_w_raw_odd", [P, KC, UNIT])[:, :, :])
        wts.place_parts(s)
        bw = [s.sb(f"branch_w{i}", [P, FT, D]) for i in range(2)]
        yT = s.sb("branches_t", [P, 2 * FT, S])
        sg = s.sb("gate_sigmoid", [P, 3, S])
        mix = s.sb("mix_part", [P, 2, S])
        bank = [s.ps(f"gate_ps{i}") for i in range(NBANK)]
        t_bank = [s.ps(f"turn_ps{i}") for i in range(2)]
        NU = len(wts.cols)
        b_in = s.sem("branch_w_loaded")
        groups = GroupMerge(s, T)
        turned, t_st, ready, sig_r, gated, part = (
            s.sem("gm_" + n) for n in ("turned", "branch_gated", "ready", "sigmoid", "gate_ready", "part"))
        y = [T["ya"], T["y0"]]
        with nc.Block() as block:

            @block.sync
            def _(sp):
                for n in range(NU):
                    if n:
                        wts.load(sp, n)
                    if n == 0:
                        groups.load(sp)
                    if n >= NU - 2:
                        sp.wait_ge(turned, 2 * FT)
                        next_w.load(sp, n - (NU - 2))
                    if n < 2:
                        sp.dma_start(bw[n][:, :, :], (wa, wb)[n]).then_inc(b_in, 16)

            @block.tensor
            def _(pe):
                n = 0

                def turn_branches():
                    pe.wait_ge(groups.st, groups.STEPS)
                    for f in range(2 * FT):
                        if f >= 2:
                            pe.wait_ge(t_st, f - 1)
                        for c in range(TT):
                            m = pe.transpose(t_bank[f % 2][:, c * P:(c + 1) * P], y[f // FT][:, c, (f % FT) * P:(f % FT + 1) * P],
                                             const["ident"][:, :])
                        m.then_inc(turned, 1)

                def tile(unit, half):
                    split_product(pe, bank[n % NBANK][:, :], lambda k: wts.parts(unit, k, slice(half * P, (half + 1) * P)),
                                  lambda k: [p[:, k, :] for p in hT], KC).then_inc(ready, 1)

                for i in range(NGU):
                    wts.wait(pe, i)
                    for half in range(2):
                        if n >= NBANK:
                            pe.wait_ge(gated, n - NBANK + 1)
                        tile(i, half)
                        n += 1
                pe.wait_ge(b_in, 32)
                for j in range(4):
                    for half in range(2):
                        for b in range(2):
                            i = NGU + 2 * j + b
                            if half == 0:
                                wts.wait(pe, i)
                            o = n - NBANK
                            if o < 2 * NGU:
                                pe.wait_ge(gated, o + 1)
                            else:
                                k, r = divmod(o - 2 * NGU, 4)
                                pe.wait_ge(sig_r, 2 * NGU + 2 * k + r + 1) if r < 2 else pe.wait_ge(part, 3 * k + r - 1)
                            tile(i, half)
                            n += 1
                        if j == 0 and half == 0:
                            turn_branches()
                            pe.wait_ge(t_st, 2 * FT)
                        for b in range(2):
                            o = n - NBANK
                            if o < 2 * NGU:
                                pe.wait_ge(gated, o + 1)
                            else:
                                k, r = divmod(o - 2 * NGU, 4)
                                pe.wait_ge(sig_r, 2 * NGU + 2 * k + r + 1) if r < 2 else pe.wait_ge(part, 3 * k + r - 1)
                            t = 2 * j + half
                            for k in range(FT):
                                m = pe.matmul(bank[n % NBANK][:, :], bw[b][:, k, t * P:(t + 1) * P], yT[:, b * FT + k, :],
                                              start=(k == 0), stop=(k == FT - 1))
                            m.then_inc(ready, 1)
                            n += 1

            @block.scalar
            def _(act):
                wts.split_high(act, 0)
                for f in range(2 * NGU):
                    if f % 2 == 0:
                        wts.split_high(act, f // 2 + 1)
                    if f == 2 * NGU - 2:
                        groups.exps(act)
                    act.wait_ge(ready, f + 1)
                    if f >= 3:
                        act.wait_ge(gated, f - 2)
                    act.activation(sg[:, f % 3, :], bank[f % NBANK][:, :], ACT.Sigmoid).then_inc(sig_r, 1)
                wts.split_high(act, NGU + 1)
                for t in range(KC):
                    for b in range(2):
                        i = 2 * NGU + 2 * t + b
                        n = 2 * NGU + 4 * t + b
                        act.wait_ge(ready, n + 1)
                        o = i - 3
                        if o < 2 * NGU:
                            act.wait_ge(gated, o + 1)
                        else:
                            k, r = divmod(o - 2 * NGU, 2)
                            act.wait_ge(part, 3 * k + r + 1)
                        act.activation(sg[:, i % 3, :], bank[n % NBANK][:, :], ACT.Sigmoid,
                                       bias=par_col(const, PARAM_AT["b_merge_2"] + b * KC + t)).then_inc(sig_r, 1)
                        if t % 2:
                            wts.split_high(act, NGU + t + 1 + b)

            @block.vector
            def _(dve):
                wts.split_low(dve, 0)
                for f in range(2 * FT):
                    if f % 2 == 0:
                        wts.split_low(dve, f // 2 + 1)
                    if f == 2 * NGU - 2:
                        groups.weigh(dve)
                    dve.wait_ge(sig_r, f + 1)
                    dve.tensor_tensor(yT[:, f, :], bank[f % NBANK][:, :], sg[:, f % 3, :], ALU.mult).then_inc(gated, 1)
                wts.split_low(dve, NGU + 1)
                for f in range(2 * FT):
                    dve.wait_ge(gated, f + 1)
                    dve.wait_ge(turned, f + 1)
                    dve.tensor_tensor(yT[:, f, :], t_bank[f % 2][:, :], yT[:, f, :], ALU.mult).then_inc(t_st, 1)
                for t in range(KC):
                    if t % 2:
                        for b in range(2):
                            wts.split_low(dve, NGU + t + 1 + b)
                    for b in range(2):
                        n = 2 * NGU + 4 * t + 2 + b
                        i = 2 * NGU + 2 * t + b
                        dve.wait_ge(ready, n + 1)
                        dve.wait_ge(sig_r, i + 1)
                        if b == 0 and t:
                            dve.wait_ge(part, 3 * t)
                        dve.tensor_tensor(mix[:, b, :], bank[n % NBANK][:, :], sg[:, i % 3, :], ALU.mult).then_inc(part, 1)
                    dve.wait_ge(part, 3 * t + 2)
                    dve.tensor_tensor(merged[:, t, :], mix[:, 0, :], mix[:, 1, :], ALU.add).then_inc(part, 1)


def second_block(nc, A, const, out):
    with Scope(nc) as b2:
        recycle(nc)
        hT = [b2.sb("block_in_high", [P, KC, S], F32R), b2.sb("block_in_low", [P, KC, S], F32R)]
        y_ab = b2.sb("y_a_b", [P, TT * (2 * HW + 2 * NH)])
        T = {"ya": y_ab[:, 0:TT * HW].rearrange("p (c w) -> p c w", c=TT),
             "scratch": y_ab,
             "y0": y_ab[:, TT * HW:].rearrange("p (c w) -> p c w", c=TT),
             "part_dram": nc.dram_tensor("class_part_dram", (S, HW + 2 * NH), F32, kind="Internal").ap()}
        qk_a = b2.sb("qk_a", [P, (FT + 2) * S])
        v0 = b2.sb("vb0", [P, TT * HW])
        with Scope(nc) as s:
            T["qa"] = qk_a[:, 0:FT * S].rearrange("p (f t) -> p f t", f=FT)
            T["ka"] = qk_a[:, FT * S:(FT + 2) * S].rearrange("p (f t) -> p f t", f=2)
            T["y12"] = qk_a[:, 0:TT * (HW + 2 * NH)].rearrange("p (c w) -> p c w", c=TT)
            T["qb"], T["kb"] = s.sb("qb", [P, 3 * FT, S]), s.sb("kb", [P, 3 * FT, S])
            T["va"], T["v12"] = s.sb("va", [P, TT, P]), s.sb("vb12", [P, TT, 2 * HW])
            T["v0"] = v0[:, :].rearrange("p (c w) -> p c w", c=TT)
            with Scope(nc) as ws:
                wts = second_weights(ws, A)
                norm_to_features(nc, const["h"], PARAM_AT["norm_gain_2"], hT, const, "n2", wts,
                                 scratch=y_ab[:, 0:TT * D].rearrange("p (c d) -> p c d", c=TT))
                project_second(nc, A, const, hT, T, wts)
            recycle(nc)
            T["band"] = [s.sb(f"band_bias{g_}", [P, NH, 3 * P]) for g_ in range(2)]
            T["classes"] = s.sb("class_bias", [P, NH, 2 * P])
            gate_w = gate_weights(b2, A, [v0[:, :].rearrange("p (k n) -> p k n", k=KC)])
            windowed_attention(nc, const, T, gate_w)
        merged = b2.sb("merged", [P, KC, S])
        wts = SplitWeights(b2, "w_out_2", A["w_out_2"].rearrange("l (k p) n -> p (l k) n", p=P), list(range(0, D, UNIT)), UNIT,
                           raw=y_ab[:, 0:2 * KC * UNIT].rearrange("p (a k n) -> p a k n", a=2, k=KC))
        gate_and_merge(nc, A, const, hT, T, merged, gate_w, wts)
        out_projection(nc, const, wts, merged, const["h"], "wo2", out.rearrange("b t d -> (b t) d"))


def program(nc, A, out):
    Scope.ended = []
    with Scope(nc) as g:
        const = {"h": g.sb("h", [P, TT, D]), "ident": g.sb("ident", [P, P]), "par": g.sb("params", [P, N_PARAMS]),
                 "heads": g.sb("heads", [P, P]), "heads_exact": g.sb("heads_exact", [P, P], F32R),
                 "head_gains": g.sb("head_gains", [P, 4]), "sink": g.sb("sink", [P, NH]),
                 "bias_dram": nc.dram_tensor("bias_rows_dram", (4, NH, SKEW, 512), F32, kind="Internal").ap(),
                 "eps": g.sb("eps", [P, 1]), "gn_eps": g.sb("gn_eps", [P, 1]), "log_shift": g.sb("log_shift", [P, 1]),
                 "x_loaded": g.sem("x_loaded"), "row_params": g.sem("row_params_loaded")}
        once = g.stack.enter_context(Scope(nc))
        const.update({"causal": once.sb("causal", [P, 4, P]), "neg_causal": once.sb("neg_causal", [P, P]),
                      "minus_ones": once.sb("minus_ones", [P, P]), "suffix": once.sb("suffix", [P, P]),
                      "level": once.sb("level", [P, 7, P]),
                      "one_minus_mu": once.sb("one_minus_mu", [P, RT]), "one_minus_ka": once.sb("one_minus_ka", [P, FT]),
                      "ffn_g": once.sb("ffn_gain", [P, D]), "fin_g": once.sb("final_gain", [P, D])})
        setup_constants(nc, A, const)
        with Scope(nc) as b1:
            mixT = b1.sb("mixer_out", [P, KC, S])
            um = b1.sb("um", [P, RT, S])
            with Scope(nc) as sc:
                qk = sc.sb("qk", [P, 2 * FT, S])
                v = sc.sb("v", [P, TT, HW])
                with Scope(nc) as s:
                    xnT = [s.sb("mixer_in_high", [P, KC, S], F32R), s.sb("mixer_in_low", [P, KC, S], F32R)]
                    wts = first_weights(s, A)
                    norm_to_features(nc, const["h"], PARAM_AT["norm_mix_g"], xnT, const, "n1", wts, const["x_loaded"])
                    project_first(nc, A, xnT, um, qk, v, const, wts)
                stick_breaking(nc, const, qk, v, mixT)
            raw = b1.sb("w_out_raw", [P, 2, KC, UNIT])
            wts = SplitWeights(b1, "w_out", A["w_out"].rearrange("l (k p) n -> p (l k) n", p=P), list(range(0, D, UNIT)), UNIT, raw=raw)
            with Scope(nc) as rw:
                R = {"gate": rw.sb("gate", [P, FT, S]), "bonus": rw.sb("bonus", [P, FT, S]),
                     "kr": rw.sb("kk_r", [P, FT * NC, 2, CH]), "bh": rw.sb("b_hat", [P, FT, S]),
                     "kh": rw.sb("k_hat", [P, FT, S]), "mid": rw.sb("mid_decay", [P, FT * NC]),
                     "ends": rw.sb("chunk_sums", [P, FT * NC])}
                rwkv_features(nc, A, const, um, R)
                R["q"] = rw.sb("q_hat", [P, FT, S])
                R["o"] = rw.sb("rwkv_out", [P, FT, S])
                R["mn"] = rw.sb("m_n", [P, FT * NC, 2, HD])
                rwkv_chunks(nc, const, um, R, raw[:, :, :, :].rearrange("p a k n -> p (a k n)"))
                rwkv_output(nc, const, R, mixT, wts)
            out_projection(nc, const, wts, mixT, const["h"], "wo")
        with Scope(nc) as moe:
            M = {"slots": moe.sb("slots", [P, 2, TT], I32), "weights": moe.sb("route_weights", [P, 2, TT]),
                 "rounds": moe.sb("rounds", [P, 1], I32),
                 "gate": [moe.sb(f"w_gate{j}", [P, KC, DE]) for j in range(NB)],
                 "up": [moe.sb(f"w_up{j}", [P, KC, DE]) for j in range(NB)],
                 "down": [moe.sb(f"w_down{j}", [P, FC, D]) for j in range(NB)],
                 "weights_in": moe.sems("expert_loaded", NB)}
            xn_dram = nc.dram_tensor("ffn_in_dram", (S, D), F32, kind="Internal").ap()
            list_dram = nc.dram_tensor("expert_lists", (LIST, 2), I32, kind="Internal").ap()
            y_dram = nc.dram_tensor("expert_rows_dram", (2 * S + LIST + NB * CAP, D), F32, kind="Internal").ap()
            route(nc, A, const, const["h"], xn_dram, list_dram, M)
            recycle(nc)
            experts(nc, A, const, xn_dram, list_dram, y_dram, M)
            combine(nc, A, const, const["h"], y_dram, M)
        once.stack.close()
        second_block(nc, A, const, out)


def shape_constants():
    def bucket(rel):
        half, exact = BUCKETS // 2, BUCKETS // 4
        n = np.abs(rel)
        large = exact + (np.log(np.maximum(n, exact).astype(np.float32) / np.float32(exact)) / np.float32(np.log(1024 / exact))
                         * np.float32(half - exact)).astype(np.int32)
        return (rel > 0) * half + np.where(n < exact, n, np.minimum(large, half - 1))

    x = np.arange(512)
    band = np.minimum(x, A_REL - 1) - (2 * P - 1)
    apart = np.minimum(x, 2 * P - 2) - (P - 1)
    rels = [band, 4 * apart, 4 * apart]
    hot = np.stack([(bucket(r)[None, :] == np.arange(BUCKETS)[:, None]) for r in rels]).astype(np.float32)
    ok = [np.abs(band) <= 128, np.abs(band) <= 64, np.abs(apart) <= 64, apart % 4 == 0]
    window = np.stack([np.broadcast_to(np.where(o, 0.0, NEG), (NH, 512)) for o in ok]).astype(np.float32)
    return {"const_bucket_hot": np.ascontiguousarray(hot), "const_window": np.ascontiguousarray(window)}


def kernel(**inputs):
    import concourse.bacc as bacc
    from concourse.bass_utils import run_bass_kernel_spmd

    nc = bacc.Bacc("TRN2", target_bir_lowering=False, num_devices=1)
    arrays, A = {}, {}
    for name, a in {**inputs, **shape_constants()}.items():
        a = np.ascontiguousarray(a)
        arrays[name + "_dram"] = a
        A[name] = nc.dram_tensor(name + "_dram", a.shape, mybir.dt.from_np(a.dtype), kind="ExternalInput").ap()
    out = nc.dram_tensor("out_dram", (1, S, D), F32, kind="ExternalOutput").ap()
    program(nc, A, out)
    r = run_bass_kernel_spmd(nc, [arrays], core_ids=[0])
    return r.results[0]["out_dram"]
```
